# Optimizing a Trainium2 kernel written in Bass

```python
import jax, jax.numpy as jnp
from jax import lax
import numpy as np

D_MODEL = 1024
BATCH = 1
SEQ = 512
DEPTH = 1

SB_HEADS = 8
SB_HEAD_DIM = 64
D_ATTN = SB_HEADS * SB_HEAD_DIM
Q_BLOCK = 128
D_RNN = D_MODEL // 2
RG_BLOCKS = 8
RG_BLOCK_DIM = D_RNN // RG_BLOCKS
CONV_WIDTH = 4
RG_C = 8.0
IN_COLS = 3 * D_ATTN + 2 * D_RNN + 2 * D_MODEL
SPLIT_POINTS = (D_ATTN, 2 * D_ATTN, 3 * D_ATTN, 3 * D_ATTN + D_RNN,
                3 * D_ATTN + 2 * D_RNN, 3 * D_ATTN + 2 * D_RNN + D_MODEL)
N_GROUPS = 4
EXPERTS_PER_GROUP = 4
N_EXPERTS = N_GROUPS * EXPERTS_PER_GROUP
TOP_K_IN_GROUP = 2
D_EXPERT = 512
PLE_DIM = 256
EPS = 1e-6

kernel_name = "hybrid_sb_rglru_hmoe_trunk"

def rms_norm(x, g):
    xf = x.astype(jnp.float32)
    y = xf * lax.rsqrt(jnp.mean(xf * xf, axis=-1, keepdims=True) + EPS)
    return (y * g.astype(jnp.float32)).astype(x.dtype)

def stick_breaking_attention(q, k, v):
    B, S, _ = q.shape
    nb = S // Q_BLOCK
    scale = SB_HEAD_DIM ** -0.5
    q = q.reshape(B, S, SB_HEADS, SB_HEAD_DIM).transpose(0, 2, 1, 3)
    k = k.reshape(B, S, SB_HEADS, SB_HEAD_DIM).transpose(0, 2, 1, 3)
    v = v.reshape(B, S, SB_HEADS, SB_HEAD_DIM).transpose(0, 2, 1, 3)
    q_blocks = q.reshape(B, SB_HEADS, nb, Q_BLOCK, SB_HEAD_DIM).transpose(2, 0, 1, 3, 4)
    key_pos = jnp.arange(S)

    def one_block(args):
        q_blk, start = args
        z = jnp.einsum('bhqd,bhkd->bhqk', q_blk, k).astype(jnp.float32) * scale
        q_pos = start + jnp.arange(Q_BLOCK)
        causal = key_pos[None, :] < q_pos[:, None]
        log_not = jnp.where(causal, jax.nn.log_sigmoid(-z), 0.0)
        suffix = lax.cumsum(log_not, axis=3, reverse=True) - log_not
        w = jnp.where(causal, jnp.exp(jax.nn.log_sigmoid(z) + suffix), 0.0)
        return jnp.einsum('bhqk,bhkd->bhqd', w.astype(v.dtype), v)

    starts = jnp.arange(nb) * Q_BLOCK
    o = lax.map(one_block, (q_blocks, starts))
    return o.transpose(1, 0, 3, 2, 4).reshape(B, S, D_ATTN)

def _linear_recurrence(c1, c2):
    a1, b1 = c1
    a2, b2 = c2
    return (a1 * a2, a2 * b1 + b2)

def rg_lru_branch(xr, xg, conv_w, conv_b, w_a, b_a, w_x, b_x, lam):
    B, S, _ = xr.shape
    xpad = jnp.pad(xr, ((0, 0), (CONV_WIDTH - 1, 0), (0, 0)))
    xc = conv_b
    for j in range(CONV_WIDTH):
        xc = xc + conv_w[j] * xpad[:, j:j + S]
    blocks = xc.reshape(B, S, RG_BLOCKS, RG_BLOCK_DIM)
    r = jax.nn.sigmoid(jnp.einsum('bsgi,gij->bsgj', blocks, w_a).reshape(B, S, D_RNN) + b_a)
    ig = jax.nn.sigmoid(jnp.einsum('bsgi,gij->bsgj', blocks, w_x).reshape(B, S, D_RNN) + b_x)
    log_a = -RG_C * jax.nn.softplus(-lam.astype(jnp.float32)) * r.astype(jnp.float32)
    a = jnp.exp(log_a)
    b = jnp.sqrt(-jnp.expm1(2.0 * log_a)) * (ig * xc).astype(jnp.float32)
    _, h = lax.associative_scan(_linear_recurrence, (a, b), axis=1)
    return h.astype(xr.dtype) * jax.nn.gelu(xg)

def hierarchical_moe(h, w_group, b_group, w_expert, b_expert, w_gate, w_up, w_down):
    B, S, D = h.shape
    ht = h.reshape(B * S, D)
    g_logits = (ht @ w_group + b_group).astype(jnp.float32)
    p_group = jax.nn.softmax(g_logits, axis=-1)
    g_idx = jnp.argmax(g_logits, axis=-1)
    gate_group = jnp.take_along_axis(p_group, g_idx[:, None], axis=1)[:, 0]
    e_logits = (ht @ w_expert + b_expert).astype(jnp.float32)
    e_logits = e_logits.reshape(-1, N_GROUPS, EXPERTS_PER_GROUP)
    sel = jnp.take_along_axis(e_logits, g_idx[:, None, None], axis=1)[:, 0]
    top_vals, top_idx = lax.top_k(sel, TOP_K_IN_GROUP)
    w_in_group = jax.nn.softmax(top_vals, axis=-1)
    within = jnp.einsum('tk,tke->te', w_in_group,
                        jax.nn.one_hot(top_idx, EXPERTS_PER_GROUP, dtype=jnp.float32))
    combine = (jax.nn.one_hot(g_idx, N_GROUPS, dtype=jnp.float32)[:, :, None]
               * within[:, None, :] * gate_group[:, None, None])
    combine = combine.reshape(-1, N_EXPERTS).astype(h.dtype)
    y = jnp.zeros_like(ht)
    for e in range(N_EXPERTS):
        he = jax.nn.silu(ht @ w_gate[e]) * (ht @ w_up[e])
        y = y + combine[:, e:e + 1] * (he @ w_down[e])
    return y.reshape(B, S, D)

def setup_inputs(seed: int = 0) -> dict:
    key = jax.random.key(seed)
    ks = jax.random.split(key, 32)

    def nrm(k, shape, scale):
        return jax.random.normal(k, shape, jnp.float32) * scale

    u = jax.random.uniform(ks[11], (DEPTH, D_RNN), jnp.float32, minval=0.9, maxval=0.999)
    s = u ** (1.0 / RG_C)
    rg_lambda = jnp.log(s) - jnp.log1p(-s)
    return {
        "x": nrm(ks[0], (BATCH, SEQ, D_MODEL), 1.0),
        "p": nrm(ks[1], (DEPTH, BATCH, SEQ, PLE_DIM), 1.0),
        "norm_mix": 1.0 + nrm(ks[2], (DEPTH, D_MODEL), 0.05),
        "w_in": nrm(ks[3], (DEPTH, D_MODEL, IN_COLS), D_MODEL ** -0.5),
        "conv_w": nrm(ks[4], (DEPTH, CONV_WIDTH, D_RNN), CONV_WIDTH ** -0.5),
        "conv_b": nrm(ks[5], (DEPTH, D_RNN), 0.01),
        "w_rg_a": nrm(ks[6], (DEPTH, RG_BLOCKS, RG_BLOCK_DIM, RG_BLOCK_DIM), RG_BLOCK_DIM ** -0.5),
        "b_rg_a": nrm(ks[7], (DEPTH, D_RNN), 0.01),
        "w_rg_x": nrm(ks[8], (DEPTH, RG_BLOCKS, RG_BLOCK_DIM, RG_BLOCK_DIM), RG_BLOCK_DIM ** -0.5),
        "b_rg_x": nrm(ks[9], (DEPTH, D_RNN), 0.01),
        "rg_lambda": rg_lambda,
        "w_attn_o": nrm(ks[12], (DEPTH, D_ATTN, D_MODEL), D_ATTN ** -0.5),
        "w_rnn_o": nrm(ks[13], (DEPTH, D_RNN, D_MODEL), D_RNN ** -0.5),
        "w_out": nrm(ks[14], (DEPTH, D_MODEL, D_MODEL), D_MODEL ** -0.5),
        "norm_moe": 1.0 + nrm(ks[15], (DEPTH, D_MODEL), 0.05),
        "w_router_group": nrm(ks[16], (DEPTH, D_MODEL, N_GROUPS), D_MODEL ** -0.5),
        "b_router_group": nrm(ks[17], (DEPTH, N_GROUPS), 0.01),
        "w_router_expert": nrm(ks[18], (DEPTH, D_MODEL, N_EXPERTS), D_MODEL ** -0.5),
        "b_router_expert": nrm(ks[19], (DEPTH, N_EXPERTS), 0.01),
        "w_exp_gate": nrm(ks[20], (DEPTH, N_EXPERTS, D_MODEL, D_EXPERT), D_MODEL ** -0.5),
        "w_exp_up": nrm(ks[21], (DEPTH, N_EXPERTS, D_MODEL, D_EXPERT), D_MODEL ** -0.5),
        "w_exp_down": nrm(ks[22], (DEPTH, N_EXPERTS, D_EXPERT, D_MODEL), D_EXPERT ** -0.5),
        "norm_ple": 1.0 + nrm(ks[23], (DEPTH, D_MODEL), 0.05),
        "w_ple_gate": nrm(ks[24], (DEPTH, D_MODEL, D_MODEL), D_MODEL ** -0.5),
        "w_ple_proj": nrm(ks[25], (DEPTH, PLE_DIM, D_MODEL), PLE_DIM ** -0.5),
        "norm_final": 1.0 + nrm(ks[26], (D_MODEL,), 0.05),
    }

def reference(x, p, norm_mix, w_in, conv_w, conv_b, w_rg_a, b_rg_a, w_rg_x, b_rg_x,
              rg_lambda, w_attn_o, w_rnn_o, w_out, norm_moe, w_router_group,
              b_router_group, w_router_expert, b_router_expert, w_exp_gate, w_exp_up,
              w_exp_down, norm_ple, w_ple_gate, w_ple_proj, norm_final):
    for i in range(DEPTH):
        h = rms_norm(x, norm_mix[i])
        proj = h @ w_in[i]
        q, k, v, xr, xg, gate_attn, gate_rnn = jnp.split(proj, SPLIT_POINTS, axis=-1)
        y_attn = stick_breaking_attention(q, k, v) @ w_attn_o[i]
        y_rnn = rg_lru_branch(xr, xg, conv_w[i], conv_b[i], w_rg_a[i], b_rg_a[i],
                              w_rg_x[i], b_rg_x[i], rg_lambda[i]) @ w_rnn_o[i]
        merged = jax.nn.sigmoid(gate_attn) * y_attn + jax.nn.sigmoid(gate_rnn) * y_rnn
        x = x + merged @ w_out[i]
        h = rms_norm(x, norm_moe[i])
        x = x + hierarchical_moe(h, w_router_group[i], b_router_group[i],
                                 w_router_expert[i], b_router_expert[i],
                                 w_exp_gate[i], w_exp_up[i], w_exp_down[i])
        gate = jax.nn.sigmoid(rms_norm(x, norm_ple[i]) @ w_ple_gate[i])
        x = x + gate * (p[i] @ w_ple_proj[i])
    return rms_norm(x, norm_final)


_drawn_inputs = setup_inputs


def setup_inputs(seed=0):
    import zlib

    import numpy as np

    out = dict(_drawn_inputs(seed))
    spreads = {}
    factors = {'b_rg_a': 32.283,
     'b_rg_x': 24.94,
     'b_router_group': 8.0,
     'b_router_expert': 6.612,
     'norm_ple': 6.815}
    for name, (base, spread) in spreads.items():
        noise = np.random.default_rng([zlib.crc32(name.encode()), seed]).standard_normal(out[name].shape)
        drawn = base * np.exp(spread * noise) if base else spread * noise
        out[name] = __import__('jax').numpy.asarray(drawn.astype(out[name].dtype))
    for name, factor in factors.items():
        out[name] = (out[name] * factor).astype(out[name].dtype)
    return out
```

```python
from contextlib import ExitStack

import concourse.bass as bass
from concourse import mybir

ALU = mybir.AluOpType
ACT = mybir.ActivationFunctionType
F32 = mybir.dt.float32
F32R = mybir.dt.float32r
I32 = mybir.dt.int32
U32 = mybir.dt.uint32
AX = mybir.AxisListType.X

P = 128
KB = 1024
BIG = 1e30
EPS = 1e-6
RAW_SLOTS = 4
SPLIT_SLOTS = 3
CH = 2048
DVE_COLS = 1536


class Banks:

    def __init__(self):
        self.full = [0] * 8
        self.free = [0] * 8
        self.at = {}

    def take(self, key, bank, fills=1, ends=None):
        self.at[key] = (bank, self.free[bank], self.full[bank], ends)
        self.full[bank] += fills if ends is None else 0
        self.free[bank] += 1


def trunk(nc, x, p, norm_mix, w_in, conv_w, conv_b, w_rg_a, b_rg_a, w_rg_x, b_rg_x, rg_lambda,
          w_attn_o, w_rnn_o, w_out, norm_moe, w_router_group, b_router_group, w_router_expert,
          b_router_expert, w_exp_gate, w_exp_up, w_exp_down, norm_ple, w_ple_gate, w_ple_proj,
          norm_final, out):
    _, S, D = x.shape
    T = S // P
    KD = D // P
    DA = w_attn_o.shape[1]
    DR = w_rnn_o.shape[1]
    HD = 64
    H = DA // HD
    NG = w_router_group.shape[2]
    NE = w_exp_gate.shape[1]
    NL = NG + NE
    PD = p.shape[3]
    HALF = 512
    RB = DR // P
    GW = w_rg_a.shape[2]
    CW = conv_w.shape[1]
    SCALE = float(HD) ** -0.5
    assert T * P == HALF and KD == 8 and H == 8 and GW * 2 == P and NE % 2 == 0

    gates_d = nc.dram_tensor("gates_scratch", (2 * KD, P, S), F32).ap()
    h2_d = nc.dram_tensor("h2_scratch", (S, D), F32).ap()
    y_d = nc.dram_tensor("expert_out_scratch", (NE * P, D), F32).ap()
    OVER = S // P - 1
    y_over_d = nc.dram_tensor("expert_over_scratch", (NE * OVER * P, D), F32).ap()
    token_of_d = nc.dram_tensor("token_of_scratch", (NE * S, 1), I32).ap()

    first_col = {"q": 0, "k": DA, "v": 2 * DA, "xr": 3 * DA, "xg": 3 * DA + DR,
                 "ga": 3 * DA + 2 * DR, "gr": 3 * DA + 2 * DR + D}
    IN_ORDER = ([("xr", 0), ("xg", 0), ("xr", 1), ("xg", 1), ("q", 0), ("k", 0), ("v", 0)]
                + [("ga", n) for n in range(4)] + [("q", 1), ("k", 1), ("v", 1)]
                + [("gr", n) for n in range(4)])
    chunk_of = {key: c for c, key in enumerate(IN_ORDER)}
    chunks = [w_in[0, :, first_col[key] + 256 * n:first_col[key] + 256 * n + 256]
              .rearrange("(p k) n -> p k n", k=KD) for key, n in IN_ORDER]
    for n in range(2):
        for key, w in (("ao", w_attn_o), ("ro", w_rnn_o)):
            chunk_of[key, n] = len(chunks)
            chunks.append(w[0, :, HALF * n:HALF * n + HALF].rearrange("(k p) n -> p k n", p=P))
    for n in range(2):
        for k in range(2):
            chunk_of["wo", n, k] = len(chunks)
            chunks.append(w_out[0, HALF * k:HALF * k + HALF, HALF * n:HALF * n + HALF]
                          .rearrange("(k p) n -> p k n", p=P))
    C_MOE = len(chunks)
    PER_E = 6
    PER_IT = 2 * PER_E
    assert PER_IT % RAW_SLOTS == 0 and PER_IT % SPLIT_SLOTS == 0
    C_TAIL = C_MOE + PER_E * NE
    proj_tail = w_ple_proj[0].rearrange("(p k) n -> p k n", k=PD // P)
    gate_tail = w_ple_gate[0].rearrange("(p k) n -> p k n", k=KD)
    tail_chunks = [proj_tail] + [gate_tail[:, 4 * k:4 * k + 4, HALF * n:HALF * n + HALF]
                                 for n in range(2) for k in range(2)]
    C_END = C_TAIL + len(tail_chunks)

    def step_base(e):
        return C_MOE + 2 + PER_E * e

    def gate_src(e, half):
        return w_exp_gate[0, e].rearrange("(p k) n -> p k n", k=KD)[:, 4 * half:4 * half + 4, :]

    banks = Banks()
    banks.take("params", 2)
    for k in range(KD):
        banks.take(("hT", k), k)
    ring = 0
    JOBS = []

    def add(job, bank=None, fills=1):
        nonlocal ring
        if bank is None:
            bank, ring = ring % 2, ring + 1
        banks.take(job, bank, fills, ends=chunk_ended_by(job))
        JOBS.append(job)

    def chunk_ended_by(job):
        kind = job[0]
        if kind in ("xr", "xg") and job[1] % 2 == 1:
            return chunk_of[kind, job[1] // 2]
        if kind in ("q", "k", "v") and job[2] == 1:
            return chunk_of[kind, job[1]]
        if kind == "g" and job[1] % 2 == 1:
            n = job[1] // 2
            return chunk_of["ga", n] if n < 4 else chunk_of["gr", n - 4]
        return None

    def add_rg(m):
        banks.take(("rga", m), 2)
        banks.take(("rgx", m), 3)
        JOBS.append(("rg", m))

    for m in (0, 1):
        add(("xr", m))
    for m in (0, 1):
        add(("xg", m))
    for m in (2, 3):
        add_rg(m - 2)
        add(("xr", m))
    for m in (2, 3):
        add(("xg", m))
    for g in range(2):
        for b in range(2):
            add(("q", g, b))
        if g == 0:
            add_rg(2)
        for b in range(2):
            add(("k", g, b))
        if g == 0:
            add_rg(3)
        for b in range(2):
            add(("v", g, b))
        fillers = [("g", m) for m in range(8 * g, 8 * g + 8)]

        def add_z(h):
            for i in range(T):
                banks.take(("z", h, i), 2 + i, fills=2)
            JOBS.append(("z", h))

        for h in range(4 * g, 4 * g + 4):
            if h == 4 * g:
                add_z(h)
            add(fillers.pop(0))
            JOBS.append(("suf", h))
            add(fillers.pop(0))
            if h % 4 != 3:
                add_z(h + 1)
            add(("pv", h), 6 + h % 2)
    for m in range(KD):
        last = m % 4 == 3
        banks.take(("ya", m), m % 2, ends=chunk_of["ao", m // 4] if last else None)
        banks.take(("yr", m), 2 + m % 2, ends=chunk_of["ro", m // 4] if last else None)
    for n in range(2):
        for i in range(T):
            banks.take(("x2", n, i), (4 + i) if n == 0 else i,
                       ends=chunk_of["wo", n, 1] if i == T - 1 else None)
    for k in range(KD):
        banks.take(("h2T", k), (4 + k) % 8)
    banks.take("logits", 0)
    banks.take("pos", 1)
    banks.take(("XT", "first"), 4)
    banks.take(("XT2", "first"), 5)
    banks.take(("G", "first"), 0, ends=C_MOE + 1)
    per_free = [1, 1, 2, 2, 2, 2, 2, 2]
    per_full = [0, 0, 0, 2, 2, 2, 2, 0]

    def take_step(par, last=False):
        c = step_base(par)
        if not last:
            banks.take(("XT", par), 4)
            banks.take(("XT2", par), 5)
        banks.take(("U", par), 2, ends=c + 1)
        if not last:
            banks.take(("G", par), (par + 1) % 2, ends=c + 3)
            c += 2
        banks.take(("heT", par), 3)
        banks.take(("Y", par, 0), 6)
        banks.take(("Y", par, 1), 7, ends=c + 3)

    keep = {}
    for e in range(NE):
        take_step(e % 2, last=(e == NE - 1))
        if e == 1:
            keep = dict(banks.at)
    banks.at = {**banks.at, **keep}
    free_after_experts = list(banks.free)
    banks.at[("Y", "last", 1)] = (*banks.at[("Y", 1, 1)][:3], banks.at[("Y", 1, 1)][3] - 2)
    for k in range(PD // P):
        banks.take(("pT", k), k)
    for i in range(T):
        for n in range(2):
            banks.take(("pp", i, n), 2 + (2 * i + n) % 6, ends=C_TAIL if (i, n) == (T - 1, 1) else None)
    for k in range(KD):
        banks.take(("h3T", k), k)
    for n in range(2):
        for i in range(T):
            banks.take(("pg", n, i), 4 * n + i, ends=C_TAIL + 2 + 2 * n if i == T - 1 else None)

    with ExitStack() as ctx:
        def sem(name):
            return ctx.enter_context(nc.semaphore(name))

        SLAB = 207 * KB
        ctx.enter_context(nc.sbuf_tensor("slab", [P, SLAB // 4], F32))
        origin = nc.sbuf_base - SLAB
        BYTES = 4

        def at(name, shape, offset, dt=F32):
            n = BYTES
            for d in shape[1:]:
                n *= d
            assert offset + n <= SLAB, name
            return nc.alloc_sbuf_tensor_at(name, shape, dt, offset=origin + offset)

        RAW0, HI0, LO0 = 0, 32 * KB, 56 * KB
        C0 = 80 * KB
        RA = 86 * KB
        RQ = RA + 32 * KB
        RO = RQ + 24 * KB
        RR = RO + 16 * KB
        RT = RR + 16 * KB

        raw = [at(f"raw{s}", [P, CH], RAW0 + 8 * KB * s) for s in range(RAW_SLOTS)]
        whi = [at(f"whi{s}", [P, CH], HI0 + 8 * KB * s, F32R) for s in range(SPLIT_SLOTS)]
        wlo = [at(f"wlo{s}", [P, CH], LO0 + 8 * KB * s, F32R) for s in range(SPLIT_SLOTS)]

        off = C0

        def small(name, shape, dt=F32):
            nonlocal off
            t = at(name, shape, off, dt)
            n = BYTES
            for d in shape[1:]:
                n *= d
            off += (n + 31) // 32 * 32
            assert off <= RA
            return t

        ident = small("ident", [P, P])
        ident_r = small("ident_r", [P, P], F32R)
        ones = small("ones", [P, P])
        before = small("before", [P, P])
        neg_from = small("neg_from", [P, P], F32R)
        neg_all = small("neg_all", [P, P], F32R)
        hidden = small("hidden", [P, P], F32R)
        g_mix = small("g_mix", [P, KD])
        g_ple = small("g_ple", [P, KD])
        params = small("params", [P, CW * RB + 4 * RB])
        lam = small("lam", [P, 6, RB])
        decay = small("decay", [P, RB])
        neghalf_col = small("neghalf_col", [P, 1])
        ss = small("ss", [P, 4, T])
        ms = small("ms", [P, 4, T])
        rstd = small("rstd", [P, 4, T])
        combine_w = small("combine_w", [P, 2, T])
        over_w = small("over_w", [P, 2, T])
        over_slot_i = small("over_slot_i", [P, 2, T], I32)
        slot_i = small("slot_i", [P, 2, T], I32)
        addr_i = small("addr_i", [P, 2, T], I32)
        token_id = small("token_id", [P, T], I32)
        token_of = small("token_of", [P, 4 * NE], I32)
        idx_now = [small(f"idx_now{s}", [P, 1], I32) for s in range(2)]
        most_i = small("most_i", [P, 1], I32)

        hT_hi = at("hT_hi", [P, KD, S], RA, F32R)
        hT_lo = at("hT_lo", [P, KD, S], RA + 16 * KB, F32R)
        x_sb = at("x_sb", [P, T, D], RQ)
        junk = at("junk", [P, D], RQ + 16 * KB)
        par_rows = at("par_rows", [CW * RB + 4 * RB, P], RQ + 20 * KB)
        wg_raw = [at(f"wg_raw{s}", [P, RB, P], RO + 2 * KB * s) for s in range(2)]
        wg_hi = [at(f"wg_hi{s}", [P, RB, P], RO + 4 * KB + 2 * KB * s, F32R) for s in range(2)]
        wg_lo = [at(f"wg_lo{s}", [P, RB, P], RO + 8 * KB + 2 * KB * s, F32R) for s in range(2)]
        q_hi = at("q_hi", [P, 2, S], RQ, F32R)
        q_lo = at("q_lo", [P, 2, S], RQ + 4 * KB, F32R)
        k_hi = at("k_hi", [P, 2, S], RQ + 8 * KB, F32R)
        k_lo = at("k_lo", [P, 2, S], RQ + 12 * KB, F32R)
        v_hi = at("v_hi", [P, T, 256], RQ + 16 * KB, F32R)
        v_lo = at("v_lo", [P, T, 256], RQ + 20 * KB, F32R)
        o_hi = at("o_hi", [P, H // 2, S], RO, F32R)
        o_lo = at("o_lo", [P, H // 2, S], RO + 8 * KB, F32R)
        r_hi = at("r_hi", [P, RB, S], RR, F32R)
        r_lo = at("r_lo", [P, RB, S], RR + 8 * KB, F32R)
        XRW = S + CW - 1
        xrp = [at(f"xrp{s}", [P, XRW], RT + 2080 * s) for s in range(2)]
        t0 = RT + 2080 * 2
        xgs = [at(f"xgs{s}", [P, S], t0 + 2 * KB * s) for s in range(2)]
        xc = [at(f"xc{s}", [P, S], t0 + 2 * KB * (2 + s)) for s in range(2)]
        xc_hi = [at(f"xc_hi{s}", [P, S], t0 + 2 * KB * (4 + s), F32R) for s in range(2)]
        xc_lo = [at(f"xc_lo{s}", [P, S], t0 + 2 * KB * (6 + s), F32R) for s in range(2)]
        th, inp, rec, aa, bb, ge = [at(n, [P, S], t0 + 2 * KB * (8 + j)) for j, n in
                                    enumerate(("th", "inp", "rec", "aa", "bb", "ge"))]
        width = [S - P * i for i in range(T)]
        start = [sum(width[:i]) for i in range(T)]
        W5 = sum(width)
        za = at("za", [P, W5], RT)
        ze = at("ze", [P, W5], RT + 5 * KB)
        zs = at("zs", [P, W5], RT + 10 * KB)
        zs_hi = at("zs_hi", [P, W5], RT + 15 * KB, F32R)
        zs_lo = at("zs_lo", [P, W5], RT + 20 * KB, F32R)
        STAGES = 4
        stage = [at(f"stage{s}", [P, S], RT + 25 * KB + 2 * KB * s) for s in range(STAGES)]
        gate_a = at("gate_a", [P, KD, S], RT)
        gate_r = at("gate_r", [P, KD, S], RT + 16 * KB)
        m_hi = at("m_hi", [P, KD, S], RA, F32R)
        m_lo = at("m_lo", [P, KD, S], RA + 16 * KB, F32R)
        x2 = at("x2", [P, T, D], RQ)
        gB = at("gB", [P, D], RQ + 20 * KB)
        h2 = at("h2", [P, T, D], RR)
        h2T = at("h2T", [P, KD, S], RO)
        off_r = RT

        def route(name, shape, dt=F32):
            nonlocal off_r
            t = at(name, shape, off_r, dt)
            n = BYTES
            for d in shape[1:]:
                n *= d
            off_r += (n + 31) // 32 * 32
            assert off_r <= RT + 5 * KB
            return t

        X = [at(f"X{s}", [P, D], RA + 4 * KB * s) for s in range(2)]
        XT_hi = [at(f"XT_hi{s}", [P, KD, P], RA + 8 * KB + 4 * KB * s, F32R) for s in range(2)]
        XT_lo = [at(f"XT_lo{s}", [P, KD, P], RA + 16 * KB + 4 * KB * s, F32R) for s in range(2)]
        Y = [at(f"Y{s}", [P, D], RA + 24 * KB + 4 * KB * s) for s in range(2)]
        KF = HALF // P
        sil = at("sil", [P, HALF], RT + 25 * KB)
        he = at("he", [P, HALF], RT + 27 * KB)
        heT_hi = at("heT_hi", [P, KF, P], RT + 29 * KB, F32R)
        heT_lo = at("heT_lo", [P, KF, P], RT + 31 * KB, F32R)
        over_raw = at("over_raw", [P, CH], RO)
        over_hi = at("over_hi", [P, CH], RO + 8 * KB, F32R)
        over_lo = at("over_lo", [P, CH], RO + 16 * KB, F32R)
        p_sb = at("p_sb", [P, T, PD], RT + 21 * KB)
        yg = [[at(f"yg{i}{k}", [P, D], RO + 4 * KB * (2 * i + k)) for k in range(2)] for i in range(T)]
        pp = at("pp", [P, T, D], RA)
        KP = PD // P
        pT_hi = at("pT_hi", [P, KP, S], RA + 16 * KB, F32R)
        pT_lo = at("pT_lo", [P, KP, S], RA + 20 * KB, F32R)
        sg = [at(f"sg{s}", [P, HALF], RA + 24 * KB + 2 * KB * s) for s in range(2)]
        junk2 = at("junk2", [P, D], RQ + 16 * KB)
        xn3 = at("xn3", [P, T, D], RT + 1 * KB + 4 * KB)
        h3_hi = at("h3_hi", [P, KD, S], RO, F32R)
        h3_lo = at("h3_lo", [P, KD, S], RR, F32R)

        w_route = route("w_route", [P, KD, NL])
        b_route = route("b_route", [1, NL])
        lg = route("lg", [P, T, NL])
        iota_i = route("iota_i", [P, NE], I32)
        rev = route("rev", [P, NE])
        e_base = route("e_base", [P, NE])
        eq = route("eq", [P, T, NE])
        cand = route("cand", [P, T, NE])
        mx = route("mx", [P, T])
        best = route("best", [P, T])
        in_group = route("in_group", [P, T, NG])
        dg = route("dg", [P, T, NG])
        gsum = route("gsum", [P, T])
        ggate = route("ggate", [P, T])
        el = route("el", [P, T, NE])
        pen = route("pen", [P, T, NG])
        M = route("M", [P, 2, T, NE])
        both = route("both", [P, T, NE])
        v12 = route("v12", [P, 2, T])
        dv = route("dv", [P, T])
        pos = route("pos", [P, T + 1, NE])
        slot = route("slot", [P, 2, T])
        place = route("place", [P, 2, T])
        over = route("over", [P, 2, T])
        ov2 = route("ov2", [P, 2, T])
        zero_i = at("zero_i", [P, 4 * NE], RR, I32)

        bank = [ctx.enter_context(nc.psum_tensor(f"bank{b}", [P, HALF], F32)) for b in range(8)]

        full = [sem(f"bank{b}_full") for b in range(8)]
        free = [sem(f"bank{b}_free") for b in range(8)]
        raw_in = [sem(f"raw{s}_in") for s in range(RAW_SLOTS)]
        hi_ready = sem("hi_ready")
        lo_dve = sem("lo_dve_ready")
        lo_pool = sem("lo_pool_ready")
        w_used = sem("w_used")
        x_in = [sem(f"x_in{i}") for i in range(T)]
        params_in = sem("params_in")
        rg_weights_in = sem("rg_weights_in")
        rg_zeroed = sem("rg_zeroed")
        consts_made = sem("consts_made")
        consts_cast = sem("consts_cast")
        ss_done = sem("ss_done")
        ms_done = sem("ms_done")
        rstd_done = sem("rstd_done")
        xn_ready = sem("xn_ready")
        hT_hi_ready = sem("hT_hi_ready")
        hT_ready = sem("hT_ready")
        lam_exp = sem("lam_exp")
        decay_ready = sem("decay_ready")
        rg_w_ready = sem("rg_w_ready")
        xg_ready = sem("xg_ready")
        xc_ready = sem("xc_ready")
        th_ready = sem("th_ready")
        root_ready = sem("root_ready")
        ge_sq = sem("ge_sq")
        ge_in = sem("ge_in")
        ge_th = sem("ge_th")
        rg_done = sem("rg_done")
        qkv_hi = sem("qkv_hi_ready")
        qkv_ready = sem("qkv_ready")
        stage_out = [sem(f"stage{s}_out") for s in range(STAGES)]
        ln_ready = sem("ln_ready")
        sp_hi_ready = sem("sp_hi_ready")
        sp_lo_ready = sem("sp_lo_ready")
        wt_ready = sem("wt_ready")
        wt_hi_ready = sem("wt_hi_ready")
        wt_lo_ready = sem("wt_lo_ready")
        o_hi_ready = sem("o_hi_ready")
        gates_in = [sem("gates_a_in"), sem("gates_r_in")]
        sig_ready = sem("sig_ready")
        merged_ready = sem("merged_ready")
        x_again = sem("x_again")
        gB_in = sem("gB_in")
        small_in = sem("small_in")
        route_made = sem("route_made")
        h2_ready = sem("h2_ready")
        h2_out = sem("h2_out")
        gexp_in = sem("gexp_in")
        gexp_ready = sem("gexp_ready")
        vexp_in = sem("vexp_in")
        vexp_ready = sem("vexp_ready")
        both_ready = sem("both_ready")
        slots_ready = sem("slots_ready")
        rows_ready = sem("rows_ready")
        table_zeroed = sem("table_zeroed")
        table_out = sem("table_out")
        table_in = sem("table_in")
        X_in = [sem(f"X{s}_in") for s in range(2)]
        XT_hi_ready = sem("XT_hi_ready")
        XT_ready = sem("XT_ready")
        sil_ready = sem("sil_ready")
        heT_hi_ready = sem("heT_hi_ready")
        heT_ready = sem("heT_ready")
        Y_out = [sem(f"Y{s}_out") for s in range(2)]
        p_in = sem("p_in")
        pT_hi_ready = sem("pT_hi_ready")
        pT_ready = sem("pT_ready")
        pp_ready = sem("pp_ready")
        yg_in = [sem(f"yg_in{i}") for i in range(T)]
        x3_ready = sem("x3_ready")
        xn3_ready = sem("xn3_ready")
        h3_hi_ready = sem("h3_hi_ready")
        h3_ready = sem("h3_ready")
        sg_ready = sem("sg_ready")
        x4_ready = sem("x4_ready")
        out_ready = sem("out_ready")
        out_done = sem("out_done")
        act_chain = sem("act_chain")
        dve_chain = sem("dve_chain")
        pool_chain = sem("pool_chain")
        index_ready = sem("index_ready")
        over_raw_in = sem("over_raw_in")
        over_hi_ready = sem("over_hi_ready")
        over_lo_ready = sem("over_lo_ready")
        over_used = sem("over_used")
        over_index = sem("over_index_ready")
        over_X_in = sem("over_X_in")
        over_XT = sem("over_XT_full")
        over_XT_hi = sem("over_XT_hi_ready")
        over_XT_ready = sem("over_XT_ready")
        over_sil = sem("over_sil_ready")
        over_he = sem("over_he_ready")
        over_heT = sem("over_heT_full")
        over_heT_hi = sem("over_heT_hi_ready")
        over_heT_ready = sem("over_heT_ready")
        over_Y_ready = sem("over_Y_ready")
        over_Y_out = sem("over_Y_out")
        over_rows_in = sem("over_rows_in")
        over_added = sem("over_added")

        block = ctx.enter_context(nc.Block())

        def wait_full(eng, key, nth=1, it=0):
            b, _, f, ends = banks.at[key]
            if ends is None:
                eng.wait_ge(full[b], f + nth + it * per_full[b])
            else:
                eng.wait_ge(w_used, ends + 1 + PER_IT * it)
            return bank[b]

        def wait_free(eng, key, it=0):
            b, r, _, _ = banks.at[key]
            if not isinstance(it, int) or r + it * per_free[b] > 0:
                eng.wait_ge(free[b], r + it * per_free[b])
            return bank[b]

        def wait_read(eng, key, it=0):
            b, r, _, _ = banks.at[key]
            eng.wait_ge(free[b], r + 1 + it * per_free[b])

        def full_of(key):
            b, _, _, ends = banks.at[key]
            return full[b] if ends is None else w_used

        def free_of(key):
            return free[banks.at[key][0]]

        def job_splits(job, done, split):
            kind = job[0]
            if kind in ("xr", "xg"):
                c = chunk_of[kind, job[1] // 2]
            elif kind in ("q", "k", "v"):
                c = chunk_of[kind, job[1]]
            elif kind == "g":
                n = job[1] // 2
                c = chunk_of["ga", n] if n < 4 else chunk_of["gr", n - 4]
            else:
                return done
            while done < c + 3:
                split(done)
                done += 1
            return done

        def further_tiles(eng, tile):
            with eng.Fori(0, NE) as e:
                with eng.Fori(0, OVER) as j:
                    tile(e, j + 1, e * OVER + j)

        def any_over(eng):
            eng.wait_ge(rows_ready, 1)
            return eng.value_load(most_i[0:1, 0:1], min_val=0, max_val=S) > P

        def chained(eng, chain):
            count = [0]

            def step(ins):
                ins.then_inc(chain, 1)
                count[0] += 1
                eng.wait_ge(chain, count[0])
            return step

        @block.sync
        def _(sp):
            for i in range(T):
                sp.dma_start(x_sb[:, i, :], x[0, P * i:P * i + P, :]).then_inc(x_in[i], 16)

            def load(c, it, src):
                s = c % RAW_SLOTS
                if c >= RAW_SLOTS:
                    sp.wait_ge(lo_dve, c + 1 - RAW_SLOTS + PER_IT * it)
                    sp.wait_ge(lo_pool, c + 1 - RAW_SLOTS + PER_IT * it)
                dst = raw[s][:].rearrange("p (k n) -> p k n", k=src.shape[1])
                sp.dma_start(dst, src).then_inc(raw_in[s], 16)

            def load_step(par, it, e, last=False):
                c = step_base(par)
                up = w_exp_up[0, e].rearrange("(p k) n -> p k n", k=KD)
                down = w_exp_down[0, e].rearrange("(p k) n -> p k n", k=KF)
                load(c, it, up[:, 0:4, :])
                load(c + 1, it, up[:, 4:8, :])
                if not last:
                    load(c + 2, it, gate_src(e + 1, 0))
                    load(c + 3, it, gate_src(e + 1, 1))
                    c += 2
                load(c + 2, it, down[:, 0:2, :])
                load(c + 3, it, down[:, 2:4, :])

            for c, src in enumerate(chunks):
                load(c, 0, src)
            for half in range(2):
                load(C_MOE + half, 0, gate_src(0, half))
            with sp.Fori(0, NE // 2 - 1) as it:
                load_step(0, it, it * 2)
                load_step(1, it, it * 2 + 1)
            load_step(0, NE // 2 - 1, NE - 2)
            load_step(1, NE // 2 - 1, NE - 1, last=True)
            for j, src in enumerate(tail_chunks):
                load(C_TAIL + j, 0, src)
            for i in range(T):
                sp.wait_ge(out_ready, i + 1)
                sp.dma_start(out[0, P * i:P * i + P, :], xn3[:, i, :]).then_inc(out_done, 16)
            sp.wait_ge(out_done, 16 * T)

        @block.gpsimd
        def _(pool):
            step = chained(pool, pool_chain)

            def lo_part(c, it=0):
                pool.wait_ge(hi_ready, c + 1 + PER_IT * it)
                pool.tensor_tensor(wlo[c % SPLIT_SLOTS][:, DVE_COLS:], raw[c % RAW_SLOTS][:, DVE_COLS:],
                                   whi[c % SPLIT_SLOTS][:, DVE_COLS:].bitcast(F32),
                                   ALU.subtract).then_inc(lo_pool, 1)

            def root_of_ms(norm, i):
                pool.wait_ge(ms_done, T * norm + i + 1)
                pool.tensor_tensor(rstd[:, norm, i:i + 1], ms[:, norm, i:i + 1], neghalf_col[:],
                                   ALU.pow).then_inc(rstd_done, 1)

            step(pool.memset(neghalf_col[:], -0.5))
            pool.memset(wg_raw[0][:], 0.0).then_inc(rg_zeroed, 1)
            pool.memset(wg_raw[1][:], 0.0).then_inc(rg_zeroed, 1)
            step(pool.memset(ones[:], 1.0))
            step(pool.affine_select(out=ident[:], in_=ones[:], compare_op=ALU.is_equal, fill=0.0,
                                    base=0, pattern=[[1, P]], channel_multiplier=-1))
            step(pool.affine_select(out=before[:], in_=ones[:], compare_op=ALU.is_gt, fill=0.0,
                                    base=0, pattern=[[1, P]], channel_multiplier=-1))
            step(pool.iota(token_id[:], pattern=[[P, T]], base=0, channel_multiplier=1))
            pool.memset(zero_i[:], 0).then_inc(consts_made, 1)
            pool.wait_ge(consts_made, 1)
            pool.dma_start(token_of_d.rearrange("(p j) o -> p (j o)", p=P), zero_i[:]).then_inc(table_zeroed, 16)
            for i in range(T):
                root_of_ms(0, i)
            lo_part(0)
            lo_part(1)

            done = 2
            for job in JOBS:
                done = job_splits(job, done, lo_part)
                if job[0] == "suf":
                    h = job[1]
                    pool.wait_ge(sp_hi_ready, h + 1)
                    pool.tensor_tensor(zs_lo[:], zs[:], zs_hi[:].bitcast(F32), ALU.subtract)\
                        .then_inc(sp_lo_ready, 1)
                if job[0] == "pv":
                    h = job[1]
                    pool.wait_ge(wt_hi_ready, h + 1)
                    pool.tensor_tensor(zs_lo[:], zs[:], zs_hi[:].bitcast(F32), ALU.subtract)\
                        .then_inc(wt_lo_ready, 1)
            for c in range(done, C_MOE + 2):
                lo_part(c)
            pool.wait_ge(merged_ready, KD)
            pool.iota(iota_i[:], pattern=[[1, NE]], base=0, channel_multiplier=0).then_inc(route_made, 1)
            for i in range(T):
                root_of_ms(1, i)
            lo_part(C_MOE + 2)
            pool.wait_ge(slots_ready, 1)
            pool.wait_ge(table_zeroed, 16)
            for k in range(2):
                for i in range(T):
                    pool.indirect_dma_start(token_of_d, bass.IndirectOffsetOnAxis(addr_i[:, k, i:i + 1].bitcast(U32), 0),
                                            token_id[:, i:i + 1], None).then_inc(table_out, 16)
            pool.wait_ge(table_out, 16 * 2 * T)
            pool.dma_start(token_of[:], token_of_d.rearrange("(p j) o -> p (j o)", p=P)).then_inc(table_in, 16)
            pool.wait_ge(table_in, 16)
            pool.wait_ge(h2_out, 16 * T)

            for par in range(2):
                step(pool.tensor_copy(idx_now[par][:], token_of[:, 4 * par:4 * par + 1]))
                pool.indirect_dma_start(X[par][:], None, h2_d,
                                        bass.IndirectOffsetOnAxis(idx_now[par][:].bitcast(U32), 0))\
                    .then_inc(X_in[par], 16)

            def pool_step(par, it, e, last=False, more=True):
                c = step_base(par)
                if more:
                    pool.wait_ge(table_in, 16)
                    wait_full(pool, ("XT2", "first") if par == 0 else ("XT2", 0), it=it)
                    pool.tensor_copy(idx_now[par][:], token_of[:, bass.ds(e * 4 + 8, 1)]).then_inc(index_ready, 1)
                    pool.wait_ge(index_ready, it * 2 + par + 1)
                lo_part(c + 2, it)
                if more:
                    pool.wait_ge(h2_out, 16 * T)
                    pool.indirect_dma_start(X[par][:], None, h2_d,
                                            bass.IndirectOffsetOnAxis(idx_now[par][:].bitcast(U32), 0))\
                        .then_inc(X_in[par], 16)
                for j in range(3, 6 if last else 8):
                    lo_part(c + j, it)

            lo_part(C_MOE + 3)
            with pool.Fori(0, NE // 2 - 1) as it:
                pool_step(0, it, it * 2)
                pool_step(1, it, it * 2 + 1)
            pool_step(0, NE // 2 - 1, NE - 2, more=False)
            pool_step(1, NE // 2 - 1, NE - 1, last=True, more=False)
            lo_part(C_TAIL + 2)

            def over_pool(e, j, n):
                pool.tensor_copy(idx_now[0][:], token_of[:, bass.ds(e * 4 + j, 1)]).then_inc(over_index, 1)
                pool.wait_ge(over_index, n + 1)
                for c in range(PER_E):
                    pool.wait_ge(over_hi_ready, n * PER_E + c + 1)
                    pool.tensor_tensor(over_lo[:], over_raw[:], over_hi[:].bitcast(F32), ALU.subtract)\
                        .then_inc(over_lo_ready, 1)
                    if c == 0:
                        pool.wait_ge(h2_out, 16 * T)
                        pool.indirect_dma_start(X[0][:], None, h2_d,
                                                bass.IndirectOffsetOnAxis(idx_now[0][:].bitcast(U32), 0))\
                            .then_inc(over_X_in, 16)
                    pool.wait_ge(over_used, n * PER_E + c + 1)

            with pool.If(any_over(pool)):
                wait_full(pool, ("XT2", 0), it=NE // 2 - 2)
                further_tiles(pool, over_pool)
                pool.wait_ge(over_Y_out, 16 * NE * OVER)
                for i in range(T):
                    for k in range(2):
                        pool.indirect_dma_start(yg[i][k][:], None, y_over_d,
                                                bass.IndirectOffsetOnAxis(over_slot_i[:, k, i:i + 1].bitcast(U32), 0))\
                            .then_inc(over_rows_in, 16)
                pool.wait_ge(over_added, 2 * T)
            for s in range(2):
                pool.wait_ge(Y_out[s], 16 * (NE // 2))
            for i in range(T):
                for k in range(2):
                    pool.indirect_dma_start(yg[i][k][:], None, y_d,
                                            bass.IndirectOffsetOnAxis(slot_i[:, k, i:i + 1].bitcast(U32), 0))\
                        .then_inc(yg_in[i], 16)
            for i in range(T):
                root_of_ms(2, i)
            for c in range(C_TAIL + 3, C_END):
                lo_part(c)
            for i in range(T):
                root_of_ms(3, i)

        @block.scalar
        def _(act):
            step = chained(act, act_chain)
            copy = ACT.Copy

            def hi_part(c, it=0):
                if c >= SPLIT_SLOTS:
                    act.wait_ge(w_used, c + 1 - SPLIT_SLOTS + PER_IT * it)
                act.wait_ge(raw_in[c % RAW_SLOTS], 16 * (c // RAW_SLOTS + 1 + PER_IT // RAW_SLOTS * it))
                act.activation(whi[c % SPLIT_SLOTS][:], raw[c % RAW_SLOTS][:], copy).then_inc(hi_ready, 1)

            def squares(norm, i, src, scrap):
                if T * norm + i > 0:
                    act.wait_ge(ss_done, T * norm + i)
                act.activation(scrap[:], src, ACT.Square, accum_out=ss[:, norm, i:i + 1]).then_inc(ss_done, 1)

            rows = [(conv_w[0].rearrange("j (m p) -> (j m) p", p=P), CW * RB)] + [
                (t[0].rearrange("(m p) -> m p", p=P), RB) for t in (conv_b, b_rg_a, b_rg_x, rg_lambda)]
            r0 = 0
            for src, n in rows:
                act.dma_start(par_rows[r0:r0 + n, :], src).then_inc(params_in, 16)
                r0 += n
            act.dma_start(g_mix[:], norm_mix[0].rearrange("(p k) -> p k", k=KD)).then_inc(params_in, 16)
            act.dma_start(g_ple[:], norm_ple[0].rearrange("(p k) -> p k", k=KD)).then_inc(params_in, 16)
            act.wait_ge(rg_zeroed, 2)
            for s, w in enumerate((w_rg_a, w_rg_x)):
                pairs = w[0].rearrange("(m a) i j -> a i m j", a=2)
                for a in range(2):
                    act.dma_start(wg_raw[s][GW * a:GW * a + GW, :, GW * a:GW * a + GW], pairs[a])\
                        .then_inc(rg_weights_in, 16)
            for i in range(T):
                act.wait_ge(x_in[i], 16)
                squares(0, i, x_sb[:, i, :], junk)
            wait_read(act, "params")
            step(act.activation(lam[:, 0, :], params[:, (CW + 3) * RB:(CW + 4) * RB], ACT.Abs))
            act.activation(lam[:, 1, :], lam[:, 0, :], ACT.Exp, scale=-1.0).then_inc(lam_exp, 1)
            hi_part(0)
            act.wait_ge(params_in, 16 * 7)
            for k in range(KD):
                b = wait_full(act, ("hT", k))
                act.activation(hT_hi[:, k, :], b[:], copy, scale=g_mix[:, k:k + 1]).then_inc(hT_hi_ready, 1)
            act.wait_ge(rg_weights_in, 64)
            for s in range(2):
                act.activation(wg_hi[s][:], wg_raw[s][:], copy).then_inc(rg_w_ready, 1)
            hi_part(1)
            done = 2
            gate_n = 0
            for job in JOBS:
                kind = job[0]
                done = job_splits(job, done, hi_part)
                if kind == "xr":
                    m = job[1]
                    b = wait_full(act, job)
                    if m >= 2:
                        act.wait_ge(rg_done, m - 1)
                    act.activation(xrp[m % 2][:, CW - 1:], b[:], copy).then_inc(free_of(job), 1)
                elif kind == "xg":
                    m = job[1]
                    b = wait_full(act, job)
                    if m >= 2:
                        act.wait_ge(rg_done, m - 1)
                    act.activation(xgs[m % 2][:], b[:], copy).then_inc(free_of(job), 1)
                elif kind == "rg":
                    m = job[1]
                    if m >= 1:
                        act.wait_ge(rg_done, m)
                    ba = params[:, (CW + 1) * RB + m:(CW + 1) * RB + m + 1]
                    bx = params[:, (CW + 2) * RB + m:(CW + 2) * RB + m + 1]
                    b = wait_full(act, ("rga", m))
                    act.activation(th[:], b[:], ACT.Sigmoid, bias=ba).then_inc(free_of(("rga", m)), 1)
                    b = wait_full(act, ("rgx", m))
                    act.activation(inp[:], b[:], ACT.Sigmoid, bias=bx).then_inc(free_of(("rgx", m)), 1)
                    wait_read(act, ("rga", m))
                    if m == 0:
                        act.wait_ge(decay_ready, 1)
                    act.activation(th[:], th[:], ACT.Tanh, scale=decay[:, m:m + 1]).then_inc(th_ready, 1)
                    wait_read(act, ("xg", m))
                    act.activation(ge[:], xgs[m % 2][:], ACT.Square).then_inc(ge_sq, 1)
                    act.wait_ge(ge_in, m + 1)
                    act.activation(ge[:], ge[:], ACT.Tanh, scale=0.7978845608028654).then_inc(ge_th, 1)
                    act.wait_ge(th_ready, m + 1)
                    act.activation(bb[:], th[:], ACT.Sqrt).then_inc(root_ready, 1)
                elif kind in ("q", "k", "v"):
                    _, g, j = job
                    b = wait_full(act, job)
                    dst = {"q": q_hi, "k": k_hi, "v": v_hi}[kind]
                    d = dst[:, 2 * j:2 * j + 2, :] if kind == "v" else dst[:, j, :]
                    src = b[:].rearrange("p (a n) -> p a n", a=2) if kind == "v" else b[:]
                    if g == 1:
                        wait_read(act, ("pv", 2))
                        wait_read(act, ("pv", 3))
                    act.activation(d, src, copy, scale=SCALE if kind == "q" else 1.0).then_inc(qkv_hi, 1)
                elif kind == "g":
                    s = gate_n % STAGES
                    b = wait_full(act, job)
                    if gate_n >= STAGES:
                        act.wait_ge(stage_out[s], 16 * (gate_n // STAGES))
                    if gate_n == 0:
                        act.wait_ge(rg_done, RB)
                    act.activation(stage[s][:], b[:], copy).then_inc(free_of(job), 1)
                    wait_read(act, job)
                    act.dma_start(gates_d[job[1]], stage[s][:]).then_inc(stage_out[s], 16)
                    gate_n += 1
                elif kind == "z":
                    h = job[1]
                    if h == 0:
                        act.wait_ge(rg_done, RB)
                    for i in range(T):
                        b = wait_full(act, ("z", h, i))
                        ins = act.activation(za[:, start[i]:start[i] + width[i]], b[:, 0:width[i]], ACT.Abs)
                    step(ins)
                    if h > 0:
                        act.wait_ge(sp_hi_ready, h)
                    step(act.activation(ze[:], za[:], ACT.Exp, scale=-1.0))
                    act.activation(ze[:], ze[:], ACT.Ln, bias=1.0).then_inc(ln_ready, 1)
                elif kind == "suf":
                    h = job[1]
                    for i in range(T):
                        b = wait_full(act, ("z", h, i), nth=2)
                        act.activation(zs[:, start[i]:start[i] + width[i]], b[:, 0:width[i]],
                                       ACT.Exp).then_inc(free_of(("z", h, i)), 1)
                elif kind == "pv":
                    h = job[1]
                    pr, s = h // 2, h % 2
                    b = wait_full(act, job)
                    act.activation(o_hi[HD * s:HD * s + HD, pr, :], b[HD * s:HD * s + HD, :], copy)\
                        .then_inc(o_hi_ready, 1)
            wait_read(act, ("pv", H - 2))
            wait_read(act, ("pv", H - 1))
            for i in range(T):
                act.dma_start(x2[:, i, :], x[0, P * i:P * i + P, :]).then_inc(x_again, 16)
            for s in range(STAGES):
                act.wait_ge(stage_out[s], 16 * (2 * KD // STAGES))
            for g, t in enumerate((gate_a, gate_r)):
                act.dma_start(t[:], gates_d[KD * g:KD * g + KD].rearrange("m p t -> p m t")).then_inc(gates_in[g], 16)
            act.dma_start(gB[:], norm_moe[0:1, :].broadcast_to([P, D])).then_inc(gB_in, 16)
            for c in range(done, chunk_of["ao", 0] + 3):
                hi_part(c)
            done = chunk_of["ao", 0] + 3
            act.wait_ge(gates_in[0], 16)
            act.wait_ge(gates_in[1], 16)
            for m in range(KD):
                act.activation(gate_a[:, m, :], gate_a[:, m, :], ACT.Sigmoid).then_inc(sig_ready, 1)
                act.activation(gate_r[:, m, :], gate_r[:, m, :], ACT.Sigmoid).then_inc(sig_ready, 1)
            for c in range(done, C_MOE + 3):
                hi_part(c)
            act.wait_ge(merged_ready, KD)
            act.dma_start(w_route[:, :, 0:NG], w_router_group[0].rearrange("(p k) n -> p k n", k=KD)).then_inc(small_in, 16)
            act.dma_start(w_route[:, :, NG:NL], w_router_expert[0].rearrange("(p k) n -> p k n", k=KD)).then_inc(small_in, 16)
            act.dma_start(b_route[:, 0:NG], b_router_group).then_inc(small_in, 16)
            act.dma_start(b_route[:, NG:NL], b_router_expert).then_inc(small_in, 16)
            act.dma_start(p_sb[:], p[0, 0].rearrange("(i p) n -> p i n", p=P)).then_inc(p_in, 16)
            for i in range(T):
                wait_read(act, ("x2", 0, i))
                wait_read(act, ("x2", 1, i))
                squares(1, i, x2[:, i, :], junk2)
            for i in range(T):
                act.wait_ge(h2_ready, i + 1)
                act.dma_start(h2_d[P * i:P * i + P, :], h2[:, i, :]).then_inc(h2_out, 16)
            for k in range(0, KD, 2):
                b = wait_full(act, ("h2T", k))
                act.activation(h2T[:, k, :], b[:], copy).then_inc(free_of(("h2T", k)), 1)
            act.wait_ge(gexp_in, 1)
            act.activation(dg[:], dg[:], ACT.Exp).then_inc(gexp_ready, 1)
            act.wait_ge(vexp_in, 1)
            act.activation(dv[:], dv[:], ACT.Exp).then_inc(vexp_ready, 1)

            def evict_XT(key, par, it, n):
                for a, bk in enumerate(("XT", "XT2")):
                    b = wait_full(act, (bk, key), it=it)
                    act.activation(XT_hi[par][:, 4 * a:4 * a + 4, :], b[:].rearrange("p (k t) -> p k t", t=P),
                                   copy).then_inc(XT_hi_ready, 1)

            evict_XT("first", 0, 0, 0)
            hi_part(C_MOE + 3)

            def act_step(par, it, last=False):
                gkey = ("G", "first") if par == 0 else ("G", 0)
                b = wait_full(act, gkey, it=it)
                wait_free(act, ("U", par), it=it)
                act.activation(sil[:], b[:], ACT.Silu).then_inc(free_of(gkey), 1)
                if not last:
                    evict_XT(par, 1 - par, it, 0)
                c = step_base(par)
                hi_part(c + 2, it)
                hi_part(c + 3, it)
                if not last:
                    hi_part(c + 4, it)
                    hi_part(c + 5, it)
                    c += 2
                b = wait_full(act, ("heT", par), it=it)
                act.activation(heT_hi[:], b[:].rearrange("p (k t) -> p k t", t=P), copy).then_inc(heT_hi_ready, 1)
                hi_part(c + 4, it)
                hi_part(c + 5, it)
                b = wait_full(act, ("Y", par, 0), it=it)
                if not isinstance(it, int) or it > 0:
                    act.wait_ge(Y_out[par], it * 16)
                act.activation(Y[par][:, 0:HALF], b[:], copy).then_inc(free_of(("Y", par, 0)), 1)
                wait_read(act, ("Y", par, 0), it=it)
                wait_read(act, ("Y", par, 1), it=it)
                act.dma_start(y_d.rearrange("(e r) d -> e r d", e=NE)[it * 2 + par, 0:P, :], Y[par][:])\
                    .then_inc(Y_out[par], 16)

            act_step(0, 0)
            act_step(1, 0)
            with act.Fori(1, NE // 2 - 1) as it:
                act_step(0, it)
                act_step(1, it)
            act_step(0, NE // 2 - 1)
            act_step(1, NE // 2 - 1, last=True)
            hi_part(C_TAIL + 2)

            def over_act(e, j, n):
                gate, up = [w[0, e].rearrange("(p k) n -> p k n", k=KD) for w in (w_exp_gate, w_exp_up)]
                down = w_exp_down[0, e].rearrange("(p k) n -> p k n", k=KF)
                parts = [gate[:, 0:4, :], gate[:, 4:8, :], up[:, 0:4, :], up[:, 4:8, :],
                         down[:, 0:2, :], down[:, 2:4, :]]

                def hi(c):
                    act.dma_start(over_raw[:].rearrange("p (k n) -> p k n", k=parts[c].shape[1]), parts[c])\
                        .then_inc(over_raw_in, 16)
                    act.wait_ge(over_raw_in, n * (16 * PER_E) + 16 * (c + 1))
                    act.activation(over_hi[:], over_raw[:], copy).then_inc(over_hi_ready, 1)
                    if c == 0:
                        act.wait_ge(over_XT, n + 1)
                        for a in range(2):
                            act.activation(XT_hi[0][:, 4 * a:4 * a + 4, :],
                                           bank[4 + a][:].rearrange("p (k t) -> p k t", t=P), copy)\
                                .then_inc(over_XT_hi, 1)
                    if c == 3:
                        act.wait_ge(over_used, n * PER_E + 2)
                        act.activation(sil[:], bank[0][:], ACT.Silu).then_inc(over_sil, 1)
                        act.wait_ge(over_heT, n + 1)
                        act.activation(heT_hi[:], bank[3][:].rearrange("p (k t) -> p k t", t=P), copy)\
                            .then_inc(over_heT_hi, 1)
                    act.wait_ge(over_used, n * PER_E + c + 1)
                for c in range(PER_E):
                    hi(c)
                for h in range(2):
                    act.activation(Y[0][:, HALF * h:HALF * h + HALF], bank[6 + h][:], copy).then_inc(over_Y_ready, 1)
                act.wait_ge(over_Y_ready, n * 2 + 2)
                act.dma_start(y_over_d.rearrange("(n r) d -> n r d", r=P)[n], Y[0][:]).then_inc(over_Y_out, 16)
                act.wait_ge(over_Y_out, n * 16 + 16)

            with act.If(any_over(act)):
                act.wait_ge(h2_out, 16 * T)
                act.wait_ge(Y_out[0], 16 * (NE // 2))
                further_tiles(act, over_act)
            for k in range(KP):
                b = wait_full(act, ("pT", k))
                act.activation(pT_hi[:, k, :], b[:], copy).then_inc(pT_hi_ready, 1)
            for i in range(T):
                for n in range(2):
                    b = wait_full(act, ("pp", i, n))
                    act.activation(pp[:, i, HALF * n:HALF * n + HALF], b[:], copy).then_inc(free_of(("pp", i, n)), 1)
            act.dma_start(gB[:], norm_final.rearrange("(o n) -> o n", o=1).broadcast_to([P, D])).then_inc(gB_in, 16)
            for i in range(T):
                act.wait_ge(x3_ready, i + 1)
                squares(2, i, x2[:, i, :], junk2)
            for k in range(KD):
                b = wait_full(act, ("h3T", k))
                act.activation(h3_hi[:, k, :], b[:], copy, scale=g_ple[:, k:k + 1]).then_inc(h3_hi_ready, 1)
            for c in range(C_TAIL + 3, C_END):
                hi_part(c)
            for n in range(2):
                for i in range(T):
                    j = T * n + i
                    b = wait_full(act, ("pg", n, i))
                    if j >= 2:
                        act.wait_ge(x4_ready, j - 1)
                    act.activation(sg[j % 2][:], b[:], ACT.Sigmoid).then_inc(sg_ready, 1)
            for i in range(T):
                act.wait_ge(x4_ready, T + i + 1)
                squares(3, i, x2[:, i, :], junk2)

        @block.vector
        def _(dve):
            step = chained(dve, dve_chain)

            def lo_part(c, it=0):
                dve.wait_ge(hi_ready, c + 1 + PER_IT * it)
                dve.tensor_tensor(wlo[c % SPLIT_SLOTS][:, 0:DVE_COLS], raw[c % RAW_SLOTS][:, 0:DVE_COLS],
                                  whi[c % SPLIT_SLOTS][:, 0:DVE_COLS].bitcast(F32),
                                  ALU.subtract).then_inc(lo_dve, 1)

            def mean_sq(norm, i):
                dve.wait_ge(ss_done, T * norm + i + 1)
                dve.tensor_scalar(ms[:, norm, i:i + 1], ss[:, norm, i:i + 1], 1.0 / D, EPS,
                                  ALU.mult, ALU.add).then_inc(ms_done, 1)

            for i in range(T):
                mean_sq(0, i)
            for i in range(T):
                dve.wait_ge(rstd_done, i + 1)
                dve.tensor_scalar(x_sb[:, i, :], x_sb[:, i, :], rstd[:, 0, i:i + 1], None, ALU.mult)\
                    .then_inc(xn_ready, 1)
            dve.wait_ge(consts_made, 1)
            dve.tensor_copy(ident_r[:], ident[:]).then_inc(consts_cast, 1)
            dve.tensor_scalar(neg_all[:], ones[:], -1.0, None, ALU.mult).then_inc(consts_cast, 1)
            dve.tensor_scalar(neg_from[:], before[:], 1.0, None, ALU.subtract).then_inc(consts_cast, 1)
            dve.tensor_scalar(hidden[:], before[:], BIG, BIG, ALU.mult, ALU.subtract).then_inc(consts_cast, 1)
            b = wait_full(dve, "params")
            dve.tensor_copy(params[:], b[:, 0:(CW + 4) * RB]).then_inc(free_of("params"), 1)
            wait_read(dve, "params")
            lm = params[:, (CW + 3) * RB:(CW + 4) * RB]
            dve.wait_ge(lam_exp, 1)
            step(dve.tensor_scalar(lam[:, 2, :], lam[:, 1, :], 2.0, None, ALU.add))
            step(dve.reciprocal(lam[:, 2, :], lam[:, 2, :]))
            step(dve.tensor_tensor(lam[:, 2, :], lam[:, 1, :], lam[:, 2, :], ALU.mult))
            step(dve.tensor_tensor(lam[:, 3, :], lam[:, 2, :], lam[:, 2, :], ALU.mult))
            step(dve.tensor_scalar(lam[:, 4, :], lam[:, 3, :], 1.0 / 17, 1.0 / 15, ALU.mult, ALU.add))
            for n in (13, 11, 9, 7, 5, 3, 1):
                step(dve.tensor_tensor(lam[:, 4, :], lam[:, 4, :], lam[:, 3, :], ALU.mult))
                step(dve.tensor_scalar(lam[:, 4, :], lam[:, 4, :], 1.0 / n, None, ALU.add))
            step(dve.scalar_tensor_tensor(out=lam[:, 4, :], in0=lam[:, 4, :], scalar=8.0, in1=lam[:, 2, :],
                                          op0=ALU.mult, op1=ALU.mult))
            step(dve.tensor_scalar(lam[:, 5, :], lm, -4.0, 0.0, ALU.mult, ALU.max))
            dve.tensor_tensor(decay[:], lam[:, 4, :], lam[:, 5, :], ALU.add).then_inc(decay_ready, 1)
            lo_part(0)
            for k in range(KD):
                dve.wait_ge(hT_hi_ready, k + 1)
                b = wait_full(dve, ("hT", k))
                if k == 0:
                    dve.wait_ge(params_in, 16 * 7)
                dve.scalar_tensor_tensor(out=hT_lo[:, k, :], in0=b[:], scalar=g_mix[:, k:k + 1],
                                         in1=hT_hi[:, k, :].bitcast(F32), op0=ALU.mult, op1=ALU.subtract)\
                    .then_inc(free_of(("hT", k)), 1)
            dve.wait_ge(rg_w_ready, 2)
            for s in range(2):
                dve.tensor_tensor(wg_lo[s][:], wg_raw[s][:], wg_hi[s][:].bitcast(F32), ALU.subtract)\
                    .then_inc(rg_w_ready, 1)
            for s in range(2):
                step(dve.memset(xrp[s][:, 0:CW - 1], 0.0))
            lo_part(1)
            done = 2
            for job in JOBS:
                kind = job[0]
                done = job_splits(job, done, lo_part)
                if kind == "xr":
                    m = job[1]
                    wait_read(dve, job)
                    s = m % 2
                    if m >= 2:
                        wait_full(dve, ("rgx", m - 2))
                    taps = [params[:, RB * j + m:RB * j + m + 1] for j in range(CW)]
                    step(dve.tensor_scalar(xc[s][:], xrp[s][:, 0:S], taps[0],
                                           params[:, CW * RB + m:CW * RB + m + 1], ALU.mult, ALU.add))
                    for j in range(1, CW):
                        step(dve.scalar_tensor_tensor(out=xc[s][:], in0=xrp[s][:, j:j + S], scalar=taps[j],
                                                      in1=xc[s][:], op0=ALU.mult, op1=ALU.add))
                    step(dve.tensor_copy(xc_hi[s][:], xc[s][:]))
                    dve.tensor_tensor(xc_lo[s][:], xc[s][:], xc_hi[s][:].bitcast(F32), ALU.subtract)\
                        .then_inc(xc_ready, 1)
                elif kind == "rg":
                    m = job[1]
                    s = m % 2
                    dve.wait_ge(ge_sq, m + 1)
                    step(dve.tensor_scalar(ge[:], ge[:], 0.044715, 1.0, ALU.mult, ALU.add))
                    dve.tensor_tensor(ge[:], ge[:], xgs[s][:], ALU.mult).then_inc(ge_in, 1)
                    dve.wait_ge(th_ready, m + 1)
                    step(dve.tensor_scalar(rec[:], th[:], 1.0, None, ALU.add))
                    step(dve.reciprocal(rec[:], rec[:]))
                    step(dve.tensor_scalar(aa[:], th[:], -1.0, 1.0, ALU.mult, ALU.add))
                    step(dve.tensor_tensor(aa[:], aa[:], rec[:], ALU.mult))
                    step(dve.tensor_tensor(inp[:], inp[:], xc[s][:], ALU.mult))
                    dve.wait_ge(root_ready, m + 1)
                    step(dve.scalar_tensor_tensor(out=bb[:], in0=bb[:], scalar=2.0, in1=rec[:],
                                                  op0=ALU.mult, op1=ALU.mult))
                    step(dve.tensor_tensor(bb[:], bb[:], inp[:], ALU.mult))
                    step(dve.tensor_tensor_scan(rec[:], aa[:], bb[:], 0.0, ALU.mult, ALU.add))
                    dve.wait_ge(ge_th, m + 1)
                    step(dve.scalar_tensor_tensor(out=ge[:], in0=ge[:], scalar=1.0, in1=xgs[s][:],
                                                  op0=ALU.add, op1=ALU.mult))
                    step(dve.scalar_tensor_tensor(out=ge[:], in0=rec[:], scalar=0.5, in1=ge[:],
                                                  op0=ALU.mult, op1=ALU.mult))
                    if m == 0:
                        dve.wait_ge(table_zeroed, 16)
                    step(dve.tensor_copy(r_hi[:, m, :], ge[:]))
                    dve.tensor_tensor(r_lo[:, m, :], ge[:], r_hi[:, m, :].bitcast(F32), ALU.subtract)\
                        .then_inc(rg_done, 1)
                elif kind in ("q", "k", "v"):
                    _, g, j = job
                    b = wait_full(dve, job)
                    n = 6 * g + 2 * "qkv".index(kind) + j + 1
                    dve.wait_ge(qkv_hi, n)
                    hi_t, lo_t = {"q": (q_hi, q_lo), "k": (k_hi, k_lo), "v": (v_hi, v_lo)}[kind]
                    if kind == "v":
                        hs, ls = hi_t[:, 2 * j:2 * j + 2, :], lo_t[:, 2 * j:2 * j + 2, :]
                        src = b[:].rearrange("p (a n) -> p a n", a=2)
                    else:
                        hs, ls, src = hi_t[:, j, :], lo_t[:, j, :], b[:]
                    dve.scalar_tensor_tensor(out=ls, in0=src, scalar=SCALE if kind == "q" else 1.0,
                                             in1=hs.bitcast(F32), op0=ALU.mult, op1=ALU.subtract)\
                        .then_inc(free_of(job), 1)
                elif kind == "suf":
                    h = job[1]
                    dve.wait_ge(ln_ready, h + 1)
                    if h >= 1:
                        wait_full(dve, ("pv", h - 1))
                    for i in range(T):
                        a, w = start[i], width[i]
                        b = wait_full(dve, ("z", h, i))
                        ins = dve.scalar_tensor_tensor(out=zs[:, a:a + w], in0=b[:, 0:w], scalar=0.0,
                                                       in1=ze[:, a:a + w], op0=ALU.max, op1=ALU.add)
                    step(ins)
                    dve.tensor_copy(zs_hi[:], zs[:]).then_inc(sp_hi_ready, 1)
                elif kind == "pv":
                    h = job[1]
                    pr, s = h // 2, h % 2
                    for i in range(T):
                        wait_read(dve, ("z", h, i))
                    dve.tensor_copy(zs_hi[:], zs[:]).then_inc(wt_hi_ready, 1)
                    b = wait_full(dve, job)
                    dve.wait_ge(o_hi_ready, h + 1)
                    dve.tensor_tensor(o_lo[HD * s:HD * s + HD, pr, :], b[HD * s:HD * s + HD, :],
                                      o_hi[HD * s:HD * s + HD, pr, :].bitcast(F32), ALU.subtract)\
                        .then_inc(free_of(job), 1)
            for c in range(done, chunk_of["ao", 0] + 3):
                lo_part(c)
            done = chunk_of["ao", 0] + 3
            for m in range(KD):
                dve.wait_ge(sig_ready, 2 * m + 2)
                b = wait_full(dve, ("ya", m))
                dve.tensor_tensor(gate_a[:, m, :], b[:], gate_a[:, m, :], ALU.mult).then_inc(free_of(("ya", m)), 1)
                b = wait_full(dve, ("yr", m))
                dve.tensor_tensor(gate_r[:, m, :], b[:], gate_r[:, m, :], ALU.mult).then_inc(free_of(("yr", m)), 1)
                for key in (("ya", m), ("yr", m)):
                    wait_read(dve, key)
                step(dve.tensor_tensor(gate_a[:, m, :], gate_a[:, m, :], gate_r[:, m, :], ALU.add))
                step(dve.tensor_copy(m_hi[:, m, :], gate_a[:, m, :]))
                dve.tensor_tensor(m_lo[:, m, :], gate_a[:, m, :], m_hi[:, m, :].bitcast(F32), ALU.subtract)\
                    .then_inc(merged_ready, 1)
                if m == 3:
                    for c in range(done, done + 2):
                        lo_part(c)
                    done += 2
            dve.wait_ge(x_again, 16 * T)
            for n in range(2):
                while done < chunk_of["wo", n, 1] + 3:
                    lo_part(done)
                    done += 1
                for i in range(T):
                    b = wait_full(dve, ("x2", n, i))
                    xs = x2[:, i, HALF * n:HALF * n + HALF]
                    dve.tensor_tensor(xs, b[:], xs, ALU.add).then_inc(free_of(("x2", n, i)), 1)
            while done < C_MOE + 3:
                lo_part(done)
                done += 1
            for i in range(T):
                mean_sq(1, i)
            dve.wait_ge(gB_in, 16)
            for i in range(T):
                dve.wait_ge(rstd_done, T + i + 1)
                dve.scalar_tensor_tensor(out=h2[:, i, :], in0=x2[:, i, :], scalar=rstd[:, 1, i:i + 1],
                                         in1=gB[:], op0=ALU.mult, op1=ALU.mult).then_inc(h2_ready, 1)
            dve.wait_ge(route_made, 1)
            step(dve.tensor_scalar(rev[:], iota_i[:], -1.0, float(NE), ALU.mult, ALU.add))
            step(dve.tensor_scalar(e_base[:], iota_i[:], float(S), None, ALU.mult))
            for k in range(1, KD, 2):
                b = wait_full(dve, ("h2T", k))
                dve.tensor_copy(h2T[:, k, :], b[:]).then_inc(free_of(("h2T", k)), 1)

            def first_max(src, n, onehot, top):
                r = rev[:, NE - n:NE].unsqueeze(1).broadcast_to([P, T, n])
                step(dve.tensor_reduce(top, src, AX, ALU.max))
                step(dve.tensor_tensor(eq[:, :, 0:n], src, top.unsqueeze(2).broadcast_to([P, T, n]), ALU.is_equal))
                step(dve.tensor_tensor(cand[:, :, 0:n], eq[:, :, 0:n], r, ALU.mult))
                step(dve.tensor_reduce(best[:], cand[:, :, 0:n], AX, ALU.max))
                step(dve.tensor_tensor(onehot, cand[:, :, 0:n], best[:].unsqueeze(2).broadcast_to([P, T, n]),
                                       ALU.is_equal))

            b = wait_full(dve, "logits")
            dve.tensor_copy(lg[:], b[:, 0:T * NL].rearrange("p (i n) -> p i n", n=NL))\
                .then_inc(free_of("logits"), 1)
            wait_read(dve, "logits")
            first_max(lg[:, :, 0:NG], NG, in_group[:], mx[:])
            dve.tensor_tensor(dg[:], lg[:, :, 0:NG], mx[:].unsqueeze(2).broadcast_to([P, T, NG]),
                              ALU.subtract).then_inc(gexp_in, 1)
            step(dve.tensor_scalar(pen[:], in_group[:], BIG, BIG, ALU.mult, ALU.subtract))
            EG = NE // NG
            for i in range(T):
                el_i = el[:, i, :].rearrange("p (g e) -> p g e", e=EG)
                dve_in = lg[:, i, NG:NL].rearrange("p (g e) -> p g e", e=EG)
                step(dve.tensor_tensor(el_i, dve_in, in_group[:, i, :].unsqueeze(2).broadcast_to([P, NG, EG]), ALU.mult))
                step(dve.tensor_tensor(el_i, el_i, pen[:, i, :].unsqueeze(2).broadcast_to([P, NG, EG]), ALU.add))
            first_max(el[:], NE, M[:, 0], v12[:, 0, :])
            step(dve.scalar_tensor_tensor(out=el[:], in0=M[:, 0], scalar=-2 * BIG, in1=el[:],
                                          op0=ALU.mult, op1=ALU.add))
            first_max(el[:], NE, M[:, 1], v12[:, 1, :])
            dve.tensor_tensor(dv[:], v12[:, 1, :], v12[:, 0, :], ALU.subtract).then_inc(vexp_in, 1)
            dve.tensor_tensor(both[:], M[:, 0], M[:, 1], ALU.add).then_inc(both_ready, 1)
            dve.wait_ge(gexp_ready, 1)
            step(dve.tensor_reduce(gsum[:], dg[:], AX, ALU.add))
            step(dve.reciprocal(ggate[:], gsum[:]))
            dve.wait_ge(vexp_ready, 1)
            step(dve.tensor_scalar(gsum[:], dv[:], 1.0, None, ALU.add))
            step(dve.reciprocal(gsum[:], gsum[:]))
            step(dve.tensor_tensor(combine_w[:, 0, :], gsum[:], ggate[:], ALU.mult))
            step(dve.tensor_tensor(combine_w[:, 1, :], combine_w[:, 0, :], dv[:], ALU.mult))
            b = wait_full(dve, "pos")
            dve.tensor_copy(pos[:], b[:, 0:(T + 1) * NE].rearrange("p (i n) -> p i n", n=NE))\
                .then_inc(free_of("pos"), 1)
            wait_read(dve, "pos")
            for k in range(2):
                step(dve.tensor_tensor(eq[:], M[:, k], pos[:, 0:T, :], ALU.mult))
                step(dve.tensor_reduce(place[:, k, :], eq[:], AX, ALU.add))
                step(dve.tensor_tensor(cand[:], M[:, k], e_base[:].unsqueeze(1).broadcast_to([P, T, NE]), ALU.mult))
                step(dve.tensor_reduce(slot[:, k, :], cand[:], AX, ALU.add))
            step(dve.tensor_scalar(over[:], place[:], float(P), None, ALU.is_ge))
            for n in (2, 3):
                step(dve.tensor_scalar(ov2[:], place[:], float(n * P), None, ALU.is_ge))
                step(dve.tensor_tensor(over[:], over[:], ov2[:], ALU.add))
            step(dve.scalar_tensor_tensor(out=ov2[:], in0=slot[:], scalar=1.0 / P, in1=over[:],
                                          op0=ALU.mult, op1=ALU.add))
            step(dve.scalar_tensor_tensor(out=ov2[:], in0=place[:], scalar=float(4 * NE), in1=ov2[:],
                                          op0=ALU.mult, op1=ALU.add))
            step(dve.scalar_tensor_tensor(out=ov2[:], in0=over[:], scalar=-float(P * 4 * NE), in1=ov2[:],
                                          op0=ALU.mult, op1=ALU.add))
            dve.tensor_copy(addr_i[:], ov2[:]).then_inc(slots_ready, 1)
            dve.wait_ge(slots_ready, 1)
            step(dve.tensor_scalar(ov2[:], place[:], float(P - 1), None, ALU.min))
            step(dve.scalar_tensor_tensor(out=ov2[:], in0=slot[:], scalar=float(P) / S, in1=ov2[:],
                                          op0=ALU.mult, op1=ALU.add))
            step(dve.tensor_copy(slot_i[:], ov2[:]))
            step(dve.tensor_scalar(ov2[:], place[:], -float(P), 0.0, ALU.add, ALU.max))
            step(dve.scalar_tensor_tensor(out=ov2[:], in0=slot[:], scalar=float(OVER * P) / S, in1=ov2[:],
                                          op0=ALU.mult, op1=ALU.add))
            step(dve.tensor_copy(over_slot_i[:], ov2[:]))
            step(dve.tensor_scalar(ov2[:], place[:], float(P), None, ALU.is_ge))
            step(dve.tensor_tensor(over_w[:], ov2[:], combine_w[:], ALU.mult))
            step(dve.tensor_tensor(combine_w[:], combine_w[:], over_w[:], ALU.subtract))
            step(dve.tensor_reduce(mx[:, 0:1], pos[:, T, :], AX, ALU.max))
            dve.tensor_copy(most_i[:], mx[:, 0:1]).then_inc(rows_ready, 1)

            def evict_XT(key, par, it, n):
                for a, bk in enumerate(("XT", "XT2")):
                    b = wait_full(dve, (bk, key), it=it)
                    dve.wait_ge(XT_hi_ready, n + a + 1)
                    dve.tensor_tensor(XT_lo[par][:, 4 * a:4 * a + 4, :], b[:].rearrange("p (k t) -> p k t", t=P),
                                      XT_hi[par][:, 4 * a:4 * a + 4, :].bitcast(F32), ALU.subtract)\
                        .then_inc(free_of((bk, key)), 1)

            evict_XT("first", 0, 0, 0)
            lo_part(C_MOE + 3)

            def dve_step(par, it, last=False):
                if not last:
                    evict_XT(par, 1 - par, it, it * 4 + 2 * par + 2)
                c = step_base(par)
                lo_part(c + 2, it)
                lo_part(c + 3, it)
                gkey = ("G", "first") if par == 0 else ("G", 0)
                wait_read(dve, gkey, it=it)
                b = wait_full(dve, ("U", par), it=it)
                dve.tensor_tensor(he[:], b[:], sil[:], ALU.mult).then_inc(free_of(("U", par)), 1)
                if not last:
                    lo_part(c + 4, it)
                    lo_part(c + 5, it)
                    c += 2
                b = wait_full(dve, ("heT", par), it=it)
                dve.wait_ge(heT_hi_ready, it * 2 + par + 1)
                dve.tensor_tensor(heT_lo[:], b[:].rearrange("p (k t) -> p k t", t=P), heT_hi[:].bitcast(F32),
                                  ALU.subtract).then_inc(free_of(("heT", par)), 1)
                lo_part(c + 4, it)
                lo_part(c + 5, it)
                b = wait_full(dve, ("Y", "last" if last else par, 1), it=it)
                if not isinstance(it, int) or it > 0:
                    dve.wait_ge(Y_out[par], it * 16)
                dve.tensor_copy(Y[par][:, HALF:], b[:]).then_inc(free_of(("Y", par, 1)), 1)

            dve_step(0, 0)
            dve_step(1, 0)
            with dve.Fori(1, NE // 2 - 1) as it:
                dve_step(0, it)
                dve_step(1, it)
            dve_step(0, NE // 2 - 1)
            dve_step(1, NE // 2 - 1, last=True)
            lo_part(C_TAIL + 2)

            def over_dve(e, j, n):
                dve.wait_ge(over_XT_hi, n * 2 + 2)
                for a in range(2):
                    dve.tensor_tensor(XT_lo[0][:, 4 * a:4 * a + 4, :],
                                      bank[4 + a][:].rearrange("p (k t) -> p k t", t=P),
                                      XT_hi[0][:, 4 * a:4 * a + 4, :].bitcast(F32), ALU.subtract)\
                        .then_inc(over_XT_ready, 1)
                dve.wait_ge(over_sil, n + 1)
                dve.wait_ge(over_used, n * PER_E + 4)
                dve.tensor_tensor(he[:], bank[1][:], sil[:], ALU.mult).then_inc(over_he, 1)
                dve.wait_ge(over_heT_hi, n + 1)
                dve.tensor_tensor(heT_lo[:], bank[3][:].rearrange("p (k t) -> p k t", t=P),
                                  heT_hi[:].bitcast(F32), ALU.subtract).then_inc(over_heT_ready, 1)

            with dve.If(any_over(dve)):
                further_tiles(dve, over_dve)
                dve.wait_ge(over_rows_in, 16 * 2 * T)
                for i in range(T):
                    for k in range(2):
                        dve.scalar_tensor_tensor(out=x2[:, i, :], in0=yg[i][k][:], scalar=over_w[:, k, i:i + 1],
                                                 in1=x2[:, i, :], op0=ALU.mult, op1=ALU.add)\
                            .then_inc(over_added, 1)
                        dve.wait_ge(over_added, 2 * i + k + 1)
            for k in range(KP):
                b = wait_full(dve, ("pT", k))
                dve.wait_ge(pT_hi_ready, k + 1)
                dve.tensor_tensor(pT_lo[:, k, :], b[:], pT_hi[:, k, :].bitcast(F32), ALU.subtract)\
                    .then_inc(free_of(("pT", k)), 1)

            for i in range(T):
                dve.wait_ge(yg_in[i], 32)
                step(dve.scalar_tensor_tensor(out=x2[:, i, :], in0=yg[i][0][:], scalar=combine_w[:, 0, i:i + 1],
                                              in1=x2[:, i, :], op0=ALU.mult, op1=ALU.add))
                dve.scalar_tensor_tensor(out=x2[:, i, :], in0=yg[i][1][:], scalar=combine_w[:, 1, i:i + 1],
                                         in1=x2[:, i, :], op0=ALU.mult, op1=ALU.add).then_inc(x3_ready, 1)
                mean_sq(2, i)
            for i in range(T):
                dve.wait_ge(rstd_done, 2 * T + i + 1)
                dve.wait_ge(x3_ready, i + 1)
                dve.tensor_scalar(xn3[:, i, :], x2[:, i, :], rstd[:, 2, i:i + 1], None, ALU.mult)\
                    .then_inc(xn3_ready, 1)
            for k in range(KD):
                b = wait_full(dve, ("h3T", k))
                dve.wait_ge(h3_hi_ready, k + 1)
                dve.scalar_tensor_tensor(out=h3_lo[:, k, :], in0=b[:], scalar=g_ple[:, k:k + 1],
                                         in1=h3_hi[:, k, :].bitcast(F32), op0=ALU.mult, op1=ALU.subtract)\
                    .then_inc(free_of(("h3T", k)), 1)
            for c in range(C_TAIL + 3, C_END):
                lo_part(c)
            for n in range(2):
                for i in range(T):
                    j = T * n + i
                    dve.wait_ge(sg_ready, j + 1)
                    wait_read(dve, ("pp", i, n))
                    cols = slice(HALF * n, HALF * n + HALF)
                    step(dve.tensor_tensor(sg[j % 2][:], sg[j % 2][:], pp[:, i, cols], ALU.mult))
                    dve.tensor_tensor(x2[:, i, cols], x2[:, i, cols], sg[j % 2][:], ALU.add).then_inc(x4_ready, 1)
            for i in range(T):
                mean_sq(3, i)
            dve.wait_ge(gB_in, 32)
            for i in range(T):
                dve.wait_ge(rstd_done, 3 * T + i + 1)
                dve.scalar_tensor_tensor(out=xn3[:, i, :], in0=x2[:, i, :], scalar=rstd[:, 3, i:i + 1],
                                         in1=gB[:], op0=ALU.mult, op1=ALU.mult).then_inc(out_ready, 1)

        @block.tensor
        def _(pe):
            def mm3(dst, lhs, rhs, first, last, skip=False):
                pe.matmul(dst, lhs[0], rhs[0], start=first, stop=False, skip_group_check=skip)
                pe.matmul(dst, lhs[0], rhs[1], start=False, stop=False, skip_group_check=skip)
                return pe.matmul(dst, lhs[1], rhs[0], start=False, stop=last, skip_group_check=skip)

            def chunk(c, k, it=0):
                s = c % SPLIT_SLOTS
                n = c + 1 + PER_IT * it
                pe.wait_ge(hi_ready, n)
                pe.wait_ge(lo_dve, n)
                pe.wait_ge(lo_pool, n)
                return [t[s][:].rearrange("p (k n) -> p k n", k=k) for t in (whi, wlo)]

            def used(ins):
                ins.then_inc(w_used, 1)

            pe.wait_ge(consts_made, 1)
            pe.wait_ge(params_in, 16 * 7)
            n = (CW + 4) * RB
            pe.transpose(bank[2][:, 0:n], par_rows[:], ident[0:n, 0:n]).then_inc(full_of("params"), 1)
            for i in range(T):
                pe.wait_ge(xn_ready, i + 1)
            for k in range(KD):
                b = wait_free(pe, ("hT", k))
                for i in range(T):
                    ins = pe.transpose(b[:, P * i:P * i + P], x_sb[:, i, k::KD], ident[:])
                ins.then_inc(full_of(("hT", k)), 1)
            hT = (hT_hi, hT_lo)
            for k in range(KD):
                wait_read(pe, ("hT", k))
            pe.wait_ge(consts_cast, 4)
            pe.wait_ge(decay_ready, 1)
            for job in JOBS:
                kind = job[0]
                if kind in ("xr", "xg", "q", "k", "g"):
                    if kind == "g":
                        n = job[1] // 2
                        c, j = (chunk_of["ga", n] if n < 4 else chunk_of["gr", n - 4]), job[1] % 2
                    elif kind in ("q", "k"):
                        c, j = chunk_of[kind, job[1]], job[2]
                    else:
                        c, j = chunk_of[kind, job[1] // 2], job[1] % 2
                    w = chunk(c, KD)
                    b = wait_free(pe, job)
                    for k in range(KD):
                        ins = mm3(b[:], [t[:, k, P * j:P * j + P] for t in w], [t[:, k, :] for t in hT],
                                  k == 0, k == KD - 1)
                    ins.then_inc(full_of(job), 1)
                elif kind == "v":
                    _, g, j = job
                    w = chunk(chunk_of["v", g], KD)
                    b = wait_free(pe, job)
                    for a in range(2):
                        i = 2 * j + a
                        for k in range(KD):
                            ins = mm3(b[:, 256 * a:256 * a + 256], [t[:, k, P * i:P * i + P] for t in hT],
                                      [t[:, k, :] for t in w], k == 0, k == KD - 1)
                    ins.then_inc(full_of(job), 1)
                elif kind == "rg":
                    m = job[1]
                    pe.wait_ge(xc_ready, m + 1)
                    for s, key in enumerate(("rga", "rgx")):
                        b = wait_free(pe, (key, m))
                        if m == 0 and s == 0:
                            pe.wait_ge(rg_w_ready, 4)
                        ins = mm3(b[:], [t[s][:, m, :] for t in (wg_hi, wg_lo)],
                                  [t[m % 2][:] for t in (xc_hi, xc_lo)], True, True)
                        ins.then_inc(full_of((key, m)), 1)
                elif kind == "z":
                    h = job[1]
                    g = h // 4
                    lp, s = (h % 4) // 2, h % 2
                    for key in ("q", "k", "v"):
                        for j in range(2):
                            wait_read(pe, (key, g, j))
                    rows = slice(HD * s, HD * s + HD)
                    for i in range(T):
                        b = wait_free(pe, ("z", h, i))
                        kk = [t[rows, lp, P * i:P * i + P] for t in (k_hi, k_lo)]
                        qq = [t[rows, lp, P * i:] for t in (q_hi, q_lo)]
                        zt = b[:, 0:width[i]]
                        pe.matmul(zt, kk[0], qq[0], start=True, stop=False, skip_group_check=True)
                        pe.matmul(b[:, 0:P], ident_r[:], hidden[:], start=False, stop=False, skip_group_check=True)
                        pe.matmul(zt, kk[0], qq[1], start=False, stop=False, skip_group_check=True)
                        pe.matmul(zt, kk[1], qq[0], start=False, stop=True, skip_group_check=True)\
                            .then_inc(full_of(("z", h, i)), 1)
                elif kind == "suf":
                    h = job[1]
                    pe.wait_ge(sp_hi_ready, h + 1)
                    pe.wait_ge(sp_lo_ready, h + 1)
                    for i in range(T):
                        b = bank[banks.at[("z", h, i)][0]]
                        for j in range(T - 1, i - 1, -1):
                            for part in (zs_hi, zs_lo):
                                ins = pe.matmul(b[:, P * (j - i):width[i]], (neg_from if j == i else neg_all)[:],
                                                part[:, start[j]:start[j] + width[j]], start=False,
                                                stop=(j == i and part is zs_lo), skip_group_check=True)
                        ins.then_inc(full_of(("z", h, i)), 1)
                elif kind == "pv":
                    h = job[1]
                    lp = (h % 4) // 2
                    pe.wait_ge(wt_hi_ready, h + 1)
                    pe.wait_ge(wt_lo_ready, h + 1)
                    b = wait_free(pe, job)
                    for i in range(T):
                        ins = mm3(b[:, P * i:], [t[:, i, P * lp:P * lp + P] for t in (v_hi, v_lo)],
                                  [t[:, start[i]:start[i] + width[i]] for t in (zs_hi, zs_lo)], i == 0, i == T - 1)
                    ins.then_inc(full_of(job), 1)
            wait_read(pe, ("pv", H - 2))
            wait_read(pe, ("pv", H - 1))
            pe.wait_ge(rg_done, RB)
            for n in range(2):
                wa = chunk(chunk_of["ao", n], 4)
                wr = chunk(chunk_of["ro", n], 4)
                for j in range(4):
                    m = 4 * n + j
                    for key, w, src in (("ya", wa, (o_hi, o_lo)), ("yr", wr, (r_hi, r_lo))):
                        b = wait_free(pe, (key, m))
                        for k in range(4):
                            ins = mm3(b[:], [t[:, k, P * j:P * j + P] for t in w], [t[:, k, :] for t in src],
                                      k == 0, k == 3)
                        ins.then_inc(full_of((key, m)), 1)
            pe.wait_ge(merged_ready, KD)
            for n in range(2):
                for kh in range(2):
                    w = chunk(chunk_of["wo", n, kh], 4)
                    for i in range(T):
                        key = ("x2", n, i)
                        b = wait_free(pe, key) if kh == 0 else bank[banks.at[key][0]]
                        for k in range(4):
                            ins = mm3(b[:], [t[:, 4 * kh + k, P * i:P * i + P] for t in (m_hi, m_lo)],
                                      [t[:, k, :] for t in w], kh == 0 and k == 0, kh == 1 and k == 3)
                        if kh == 1:
                            ins.then_inc(full_of(key), 1)
                        elif i == T - 1:
                            ins.then_inc(w_used, 1)
            for i in range(T):
                pe.wait_ge(h2_ready, i + 1)
            for k in range(KD):
                key = ("h2T", k)
                b = wait_free(pe, key)
                for i in range(T):
                    ins = pe.transpose(b[:, P * i:P * i + P], h2[:, i, k::KD], ident[:])
                ins.then_inc(full_of(key), 1)
            for k in range(KD):
                wait_read(pe, ("h2T", k))
            pe.wait_ge(small_in, 64)
            b = wait_free(pe, "logits")
            for i in range(T):
                cols = b[:, NL * i:NL * i + NL]
                for k in range(KD):
                    pe.matmul(cols, h2T[:, k, P * i:P * i + P], w_route[:, k, :], start=(k == 0), stop=False)
                ins = pe.matmul(cols, ones[0:1, :], b_route[:], start=False, stop=True)
            ins.then_inc(full_of("logits"), 1)
            pe.wait_ge(both_ready, 1)
            b = wait_free(pe, "pos")
            for i in range(T + 1):
                cols = b[:, NE * i:NE * i + NE]
                for j in range(min(i + 1, T)):
                    lhs = before if j == i else ones
                    ins = pe.matmul(cols, lhs[:], both[:, j, :], start=(j == 0), stop=(j == min(i, T - 1)))
            ins.then_inc(full_of("pos"), 1)

            def transpose_X(key, par, it, n):
                pe.wait_ge(X_in[par], n)
                for a, bk in enumerate(("XT", "XT2")):
                    b = wait_free(pe, (bk, key), it=it)
                    for k in range(4):
                        ins = pe.transpose(b[:, P * k:P * k + P], X[par][:, 4 * a + k::KD], ident[:])
                    ins.then_inc(full_of((bk, key)), 1)

            def up_or_gate(key, c, it, par):
                b = wait_free(pe, key, it=it)
                for half in range(2):
                    w = chunk(c + half, 4, it)
                    for k in range(4):
                        kk = 4 * half + k
                        ins = mm3(b[:], [t[par][:, kk, :] for t in (XT_hi, XT_lo)], [t[:, k, :] for t in w],
                                  kk == 0, kk == KD - 1)
                    ins.then_inc(w_used, 1)

            def XT_done(key, it):
                for bk in ("XT", "XT2"):
                    wait_read(pe, (bk, key), it=it)

            transpose_X("first", 0, 0, 16)
            XT_done("first", 0)
            up_or_gate(("G", "first"), C_MOE, 0, 0)

            def pe_step(par, it, last=False):
                c = step_base(par)
                if not last:
                    transpose_X(par, 1 - par, it, it * 16 + 16 + 16 * par)
                up_or_gate(("U", par), c, it, par)
                if not last:
                    XT_done(par, it)
                    up_or_gate(("G", par), c + 2, it, 1 - par)
                    c += 2
                wait_read(pe, ("U", par), it=it)
                b = wait_free(pe, ("heT", par), it=it)
                for k in range(KF):
                    ins = pe.transpose(b[:, P * k:P * k + P], he[:, k::KF], ident[:])
                ins.then_inc(full_of(("heT", par)), 1)
                wait_read(pe, ("heT", par), it=it)
                ys = [wait_free(pe, ("Y", par, n), it=it) for n in range(2)]
                for half in range(2):
                    w = chunk(c + 2 + half, 2, it)
                    for k in range(2):
                        kk = 2 * half + k
                        for n in range(2):
                            ins = mm3(ys[n][:], [t[:, kk, :] for t in (heT_hi, heT_lo)],
                                      [t[:, k, HALF * n:HALF * n + HALF] for t in w], kk == 0, kk == KF - 1)
                            if kk == KF - 1:
                                ins.then_inc(full_of(("Y", par, n)), 1)
                    if half == 0:
                        ins.then_inc(w_used, 1)

            with pe.Fori(0, NE // 2 - 1) as it:
                pe_step(0, it)
                pe_step(1, it)
            pe_step(0, NE // 2 - 1)
            pe_step(1, NE // 2 - 1, last=True)

            def over_pe(e, j, n):
                def use(c, k, products):
                    pe.wait_ge(over_lo_ready, n * PER_E + c + 1)
                    products([t[:].rearrange("p (k n) -> p k n", k=k) for t in (over_hi, over_lo)])\
                        .then_inc(over_used, 1)

                def in_features(b, half):
                    def products(w):
                        for k in range(4):
                            kk = 4 * half + k
                            ins = mm3(b[:], [t[0][:, kk, :] for t in (XT_hi, XT_lo)], [t[:, k, :] for t in w],
                                      kk == 0, kk == KD - 1)
                        return ins
                    return products

                def down(half):
                    def products(w):
                        for h in range(2):
                            for k in range(2):
                                kk = 2 * half + k
                                ins = mm3(bank[6 + h][:], [t[:, kk, :] for t in (heT_hi, heT_lo)],
                                          [t[:, k, HALF * h:HALF * h + HALF] for t in w], kk == 0, kk == KF - 1)
                        return ins
                    return products

                pe.wait_ge(over_X_in, n * 16 + 16)
                for k in range(KD):
                    ins = pe.transpose(bank[4 + k // 4][:, P * (k % 4):P * (k % 4) + P], X[0][:, k::KD], ident[:])
                ins.then_inc(over_XT, 1)
                pe.wait_ge(over_XT_ready, n * 2 + 2)
                for half in range(2):
                    use(half, 4, in_features(bank[0], half))
                for half in range(2):
                    use(2 + half, 4, in_features(bank[1], half))
                pe.wait_ge(over_he, n + 1)
                for k in range(KF):
                    ins = pe.transpose(bank[3][:, P * k:P * k + P], he[:, k::KF], ident[:])
                ins.then_inc(over_heT, 1)
                pe.wait_ge(over_heT_ready, n + 1)
                for half in range(2):
                    use(4 + half, 2, down(half))
                pe.wait_ge(over_Y_ready, n * 2 + 2)

            with pe.If(any_over(pe)):
                for b in range(8):
                    pe.wait_ge(free[b], free_after_experts[b])
                further_tiles(pe, over_pe)

            pe.wait_ge(p_in, 16)
            for k in range(KP):
                b = wait_free(pe, ("pT", k))
                for i in range(T):
                    ins = pe.transpose(b[:, P * i:P * i + P], p_sb[:, i, k::KP], ident[:])
                ins.then_inc(full_of(("pT", k)), 1)
            for k in range(KP):
                wait_read(pe, ("pT", k))
            w = chunk(C_TAIL, KP)
            for i in range(T):
                for n in range(2):
                    b = wait_free(pe, ("pp", i, n))
                    for k in range(KP):
                        ins = mm3(b[:], [t[:, k, P * i:P * i + P] for t in (pT_hi, pT_lo)],
                                  [t[:, k, HALF * n:HALF * n + HALF] for t in w], k == 0, k == KP - 1)
                    ins.then_inc(full_of(("pp", i, n)), 1)
            for i in range(T):
                pe.wait_ge(xn3_ready, i + 1)
            for k in range(KD):
                b = wait_free(pe, ("h3T", k))
                for i in range(T):
                    ins = pe.transpose(b[:, P * i:P * i + P], xn3[:, i, k::KD], ident[:])
                ins.then_inc(full_of(("h3T", k)), 1)
            for k in range(KD):
                wait_read(pe, ("h3T", k))
            for n in range(2):
                for kh in range(2):
                    w = chunk(C_TAIL + 1 + 2 * n + kh, 4)
                    for i in range(T):
                        key = ("pg", n, i)
                        b = bank[banks.at[key][0]]
                        for k in range(4):
                            ins = mm3(b[:], [t[:, 4 * kh + k, P * i:P * i + P] for t in (h3_hi, h3_lo)],
                                      [t[:, k, :] for t in w], kh == 0 and k == 0, kh == 1 and k == 3)
                        if kh == 1:
                            ins.then_inc(full_of(key), 1)
                        elif i == T - 1:
                            ins.then_inc(w_used, 1)


_INS = ["x", "p", "norm_mix", "w_in", "conv_w", "conv_b", "w_rg_a", "b_rg_a", "w_rg_x", "b_rg_x", "rg_lambda",
        "w_attn_o", "w_rnn_o", "w_out", "norm_moe", "w_router_group", "b_router_group", "w_router_expert",
        "b_router_expert", "w_exp_gate", "w_exp_up", "w_exp_down", "norm_ple", "w_ple_gate", "w_ple_proj",
        "norm_final"]
_OUTS = [((1, 512, 1024), "float32")]


def kernel(**inputs):
    import numpy as _np
    import concourse.bacc as _bacc
    from concourse import mybir as _mybir
    from concourse.bass_utils import run_bass_kernel_spmd as _run

    nc = _bacc.Bacc("TRN2", target_bir_lowering=False, num_devices=1)
    arrays, args = {}, []
    for name in _INS:
        a = _np.ascontiguousarray(inputs[name])
        arrays[f"in_{name}_dram"] = a
        args.append(nc.dram_tensor(f"in_{name}_dram", a.shape, _mybir.dt.from_np(a.dtype), kind="ExternalInput").ap())
    for i, (shape, dtype) in enumerate(_OUTS):
        dt = _mybir.dt.from_np(_np.dtype(dtype))
        args.append(nc.dram_tensor(f"out_{i}_dram", shape, dt, kind="ExternalOutput").ap())
    trunk(nc, *args)
    r = _run(nc, [arrays], core_ids=[0])
    return r.results[0]["out_0_dram"]
```

```python
from contextlib import ExitStack

import concourse.bass as bass
from concourse import mybir

ALU = mybir.AluOpType
ACT = mybir.ActivationFunctionType
F32 = mybir.dt.float32
F32R = mybir.dt.float32r
I32 = mybir.dt.int32
U32 = mybir.dt.uint32
AX = mybir.AxisListType.X

P = 128
KB = 1024
BIG = 1e30
EPS = 1e-6
RAW_SLOTS = 4
SPLIT_SLOTS = 3
CH = 2048
DVE_COLS = 1536


class Banks:

    def __init__(self):
        self.full = [0] * 8
        self.free = [0] * 8
        self.at = {}

    def take(self, key, bank, fills=1, ends=None):
        self.at[key] = (bank, self.free[bank], self.full[bank], ends)
        self.full[bank] += fills if ends is None else 0
        self.free[bank] += 1


def trunk(nc, x, p, norm_mix, w_in, conv_w, conv_b, w_rg_a, b_rg_a, w_rg_x, b_rg_x, rg_lambda,
          w_attn_o, w_rnn_o, w_out, norm_moe, w_router_group, b_router_group, w_router_expert,
          b_router_expert, w_exp_gate, w_exp_up, w_exp_down, norm_ple, w_ple_gate, w_ple_proj,
          norm_final, out):
    _, S, D = x.shape
    T = S // P
    KD = D // P
    DA = w_attn_o.shape[1]
    DR = w_rnn_o.shape[1]
    HD = 64
    H = DA // HD
    NG = w_router_group.shape[2]
    NE = w_exp_gate.shape[1]
    NL = NG + NE
    PD = p.shape[3]
    HALF = 512
    RB = DR // P
    GW = w_rg_a.shape[2]
    CW = conv_w.shape[1]
    SCALE = float(HD) ** -0.5
    assert T * P == HALF and KD == 8 and H == 8 and GW * 2 == P and NE % 2 == 0

    gates_d = nc.dram_tensor("gates_scratch", (2 * KD, P, S), F32).ap()
    h2_d = nc.dram_tensor("h2_scratch", (S, D), F32).ap()
    y_d = nc.dram_tensor("expert_out_scratch", (NE * P, D), F32).ap()
    OVER = S // P - 1
    y_over_d = nc.dram_tensor("expert_over_scratch", (NE * OVER * P, D), F32).ap()
    token_of_d = nc.dram_tensor("token_of_scratch", (NE * S, 1), I32).ap()

    first_col = {"q": 0, "k": DA, "v": 2 * DA, "xr": 3 * DA, "xg": 3 * DA + DR,
                 "ga": 3 * DA + 2 * DR, "gr": 3 * DA + 2 * DR + D}
    IN_ORDER = ([("xr", 0), ("xg", 0), ("q", 0), ("k", 0), ("xr", 1), ("xg", 1), ("v", 0)]
                + [("ga", n) for n in range(4)] + [("q", 1), ("k", 1), ("v", 1)]
                + [("gr", n) for n in range(4)])
    chunk_of = {key: c for c, key in enumerate(IN_ORDER)}
    chunks = [w_in[0, :, first_col[key] + 256 * n:first_col[key] + 256 * n + 256]
              .rearrange("(p k) n -> p k n", k=KD) for key, n in IN_ORDER]
    for n in range(2):
        for key, w in (("ao", w_attn_o), ("ro", w_rnn_o)):
            chunk_of[key, n] = len(chunks)
            chunks.append(w[0, :, HALF * n:HALF * n + HALF].rearrange("(k p) n -> p k n", p=P))
    for n in range(2):
        for k in range(2):
            chunk_of["wo", n, k] = len(chunks)
            chunks.append(w_out[0, HALF * k:HALF * k + HALF, HALF * n:HALF * n + HALF]
                          .rearrange("(k p) n -> p k n", p=P))
    C_MOE = len(chunks)
    PER_E = 6
    PER_IT = 2 * PER_E
    assert PER_IT % RAW_SLOTS == 0 and PER_IT % SPLIT_SLOTS == 0
    C_TAIL = C_MOE + PER_E * NE
    proj_tail = w_ple_proj[0].rearrange("(p k) n -> p k n", k=PD // P)
    gate_tail = w_ple_gate[0].rearrange("(p k) n -> p k n", k=KD)
    tail_chunks = [proj_tail] + [gate_tail[:, 4 * k:4 * k + 4, HALF * n:HALF * n + HALF]
                                 for n in range(2) for k in range(2)]
    C_END = C_TAIL + len(tail_chunks)

    def step_base(e):
        return C_MOE + 2 + PER_E * e

    def gate_src(e, half):
        return w_exp_gate[0, e].rearrange("(p k) n -> p k n", k=KD)[:, 4 * half:4 * half + 4, :]

    banks = Banks()
    for k in range(KD):
        banks.take(("hT", k), k)
    banks.take("params", 7)
    ring = 0
    JOBS = []

    def add(job, bank=None, fills=1):
        nonlocal ring
        if bank is None:
            bank, ring = ring % 2, ring + 1
        banks.take(job, bank, fills, ends=chunk_ended_by(job))
        JOBS.append(job)

    def chunk_ended_by(job):
        kind = job[0]
        if kind in ("xr", "xg") and job[1] % 2 == 1:
            return chunk_of[kind, job[1] // 2]
        if kind in ("q", "k", "v") and job[2] == 1:
            return chunk_of[kind, job[1]]
        if kind == "g" and job[1] % 2 == 1:
            n = job[1] // 2
            return chunk_of["ga", n] if n < 4 else chunk_of["gr", n - 4]
        return None

    def add_rg(pair):
        for m in (2 * pair, 2 * pair + 1):
            banks.take(("rga", m), 2 + 2 * (m % 2))
            banks.take(("rgx", m), 3 + 2 * (m % 2))
        JOBS.append(("rg", pair))

    def add_rec(m):
        JOBS.append(("rec", m))

    def add_pair(pair):
        for kind in ("xr", "xg"):
            for m in (2 * pair, 2 * pair + 1):
                add((kind, m))
        add_rg(pair)

    add_pair(0)
    add(("q", 0, 0))
    add(("q", 0, 1))
    add_rec(0)
    add(("k", 0, 0))
    add_rec(1)
    add(("k", 0, 1))
    add_pair(1)
    add(("v", 0, 0))
    add_rec(2)
    add(("v", 0, 1))
    add_rec(3)

    def add_z(h):
        for b in range(3):
            banks.take(("z", h, b), 2 + b)
        JOBS.append(("z", h))

    def add_wT(h):
        for b in range(3):
            banks.take(("wT", h, b), 5 + b)
        JOBS.append(("wT", h))

    fillers = [("g", m) for m in range(2 * KD)]
    for g in range(2):
        if g == 1:
            for b in range(2):
                add(("q", g, b))
            add(("pv", H // 2 - 1))
            for kind in ("k", "v"):
                for b in range(2):
                    add((kind, g, b))
        for h in range(4 * g, 4 * g + 4):
            add_z(h)
            add(fillers.pop(0))
            if h % 4 > 0:
                add(("pv", h - 1))
            add(fillers.pop(0))
            add_wT(h)
    add(("pv", H - 1))
    for m in range(KD):
        last = m % 4 == 3
        banks.take(("ya", m), m % 2, ends=chunk_of["ao", m // 4] if last else None)
        banks.take(("yr", m), 2 + m % 2, ends=chunk_of["ro", m // 4] if last else None)
    for n in range(2):
        for i in range(T):
            banks.take(("x2", n, i), (4 + i) if n == 0 else i,
                       ends=chunk_of["wo", n, 1] if i == T - 1 else None)
    for k in range(KD):
        banks.take(("h2T", k), (4 + k) % 8)
    banks.take("logits", 0)
    banks.take("pos", 1)
    banks.take(("XT", "first"), 4)
    banks.take(("XT2", "first"), 5)
    banks.take(("G", "first"), 0, ends=C_MOE + 1)
    per_free = [1, 1, 2, 2, 2, 2, 2, 2]
    per_full = [0, 0, 0, 2, 2, 2, 2, 0]

    def take_step(par, last=False):
        c = step_base(par)
        if not last:
            banks.take(("XT", par), 4)
            banks.take(("XT2", par), 5)
        banks.take(("U", par), 2, ends=c + 1)
        if not last:
            banks.take(("G", par), (par + 1) % 2, ends=c + 3)
            c += 2
        banks.take(("heT", par), 3)
        banks.take(("Y", par, 0), 6)
        banks.take(("Y", par, 1), 7, ends=c + 3)

    keep = {}
    for e in range(NE):
        take_step(e % 2, last=(e == NE - 1))
        if e == 1:
            keep = dict(banks.at)
    banks.at = {**banks.at, **keep}
    free_after_experts = list(banks.free)
    banks.at[("Y", "last", 1)] = (*banks.at[("Y", 1, 1)][:3], banks.at[("Y", 1, 1)][3] - 2)
    for k in range(PD // P):
        banks.take(("pT", k), k)
    for i in range(T):
        for n in range(2):
            banks.take(("pp", i, n), 2 + (2 * i + n) % 6, ends=C_TAIL if (i, n) == (T - 1, 1) else None)
    for k in range(KD):
        banks.take(("h3T", k), k)
    for n in range(2):
        for i in range(T):
            banks.take(("pg", n, i), 4 * n + i, ends=C_TAIL + 2 + 2 * n if i == T - 1 else None)

    with ExitStack() as ctx:
        def sem(name):
            return ctx.enter_context(nc.semaphore(name))

        SLAB = 207 * KB
        ctx.enter_context(nc.sbuf_tensor("slab", [P, SLAB // 4], F32))
        origin = nc.sbuf_base - SLAB
        BYTES = 4

        def at(name, shape, offset, dt=F32):
            n = BYTES
            for d in shape[1:]:
                n *= d
            assert offset + n <= SLAB, name
            return nc.alloc_sbuf_tensor_at(name, shape, dt, offset=origin + offset)

        RAW0, HI0, LO0 = 0, 32 * KB, 56 * KB
        C0 = 80 * KB
        RA = 86 * KB
        RQ = RA + 32 * KB
        RO = RQ + 24 * KB
        RR = RO + 16 * KB
        RT = RR + 16 * KB

        raw = [at(f"raw{s}", [P, CH], RAW0 + 8 * KB * s) for s in range(RAW_SLOTS)]
        whi = [at(f"whi{s}", [P, CH], HI0 + 8 * KB * s, F32R) for s in range(SPLIT_SLOTS)]
        wlo = [at(f"wlo{s}", [P, CH], LO0 + 8 * KB * s, F32R) for s in range(SPLIT_SLOTS)]

        off = C0

        def small(name, shape, dt=F32):
            nonlocal off
            t = at(name, shape, off, dt)
            n = BYTES
            for d in shape[1:]:
                n *= d
            off += (n + 31) // 32 * 32
            assert off <= RA
            return t

        ident = small("ident", [P, P])
        ident_r = small("ident_r", [P, P], F32R)
        ones = small("ones", [P, P])
        before = small("before", [P, P])
        hidden = small("hidden", [P, P], F32R)
        g_mix = small("g_mix", [P, KD])
        g_ple = small("g_ple", [P, KD])
        params = small("params", [P, CW * RB + 4 * RB])
        lam = small("lam", [P, 6, RB])
        decay = small("decay", [P, RB])
        log_a = small("log_a", [P, RB])
        neghalf_col = small("neghalf_col", [P, 1])
        ss = small("ss", [P, 4, T])
        ms = small("ms", [P, 4, T])
        rstd = small("rstd", [P, 4, T])
        combine_w = small("combine_w", [P, 2, T])
        over_w = small("over_w", [P, 2, T])
        over_slot_i = small("over_slot_i", [P, 2, T], I32)
        slot_i = small("slot_i", [P, 2, T], I32)
        addr_i = small("addr_i", [P, 2, T], I32)
        token_id = small("token_id", [P, T], I32)
        token_of = small("token_of", [P, 4 * NE], I32)
        idx_now = [small(f"idx_now{s}", [P, 1], I32) for s in range(2)]
        most_i = small("most_i", [P, 1], I32)

        hT_hi = at("hT_hi", [P, KD, S], RA, F32R)
        hT_lo = at("hT_lo", [P, KD, S], RA + 16 * KB, F32R)
        x_sb = at("x_sb", [P, T, D], RQ)
        junk = at("junk", [P, D], RQ + 16 * KB)
        par_rows = at("par_rows", [CW * RB + 4 * RB, P], RQ + 20 * KB)
        wg_raw = [at(f"wg_raw{s}", [P, RB, P], RO + 2 * KB * s) for s in range(2)]
        wg_hi = [at(f"wg_hi{s}", [P, RB, P], RO + 4 * KB + 2 * KB * s, F32R) for s in range(2)]
        wg_lo = [at(f"wg_lo{s}", [P, RB, P], RO + 8 * KB + 2 * KB * s, F32R) for s in range(2)]
        q_hi = at("q_hi", [P, 2, S], RQ, F32R)
        q_lo = at("q_lo", [P, 2, S], RQ + 4 * KB, F32R)
        k_hi = at("k_hi", [P, 2, S], RQ + 8 * KB, F32R)
        k_lo = at("k_lo", [P, 2, S], RQ + 12 * KB, F32R)
        v_hi = at("v_hi", [P, T, 256], RQ + 16 * KB, F32R)
        v_lo = at("v_lo", [P, T, 256], RQ + 20 * KB, F32R)
        o_hi = at("o_hi", [P, H // 2, S], RO, F32R)
        o_lo = at("o_lo", [P, H // 2, S], RO + 8 * KB, F32R)
        r_hi = at("r_hi", [P, RB, S], RR, F32R)
        r_lo = at("r_lo", [P, RB, S], RR + 8 * KB, F32R)
        XRW = S + CW - 1
        xrp = [at(f"xrp{s}", [P, XRW], RT + 2080 * s) for s in range(2)]
        t0 = RT + 2080 * 2
        xgs, xc, xc_hi, xc_lo, rr, th, ig = [
            [at(f"{n}{s}", [P, S], t0 + 2 * KB * (2 * j + s), F32R if n in ("xc_hi", "xc_lo") else F32)
             for s in range(2)] for j, n in enumerate(("xgs", "xc", "xc_hi", "xc_lo", "rr", "th", "ig"))]
        ge = [at(f"ge{s}", [P, S], RO + 12 * KB + 2 * KB * s) for s in range(2)]
        seen = [P * (i + 1) for i in range(T)]
        Z_IN = [[(3, 0)], [(2, 0), (0, seen[2])], [(1, 0)]]
        W_IN = [[(0, 0)], [(1, 0), (3, seen[2])], [(2, 0)]]
        FILL = [HALF, HALF, seen[1]]
        W5 = sum(FILL)
        z_at = {i: HALF * b + col for b in range(3) for i, col in Z_IN[b]}
        w_at = {j: HALF * b + col for b in range(3) for j, col in W_IN[b]}
        beta = at("beta", [P, W5], RT)
        rest = at("rest", [P, W5], RT + 5 * KB)
        left = at("left", [P, W5 + T], RT + 10 * KB)
        left_at = {i: z_at[i] + n for n, i in enumerate(sorted(range(T), key=lambda i: z_at[i]))}
        wT_hi = at("wT_hi", [P, W5], RT + 15 * KB + 32, F32R)
        wT_lo = at("wT_lo", [P, W5], RT + 20 * KB + 32, F32R)
        STAGES = 3
        stage = [at(f"stage{s}", [P, S], RT + 25 * KB + 32 + 2 * KB * s) for s in range(STAGES)]
        gate_a = at("gate_a", [P, KD, S], RT)
        gate_r = at("gate_r", [P, KD, S], RT + 16 * KB)
        m_hi = at("m_hi", [P, KD, S], RA, F32R)
        m_lo = at("m_lo", [P, KD, S], RA + 16 * KB, F32R)
        x2 = at("x2", [P, T, D], RQ)
        gB = at("gB", [P, D], RQ + 20 * KB)
        h2 = at("h2", [P, T, D], RR)
        h2T = at("h2T", [P, KD, S], RO)
        off_r = RT

        def route(name, shape, dt=F32):
            nonlocal off_r
            t = at(name, shape, off_r, dt)
            n = BYTES
            for d in shape[1:]:
                n *= d
            off_r += (n + 31) // 32 * 32
            assert off_r <= RT + 5 * KB
            return t

        X = [at(f"X{s}", [P, D], RA + 4 * KB * s) for s in range(2)]
        XT_hi = [at(f"XT_hi{s}", [P, KD, P], RA + 8 * KB + 4 * KB * s, F32R) for s in range(2)]
        XT_lo = [at(f"XT_lo{s}", [P, KD, P], RA + 16 * KB + 4 * KB * s, F32R) for s in range(2)]
        Y = [at(f"Y{s}", [P, D], RA + 24 * KB + 4 * KB * s) for s in range(2)]
        KF = HALF // P
        sil = at("sil", [P, HALF], RT + 25 * KB)
        he = at("he", [P, HALF], RT + 27 * KB)
        heT_hi = at("heT_hi", [P, KF, P], RT + 29 * KB, F32R)
        heT_lo = at("heT_lo", [P, KF, P], RT + 31 * KB, F32R)
        over_raw = at("over_raw", [P, CH], RO)
        over_hi = at("over_hi", [P, CH], RO + 8 * KB, F32R)
        over_lo = at("over_lo", [P, CH], RO + 16 * KB, F32R)
        p_sb = at("p_sb", [P, T, PD], RT + 21 * KB)
        yg = [[at(f"yg{i}{k}", [P, D], RO + 4 * KB * (2 * i + k)) for k in range(2)] for i in range(T)]
        pp = at("pp", [P, T, D], RA)
        KP = PD // P
        pT_hi = at("pT_hi", [P, KP, S], RA + 16 * KB, F32R)
        pT_lo = at("pT_lo", [P, KP, S], RA + 20 * KB, F32R)
        sg = [at(f"sg{s}", [P, HALF], RA + 24 * KB + 2 * KB * s) for s in range(2)]
        junk2 = at("junk2", [P, D], RQ + 16 * KB)
        xn3 = at("xn3", [P, T, D], RT + 1 * KB + 4 * KB)
        h3_hi = at("h3_hi", [P, KD, S], RO, F32R)
        h3_lo = at("h3_lo", [P, KD, S], RR, F32R)

        w_route = route("w_route", [P, KD, NL])
        b_route = route("b_route", [1, NL])
        lg = route("lg", [P, T, NL])
        iota_i = route("iota_i", [P, NE], I32)
        rev = route("rev", [P, NE])
        e_base = route("e_base", [P, NE])
        eq = route("eq", [P, T, NE])
        cand = route("cand", [P, T, NE])
        mx = route("mx", [P, T])
        best = route("best", [P, T])
        in_group = route("in_group", [P, T, NG])
        dg = route("dg", [P, T, NG])
        gsum = route("gsum", [P, T])
        ggate = route("ggate", [P, T])
        el = route("el", [P, T, NE])
        pen = route("pen", [P, T, NG])
        M = route("M", [P, 2, T, NE])
        both = route("both", [P, T, NE])
        v12 = route("v12", [P, 2, T])
        dv = route("dv", [P, T])
        pos = route("pos", [P, T + 1, NE])
        slot = route("slot", [P, 2, T])
        place = route("place", [P, 2, T])
        over = route("over", [P, 2, T])
        ov2 = route("ov2", [P, 2, T])
        zero_i = at("zero_i", [P, 4 * NE], RR, I32)

        bank = [ctx.enter_context(nc.psum_tensor(f"bank{b}", [P, HALF], F32)) for b in range(8)]

        full = [sem(f"bank{b}_full") for b in range(8)]
        free = [sem(f"bank{b}_free") for b in range(8)]
        raw_in = [sem(f"raw{s}_in") for s in range(RAW_SLOTS)]
        hi_ready = sem("hi_ready")
        lo_dve = sem("lo_dve_ready")
        lo_pool = sem("lo_pool_ready")
        w_used = sem("w_used")
        x_in = [sem(f"x_in{i}") for i in range(T)]
        params_in = sem("params_in")
        g_mix_in = sem("g_mix_in")
        g_ple_in = sem("g_ple_in")
        rg_weights_in = sem("rg_weights_in")
        rg_zeroed = sem("rg_zeroed")
        consts_made = sem("consts_made")
        consts_cast = sem("consts_cast")
        ss_done = sem("ss_done")
        ms_done = sem("ms_done")
        rstd_done = sem("rstd_done")
        xn_ready = sem("xn_ready")
        hT_hi_ready = sem("hT_hi_ready")
        hT_ready = sem("hT_ready")
        lam_exp = sem("lam_exp")
        decay_ready = sem("decay_ready")
        rg_w_ready = sem("rg_w_ready")
        xg_ready = sem("xg_ready")
        xc_ready = sem("xc_ready")
        th_ready = sem("th_ready")
        root_ready = sem("root_ready")
        a_ready = sem("a_ready")
        ig_ready = sem("input_gated")
        ge_sq = sem("ge_sq")
        ge_in = sem("ge_in")
        ge_th = sem("ge_th")
        rg_done = sem("rg_done")
        qkv_hi = sem("qkv_hi_ready")
        qkv_ready = sem("qkv_ready")
        stage_out = [sem(f"stage{s}_out") for s in range(STAGES)]
        ones_set = sem("left_ones_set")
        left_ready = sem("left_ready")
        weights_ready = sem("attention_weights_ready")
        wT_hi_ready = sem("wT_hi_ready")
        o_hi_ready = sem("o_hi_ready")
        gates_in = [sem("gates_a_in"), sem("gates_r_in")]
        sig_ready = sem("sig_ready")
        merged_ready = sem("merged_ready")
        x_again = sem("x_again")
        gB_in = sem("gB_in")
        small_in = sem("small_in")
        route_made = sem("route_made")
        h2_ready = sem("h2_ready")
        h2_out = sem("h2_out")
        gexp_in = sem("gexp_in")
        gexp_ready = sem("gexp_ready")
        vexp_in = sem("vexp_in")
        vexp_ready = sem("vexp_ready")
        both_ready = sem("both_ready")
        slots_ready = sem("slots_ready")
        rows_ready = sem("rows_ready")
        table_zeroed = sem("table_zeroed")
        table_out = sem("table_out")
        table_in = sem("table_in")
        X_in = [sem(f"X{s}_in") for s in range(2)]
        XT_hi_ready = sem("XT_hi_ready")
        XT_ready = sem("XT_ready")
        sil_ready = sem("sil_ready")
        heT_hi_ready = sem("heT_hi_ready")
        heT_ready = sem("heT_ready")
        Y_out = [sem(f"Y{s}_out") for s in range(2)]
        p_in = sem("p_in")
        pT_hi_ready = sem("pT_hi_ready")
        pT_ready = sem("pT_ready")
        pp_ready = sem("pp_ready")
        yg_in = [sem(f"yg_in{i}") for i in range(T)]
        x3_ready = sem("x3_ready")
        xn3_ready = sem("xn3_ready")
        h3_hi_ready = sem("h3_hi_ready")
        h3_ready = sem("h3_ready")
        sg_ready = sem("sg_ready")
        x4_ready = sem("x4_ready")
        out_ready = sem("out_ready")
        out_done = sem("out_done")
        act_chain = sem("act_chain")
        dve_chain = sem("dve_chain")
        pool_chain = sem("pool_chain")
        index_ready = sem("index_ready")
        over_raw_in = sem("over_raw_in")
        over_hi_ready = sem("over_hi_ready")
        over_lo_ready = sem("over_lo_ready")
        over_used = sem("over_used")
        over_index = sem("over_index_ready")
        over_X_in = sem("over_X_in")
        over_XT = sem("over_XT_full")
        over_XT_hi = sem("over_XT_hi_ready")
        over_XT_ready = sem("over_XT_ready")
        over_sil = sem("over_sil_ready")
        over_he = sem("over_he_ready")
        over_heT = sem("over_heT_full")
        over_heT_hi = sem("over_heT_hi_ready")
        over_heT_ready = sem("over_heT_ready")
        over_Y_ready = sem("over_Y_ready")
        over_Y_out = sem("over_Y_out")
        over_rows_in = sem("over_rows_in")
        over_added = sem("over_added")

        block = ctx.enter_context(nc.Block())

        def wait_full(eng, key, nth=1, it=0):
            b, _, f, ends = banks.at[key]
            if ends is None:
                eng.wait_ge(full[b], f + nth + it * per_full[b])
            else:
                eng.wait_ge(w_used, ends + 1 + PER_IT * it)
            return bank[b]

        def wait_free(eng, key, it=0):
            b, r, _, _ = banks.at[key]
            if not isinstance(it, int) or r + it * per_free[b] > 0:
                eng.wait_ge(free[b], r + it * per_free[b])
            return bank[b]

        def wait_read(eng, key, it=0):
            b, r, _, _ = banks.at[key]
            eng.wait_ge(free[b], r + 1 + it * per_free[b])

        def full_of(key):
            b, _, _, ends = banks.at[key]
            return full[b] if ends is None else w_used

        def free_of(key):
            return free[banks.at[key][0]]

        def job_splits(job, done, split):
            kind = job[0]
            if kind in ("xr", "xg"):
                c = chunk_of[kind, job[1] // 2]
            elif kind in ("q", "k", "v"):
                c = chunk_of[kind, job[1]]
            elif kind == "g":
                n = job[1] // 2
                c = chunk_of["ga", n] if n < 4 else chunk_of["gr", n - 4]
            else:
                return done
            while done < c + 3:
                split(done)
                done += 1
            return done

        def further_tiles(eng, tile):
            with eng.Fori(0, NE) as e:
                with eng.Fori(0, OVER) as j:
                    tile(e, j + 1, e * OVER + j)

        def any_over(eng):
            eng.wait_ge(rows_ready, 1)
            return eng.value_load(most_i[0:1, 0:1], min_val=0, max_val=S) > P

        def chained(eng, chain):
            count = [0]

            def step(ins):
                ins.then_inc(chain, 1)
                count[0] += 1
                eng.wait_ge(chain, count[0])
            return step

        @block.sync
        def _(sp):
            for i in range(T):
                sp.dma_start(x_sb[:, i, :], x[0, P * i:P * i + P, :]).then_inc(x_in[i], 16)
            sp.dma_start(g_mix[:], norm_mix[0].rearrange("(p k) -> p k", k=KD)).then_inc(g_mix_in, 16)

            def load(c, it, src):
                s = c % RAW_SLOTS
                if c >= RAW_SLOTS:
                    sp.wait_ge(lo_dve, c + 1 - RAW_SLOTS + PER_IT * it)
                    sp.wait_ge(lo_pool, c + 1 - RAW_SLOTS + PER_IT * it)
                dst = raw[s][:].rearrange("p (k n) -> p k n", k=src.shape[1])
                sp.dma_start(dst, src).then_inc(raw_in[s], 16)

            def load_step(par, it, e, last=False):
                c = step_base(par)
                up = w_exp_up[0, e].rearrange("(p k) n -> p k n", k=KD)
                down = w_exp_down[0, e].rearrange("(p k) n -> p k n", k=KF)
                load(c, it, up[:, 0:4, :])
                load(c + 1, it, up[:, 4:8, :])
                if not last:
                    load(c + 2, it, gate_src(e + 1, 0))
                    load(c + 3, it, gate_src(e + 1, 1))
                    c += 2
                load(c + 2, it, down[:, 0:2, :])
                load(c + 3, it, down[:, 2:4, :])

            load(0, 0, chunks[0])
            rows = [(conv_w[0].rearrange("j (m p) -> (j m) p", p=P), CW * RB)] + [
                (t[0].rearrange("(m p) -> m p", p=P), RB) for t in (conv_b, b_rg_a, b_rg_x, rg_lambda)]
            r0 = 0
            for src, n in rows:
                sp.dma_start(par_rows[r0:r0 + n, :], src).then_inc(params_in, 16)
                r0 += n
            load(1, 0, chunks[1])
            sp.wait_ge(rg_zeroed, 2)
            for s, w in enumerate((w_rg_a, w_rg_x)):
                pairs = w[0].rearrange("(m a) i j -> a i m j", a=2)
                for a in range(2):
                    sp.dma_start(wg_raw[s][GW * a:GW * a + GW, :, GW * a:GW * a + GW], pairs[a])\
                        .then_inc(rg_weights_in, 16)
            sp.dma_start(g_ple[:], norm_ple[0].rearrange("(p k) -> p k", k=KD)).then_inc(g_ple_in, 16)
            for c, src in list(enumerate(chunks))[2:]:
                load(c, 0, src)
            for half in range(2):
                load(C_MOE + half, 0, gate_src(0, half))
            def rows_out(par, it):
                wait_read(sp, ("Y", par, 1), it=it)
                sp.dma_start(y_d.rearrange("(e r) d -> e r d", e=NE)[it * 2 + par], Y[par][:])\
                    .then_inc(Y_out[par], 16)

            load_step(0, 0, 0)
            load_step(1, 0, 1)
            with sp.Fori(1, NE // 2 - 1) as it:
                rows_out(0, it - 1)
                load_step(0, it, it * 2)
                rows_out(1, it - 1)
                load_step(1, it, it * 2 + 1)
            rows_out(0, NE // 2 - 2)
            load_step(0, NE // 2 - 1, NE - 2)
            rows_out(1, NE // 2 - 2)
            load_step(1, NE // 2 - 1, NE - 1, last=True)
            rows_out(0, NE // 2 - 1)
            for j, src in enumerate(tail_chunks):
                load(C_TAIL + j, 0, src)
            rows_out(1, NE // 2 - 1)
            for i in range(T):
                sp.wait_ge(out_ready, i + 1)
                sp.dma_start(out[0, P * i:P * i + P, :], xn3[:, i, :]).then_inc(out_done, 16)
            sp.wait_ge(out_done, 16 * T)

        @block.gpsimd
        def _(pool):
            step = chained(pool, pool_chain)

            def lo_part(c, it=0):
                pool.wait_ge(hi_ready, c + 1 + PER_IT * it)
                pool.tensor_tensor(wlo[c % SPLIT_SLOTS][:, DVE_COLS:], raw[c % RAW_SLOTS][:, DVE_COLS:],
                                   whi[c % SPLIT_SLOTS][:, DVE_COLS:].bitcast(F32),
                                   ALU.subtract).then_inc(lo_pool, 1)

            def root_of_ms(norm, i):
                pool.wait_ge(ms_done, T * norm + i + 1)
                pool.tensor_tensor(rstd[:, norm, i:i + 1], ms[:, norm, i:i + 1], neghalf_col[:],
                                   ALU.pow).then_inc(rstd_done, 1)

            step(pool.memset(neghalf_col[:], -0.5))
            pool.memset(wg_raw[0][:], 0.0).then_inc(rg_zeroed, 1)
            pool.memset(wg_raw[1][:], 0.0).then_inc(rg_zeroed, 1)
            step(pool.memset(ones[:], 1.0))
            step(pool.affine_select(out=ident[:], in_=ones[:], compare_op=ALU.is_equal, fill=0.0,
                                    base=0, pattern=[[1, P]], channel_multiplier=-1))
            step(pool.affine_select(out=before[:], in_=ones[:], compare_op=ALU.is_gt, fill=0.0,
                                    base=0, pattern=[[1, P]], channel_multiplier=-1))
            step(pool.iota(token_id[:], pattern=[[P, T]], base=0, channel_multiplier=1))
            pool.memset(zero_i[:], 0).then_inc(consts_made, 1)
            pool.wait_ge(consts_made, 1)
            pool.dma_start(token_of_d.rearrange("(p j) o -> p (j o)", p=P), zero_i[:]).then_inc(table_zeroed, 16)
            for i in range(T):
                root_of_ms(0, i)
            lo_part(0)
            lo_part(1)

            done = 2
            for job in JOBS:
                done = job_splits(job, done, lo_part)
                if job[0] == "rg":
                    for m in (2 * job[1], 2 * job[1] + 1):
                        pool.wait_ge(ge_sq, m + 1)
                        step(pool.tensor_scalar(ge[m % 2][:], ge[m % 2][:], 0.044715, 1.0, ALU.mult, ALU.add))
                        pool.tensor_tensor(ge[m % 2][:], ge[m % 2][:], xgs[m % 2][:], ALU.mult).then_inc(ge_in, 1)
                    for m in (2 * job[1], 2 * job[1] + 1):
                        wait_read(pool, ("rgx", m))
                        pool.wait_ge(xc_ready, m + 1)
                        pool.tensor_tensor(ig[m % 2][:], ig[m % 2][:], xc[m % 2][:], ALU.mult).then_inc(ig_ready, 1)
            for c in range(done, C_MOE + 2):
                lo_part(c)
            pool.wait_ge(merged_ready, KD)
            pool.iota(iota_i[:], pattern=[[1, NE]], base=0, channel_multiplier=0).then_inc(route_made, 1)
            for i in range(T):
                root_of_ms(1, i)
            lo_part(C_MOE + 2)
            pool.wait_ge(slots_ready, 1)
            pool.wait_ge(table_zeroed, 16)
            for k in range(2):
                for i in range(T):
                    pool.indirect_dma_start(token_of_d, bass.IndirectOffsetOnAxis(addr_i[:, k, i:i + 1].bitcast(U32), 0),
                                            token_id[:, i:i + 1], None).then_inc(table_out, 16)
            pool.wait_ge(table_out, 16 * 2 * T)
            pool.dma_start(token_of[:], token_of_d.rearrange("(p j) o -> p (j o)", p=P)).then_inc(table_in, 16)
            pool.wait_ge(table_in, 16)
            pool.wait_ge(h2_out, 16 * T)

            for par in range(2):
                step(pool.tensor_copy(idx_now[par][:], token_of[:, 4 * par:4 * par + 1]))
                pool.indirect_dma_start(X[par][:], None, h2_d,
                                        bass.IndirectOffsetOnAxis(idx_now[par][:].bitcast(U32), 0))\
                    .then_inc(X_in[par], 16)

            def pool_step(par, it, e, last=False, more=True):
                c = step_base(par)
                if more:
                    pool.wait_ge(table_in, 16)
                    wait_full(pool, ("XT2", "first") if par == 0 else ("XT2", 0), it=it)
                    pool.tensor_copy(idx_now[par][:], token_of[:, bass.ds(e * 4 + 8, 1)]).then_inc(index_ready, 1)
                    pool.wait_ge(index_ready, it * 2 + par + 1)
                lo_part(c + 2, it)
                if more:
                    pool.wait_ge(h2_out, 16 * T)
                    pool.indirect_dma_start(X[par][:], None, h2_d,
                                            bass.IndirectOffsetOnAxis(idx_now[par][:].bitcast(U32), 0))\
                        .then_inc(X_in[par], 16)
                for j in range(3, 6 if last else 8):
                    lo_part(c + j, it)

            lo_part(C_MOE + 3)
            with pool.Fori(0, NE // 2 - 1) as it:
                pool_step(0, it, it * 2)
                pool_step(1, it, it * 2 + 1)
            pool_step(0, NE // 2 - 1, NE - 2, more=False)
            pool_step(1, NE // 2 - 1, NE - 1, last=True, more=False)
            lo_part(C_TAIL + 2)

            def over_pool(e, j, n):
                pool.tensor_copy(idx_now[0][:], token_of[:, bass.ds(e * 4 + j, 1)]).then_inc(over_index, 1)
                pool.wait_ge(over_index, n + 1)
                for c in range(PER_E):
                    pool.wait_ge(over_hi_ready, n * PER_E + c + 1)
                    pool.tensor_tensor(over_lo[:], over_raw[:], over_hi[:].bitcast(F32), ALU.subtract)\
                        .then_inc(over_lo_ready, 1)
                    if c == 0:
                        pool.wait_ge(h2_out, 16 * T)
                        pool.indirect_dma_start(X[0][:], None, h2_d,
                                                bass.IndirectOffsetOnAxis(idx_now[0][:].bitcast(U32), 0))\
                            .then_inc(over_X_in, 16)
                    pool.wait_ge(over_used, n * PER_E + c + 1)

            with pool.If(any_over(pool)):
                wait_full(pool, ("XT2", 0), it=NE // 2 - 2)
                further_tiles(pool, over_pool)
                pool.wait_ge(over_Y_out, 16 * NE * OVER)
                for i in range(T):
                    for k in range(2):
                        pool.indirect_dma_start(yg[i][k][:], None, y_over_d,
                                                bass.IndirectOffsetOnAxis(over_slot_i[:, k, i:i + 1].bitcast(U32), 0))\
                            .then_inc(over_rows_in, 16)
                pool.wait_ge(over_added, 2 * T)
            for s in range(2):
                pool.wait_ge(Y_out[s], 16 * (NE // 2))
            for i in range(T):
                for k in range(2):
                    pool.indirect_dma_start(yg[i][k][:], None, y_d,
                                            bass.IndirectOffsetOnAxis(slot_i[:, k, i:i + 1].bitcast(U32), 0))\
                        .then_inc(yg_in[i], 16)
            for i in range(T):
                root_of_ms(2, i)
            for c in range(C_TAIL + 3, C_END):
                lo_part(c)
            for i in range(T):
                root_of_ms(3, i)

        @block.scalar
        def _(act):
            step = chained(act, act_chain)
            copy = ACT.Copy

            def hi_part(c, it=0):
                if c >= SPLIT_SLOTS:
                    act.wait_ge(w_used, c + 1 - SPLIT_SLOTS + PER_IT * it)
                act.wait_ge(raw_in[c % RAW_SLOTS], 16 * (c // RAW_SLOTS + 1 + PER_IT // RAW_SLOTS * it))
                act.activation(whi[c % SPLIT_SLOTS][:], raw[c % RAW_SLOTS][:], copy).then_inc(hi_ready, 1)

            def squares(norm, i, src, scrap):
                if T * norm + i > 0:
                    act.wait_ge(ss_done, T * norm + i)
                act.activation(scrap[:], src, ACT.Square, accum_out=ss[:, norm, i:i + 1]).then_inc(ss_done, 1)

            for i in range(T):
                act.wait_ge(x_in[i], 16)
                squares(0, i, x_sb[:, i, :], junk)
            hi_part(0)
            act.wait_ge(g_mix_in, 16)
            for k in range(KD):
                b = wait_full(act, ("hT", k))
                act.activation(hT_hi[:, k, :], b[:], copy, scale=g_mix[:, k:k + 1]).then_inc(hT_hi_ready, 1)
            hi_part(1)
            act.wait_ge(rg_weights_in, 64)
            for s in range(2):
                act.activation(wg_hi[s][:], wg_raw[s][:], copy).then_inc(rg_w_ready, 1)
            wait_read(act, "params")
            step(act.activation(lam[:, 0, :], params[:, (CW + 3) * RB:(CW + 4) * RB], ACT.Abs))
            act.activation(lam[:, 1, :], lam[:, 0, :], ACT.Exp, scale=-1.0).then_inc(lam_exp, 1)
            done = 2
            gate_n = 0
            for job in JOBS:
                kind = job[0]
                done = job_splits(job, done, hi_part)
                if kind == "xr":
                    m = job[1]
                    b = wait_full(act, job)
                    if m >= 2:
                        act.wait_ge(rg_done, m - 1)
                    act.activation(xrp[m % 2][:, CW - 1:], b[:], copy).then_inc(free_of(job), 1)
                elif kind == "xg":
                    m = job[1]
                    b = wait_full(act, job)
                    if m >= 2:
                        act.wait_ge(rg_done, m - 1)
                    act.activation(xgs[m % 2][:], b[:], copy).then_inc(free_of(job), 1)
                elif kind == "rg":
                    ms_ = (2 * job[1], 2 * job[1] + 1)
                    if job[1] > 0:
                        act.wait_ge(rg_done, ms_[0])
                    else:
                        act.wait_ge(decay_ready, 2)
                    for m in ms_:
                        ba = params[:, (CW + 1) * RB + m:(CW + 1) * RB + m + 1]
                        bx = params[:, (CW + 2) * RB + m:(CW + 2) * RB + m + 1]
                        b = wait_full(act, ("rga", m))
                        act.activation(rr[m % 2][:], b[:], ACT.Sigmoid, bias=ba).then_inc(free_of(("rga", m)), 1)
                        b = wait_full(act, ("rgx", m))
                        act.activation(ig[m % 2][:], b[:], ACT.Sigmoid, bias=bx).then_inc(free_of(("rgx", m)), 1)
                    for m in ms_:
                        wait_read(act, ("xg", m))
                        act.activation(ge[m % 2][:], xgs[m % 2][:], ACT.Square).then_inc(ge_sq, 1)
                    for m in ms_:
                        wait_read(act, ("rga", m))
                        act.activation(th[m % 2][:], rr[m % 2][:], ACT.Tanh, scale=decay[:, m:m + 1])\
                            .then_inc(th_ready, 1)
                    for m in ms_:
                        act.wait_ge(ge_in, m + 1)
                        act.activation(ge[m % 2][:], ge[m % 2][:], ACT.Tanh, scale=0.7978845608028654)\
                            .then_inc(ge_th, 1)
                    for m in ms_:
                        act.wait_ge(th_ready, m + 1)
                        act.activation(rr[m % 2][:], rr[m % 2][:], ACT.Exp, scale=log_a[:, m:m + 1])\
                            .then_inc(a_ready, 1)
                    for m in ms_:
                        act.activation(th[m % 2][:], th[m % 2][:], ACT.Sqrt).then_inc(root_ready, 1)
                elif kind in ("q", "k", "v"):
                    _, g, j = job
                    b = wait_full(act, job)
                    dst = {"q": q_hi, "k": k_hi, "v": v_hi}[kind]
                    d = dst[:, 2 * j:2 * j + 2, :] if kind == "v" else dst[:, j, :]
                    src = b[:].rearrange("p (a n) -> p a n", a=2) if kind == "v" else b[:]
                    if g == 1:
                        if kind == "v":
                            wait_full(act, ("pv", H // 2 - 1))
                        else:
                            wait_full(act, ("wT", H // 2 - 1, 2))
                    act.activation(d, src, copy, scale=SCALE if kind == "q" else 1.0).then_inc(qkv_hi, 1)
                elif kind == "g":
                    s = gate_n % STAGES
                    b = wait_full(act, job)
                    if gate_n >= STAGES:
                        act.wait_ge(stage_out[s], 16 * (gate_n // STAGES))
                    if gate_n == 0:
                        act.wait_ge(rg_done, RB)
                    act.activation(stage[s][:], b[:], copy).then_inc(free_of(job), 1)
                    wait_read(act, job)
                    act.dma_start(gates_d[job[1]], stage[s][:]).then_inc(stage_out[s], 16)
                    gate_n += 1
                elif kind == "z":
                    h = job[1]
                    if h == 0:
                        act.wait_ge(rg_done, RB)
                    else:
                        wait_full(act, ("wT", h - 1, 2))
                    for b in range(3):
                        zb = wait_full(act, ("z", h, b))
                        cols = slice(HALF * b, HALF * b + FILL[b])
                        act.activation(beta[:, cols], zb[:, 0:FILL[b]], ACT.Sigmoid)
                        act.activation(rest[:, cols], zb[:, 0:FILL[b]], ACT.Sigmoid, scale=-1.0)\
                            .then_inc(free_of(("z", h, b)), 1)
                elif kind == "wT":
                    h = job[1]
                    if h > 0:
                        wait_full(act, ("pv", h - 1))
                    for b in range(3):
                        wb = wait_full(act, ("wT", h, b))
                        act.activation(wT_hi[:, HALF * b:HALF * b + FILL[b]], wb[:, 0:FILL[b]], copy)\
                            .then_inc(wT_hi_ready, 1)
                elif kind == "pv":
                    h = job[1]
                    pr, s = h // 2, h % 2
                    b = wait_full(act, job)
                    act.activation(o_hi[HD * s:HD * s + HD, pr, :], b[HD * s:HD * s + HD, :], copy)\
                        .then_inc(o_hi_ready, 1)
            wait_read(act, ("pv", H - 2))
            wait_read(act, ("pv", H - 1))
            for i in range(T):
                act.dma_start(x2[:, i, :], x[0, P * i:P * i + P, :]).then_inc(x_again, 16)
            for s in range(STAGES):
                act.wait_ge(stage_out[s], 16 * len(range(s, 2 * KD, STAGES)))
            for g, t in enumerate((gate_a, gate_r)):
                act.dma_start(t[:], gates_d[KD * g:KD * g + KD].rearrange("m p t -> p m t")).then_inc(gates_in[g], 16)
            act.dma_start(gB[:], norm_moe[0:1, :].broadcast_to([P, D])).then_inc(gB_in, 16)
            for c in range(done, chunk_of["ao", 0] + 3):
                hi_part(c)
            done = chunk_of["ao", 0] + 3
            act.wait_ge(gates_in[0], 16)
            act.wait_ge(gates_in[1], 16)
            for m in range(KD):
                act.activation(gate_a[:, m, :], gate_a[:, m, :], ACT.Sigmoid).then_inc(sig_ready, 1)
                act.activation(gate_r[:, m, :], gate_r[:, m, :], ACT.Sigmoid).then_inc(sig_ready, 1)
            for c in range(done, C_MOE + 3):
                hi_part(c)
            act.wait_ge(merged_ready, KD)
            act.dma_start(w_route[:, :, 0:NG], w_router_group[0].rearrange("(p k) n -> p k n", k=KD)).then_inc(small_in, 16)
            act.dma_start(w_route[:, :, NG:NL], w_router_expert[0].rearrange("(p k) n -> p k n", k=KD)).then_inc(small_in, 16)
            act.dma_start(b_route[:, 0:NG], b_router_group).then_inc(small_in, 16)
            act.dma_start(b_route[:, NG:NL], b_router_expert).then_inc(small_in, 16)
            act.dma_start(p_sb[:], p[0, 0].rearrange("(i p) n -> p i n", p=P)).then_inc(p_in, 16)
            for i in range(T):
                wait_read(act, ("x2", 0, i))
                wait_read(act, ("x2", 1, i))
                squares(1, i, x2[:, i, :], junk2)
            for i in range(T):
                act.wait_ge(h2_ready, i + 1)
                act.dma_start(h2_d[P * i:P * i + P, :], h2[:, i, :]).then_inc(h2_out, 16)
            for k in range(0, KD, 2):
                b = wait_full(act, ("h2T", k))
                act.activation(h2T[:, k, :], b[:], copy).then_inc(free_of(("h2T", k)), 1)
            act.wait_ge(gexp_in, 1)
            act.activation(dg[:], dg[:], ACT.Exp).then_inc(gexp_ready, 1)
            act.wait_ge(vexp_in, 1)
            act.activation(dv[:], dv[:], ACT.Exp).then_inc(vexp_ready, 1)

            def evict_XT(key, par, it, n):
                for a, bk in enumerate(("XT", "XT2")):
                    b = wait_full(act, (bk, key), it=it)
                    act.activation(XT_hi[par][:, 4 * a:4 * a + 4, :], b[:].rearrange("p (k t) -> p k t", t=P),
                                   copy).then_inc(XT_hi_ready, 1)

            evict_XT("first", 0, 0, 0)
            hi_part(C_MOE + 3)

            def act_step(par, it, last=False):
                gkey = ("G", "first") if par == 0 else ("G", 0)
                b = wait_full(act, gkey, it=it)
                wait_free(act, ("U", par), it=it)
                act.activation(sil[:], b[:], ACT.Silu).then_inc(free_of(gkey), 1)
                if not last:
                    evict_XT(par, 1 - par, it, 0)
                c = step_base(par)
                hi_part(c + 2, it)
                hi_part(c + 3, it)
                if not last:
                    hi_part(c + 4, it)
                b = wait_full(act, ("heT", par), it=it)
                act.activation(heT_hi[:], b[:].rearrange("p (k t) -> p k t", t=P), copy).then_inc(heT_hi_ready, 1)
                if not last:
                    hi_part(c + 5, it)
                    c += 2
                hi_part(c + 4, it)
                hi_part(c + 5, it)
                b = wait_full(act, ("Y", par, 0), it=it)
                if not isinstance(it, int) or it > 0:
                    act.wait_ge(Y_out[par], it * 16)
                act.activation(Y[par][:, 0:HALF], b[:], copy).then_inc(free_of(("Y", par, 0)), 1)

            act_step(0, 0)
            act_step(1, 0)
            with act.Fori(1, NE // 2 - 1) as it:
                act_step(0, it)
                act_step(1, it)
            act_step(0, NE // 2 - 1)
            act_step(1, NE // 2 - 1, last=True)
            hi_part(C_TAIL + 2)

            def over_act(e, j, n):
                gate, up = [w[0, e].rearrange("(p k) n -> p k n", k=KD) for w in (w_exp_gate, w_exp_up)]
                down = w_exp_down[0, e].rearrange("(p k) n -> p k n", k=KF)
                parts = [gate[:, 0:4, :], gate[:, 4:8, :], up[:, 0:4, :], up[:, 4:8, :],
                         down[:, 0:2, :], down[:, 2:4, :]]

                def hi(c):
                    act.dma_start(over_raw[:].rearrange("p (k n) -> p k n", k=parts[c].shape[1]), parts[c])\
                        .then_inc(over_raw_in, 16)
                    act.wait_ge(over_raw_in, n * (16 * PER_E) + 16 * (c + 1))
                    act.activation(over_hi[:], over_raw[:], copy).then_inc(over_hi_ready, 1)
                    if c == 0:
                        act.wait_ge(over_XT, n + 1)
                        for a in range(2):
                            act.activation(XT_hi[0][:, 4 * a:4 * a + 4, :],
                                           bank[4 + a][:].rearrange("p (k t) -> p k t", t=P), copy)\
                                .then_inc(over_XT_hi, 1)
                    if c == 3:
                        act.wait_ge(over_used, n * PER_E + 2)
                        act.activation(sil[:], bank[0][:], ACT.Silu).then_inc(over_sil, 1)
                        act.wait_ge(over_heT, n + 1)
                        act.activation(heT_hi[:], bank[3][:].rearrange("p (k t) -> p k t", t=P), copy)\
                            .then_inc(over_heT_hi, 1)
                    act.wait_ge(over_used, n * PER_E + c + 1)
                for c in range(PER_E):
                    hi(c)
                for h in range(2):
                    act.activation(Y[0][:, HALF * h:HALF * h + HALF], bank[6 + h][:], copy).then_inc(over_Y_ready, 1)
                act.wait_ge(over_Y_ready, n * 2 + 2)
                act.dma_start(y_over_d.rearrange("(n r) d -> n r d", r=P)[n], Y[0][:]).then_inc(over_Y_out, 16)
                act.wait_ge(over_Y_out, n * 16 + 16)

            with act.If(any_over(act)):
                act.wait_ge(h2_out, 16 * T)
                act.wait_ge(Y_out[0], 16 * (NE // 2))
                further_tiles(act, over_act)
            for k in range(KP):
                b = wait_full(act, ("pT", k))
                act.activation(pT_hi[:, k, :], b[:], copy).then_inc(pT_hi_ready, 1)
            for i in range(T):
                for n in range(2):
                    b = wait_full(act, ("pp", i, n))
                    act.activation(pp[:, i, HALF * n:HALF * n + HALF], b[:], copy).then_inc(free_of(("pp", i, n)), 1)
            act.dma_start(gB[:], norm_final.rearrange("(o n) -> o n", o=1).broadcast_to([P, D])).then_inc(gB_in, 16)
            for i in range(T):
                act.wait_ge(x3_ready, i + 1)
                squares(2, i, x2[:, i, :], junk2)
            for k in range(KD):
                b = wait_full(act, ("h3T", k))
                if k == 0:
                    act.wait_ge(g_ple_in, 16)
                act.activation(h3_hi[:, k, :], b[:], copy, scale=g_ple[:, k:k + 1]).then_inc(h3_hi_ready, 1)
            for c in range(C_TAIL + 3, C_END):
                hi_part(c)
            for n in range(2):
                for i in range(T):
                    j = T * n + i
                    b = wait_full(act, ("pg", n, i))
                    if j >= 2:
                        act.wait_ge(x4_ready, j - 1)
                    act.activation(sg[j % 2][:], b[:], ACT.Sigmoid).then_inc(sg_ready, 1)
            for i in range(T):
                act.wait_ge(x4_ready, T + i + 1)
                squares(3, i, x2[:, i, :], junk2)

        @block.vector
        def _(dve):
            step = chained(dve, dve_chain)

            def lo_part(c, it=0):
                dve.wait_ge(hi_ready, c + 1 + PER_IT * it)
                dve.tensor_tensor(wlo[c % SPLIT_SLOTS][:, 0:DVE_COLS], raw[c % RAW_SLOTS][:, 0:DVE_COLS],
                                  whi[c % SPLIT_SLOTS][:, 0:DVE_COLS].bitcast(F32),
                                  ALU.subtract).then_inc(lo_dve, 1)

            def mean_sq(norm, i):
                dve.wait_ge(ss_done, T * norm + i + 1)
                dve.tensor_scalar(ms[:, norm, i:i + 1], ss[:, norm, i:i + 1], 1.0 / D, EPS,
                                  ALU.mult, ALU.add).then_inc(ms_done, 1)

            for i in range(T):
                mean_sq(0, i)
                dve.wait_ge(rstd_done, i + 1)
                dve.tensor_scalar(x_sb[:, i, :], x_sb[:, i, :], rstd[:, 0, i:i + 1], None, ALU.mult)\
                    .then_inc(xn_ready, 1)
            dve.wait_ge(consts_made, 1)
            dve.tensor_copy(ident_r[:], ident[:]).then_inc(consts_cast, 1)
            dve.tensor_scalar(hidden[:], before[:], BIG, BIG, ALU.mult, ALU.subtract).then_inc(consts_cast, 1)
            lo_part(0)
            for k in range(KD):
                dve.wait_ge(hT_hi_ready, k + 1)
                b = wait_full(dve, ("hT", k))
                if k == 0:
                    dve.wait_ge(g_mix_in, 16)
                dve.scalar_tensor_tensor(out=hT_lo[:, k, :], in0=b[:], scalar=g_mix[:, k:k + 1],
                                         in1=hT_hi[:, k, :].bitcast(F32), op0=ALU.mult, op1=ALU.subtract)\
                    .then_inc(free_of(("hT", k)), 1)
            lo_part(1)
            b = wait_full(dve, "params")
            dve.tensor_copy(params[:], b[:, 0:(CW + 4) * RB]).then_inc(free_of("params"), 1)
            wait_read(dve, "params")
            lm = params[:, (CW + 3) * RB:(CW + 4) * RB]
            dve.wait_ge(lam_exp, 1)
            step(dve.tensor_scalar(lam[:, 2, :], lam[:, 1, :], 2.0, None, ALU.add))
            step(dve.reciprocal(lam[:, 2, :], lam[:, 2, :]))
            step(dve.tensor_tensor(lam[:, 2, :], lam[:, 1, :], lam[:, 2, :], ALU.mult))
            step(dve.tensor_tensor(lam[:, 3, :], lam[:, 2, :], lam[:, 2, :], ALU.mult))
            step(dve.tensor_scalar(lam[:, 4, :], lam[:, 3, :], 1.0 / 17, 1.0 / 15, ALU.mult, ALU.add))
            for n in (13, 11, 9, 7, 5, 3, 1):
                step(dve.tensor_tensor(lam[:, 4, :], lam[:, 4, :], lam[:, 3, :], ALU.mult))
                step(dve.tensor_scalar(lam[:, 4, :], lam[:, 4, :], 1.0 / n, None, ALU.add))
            step(dve.scalar_tensor_tensor(out=lam[:, 4, :], in0=lam[:, 4, :], scalar=8.0, in1=lam[:, 2, :],
                                          op0=ALU.mult, op1=ALU.mult))
            step(dve.tensor_scalar(lam[:, 5, :], lm, -4.0, 0.0, ALU.mult, ALU.max))
            dve.tensor_tensor(decay[:], lam[:, 4, :], lam[:, 5, :], ALU.add).then_inc(decay_ready, 1)
            dve.wait_ge(decay_ready, 1)
            dve.tensor_scalar(log_a[:], decay[:], -2.0, None, ALU.mult).then_inc(decay_ready, 1)
            dve.wait_ge(rg_w_ready, 2)
            for s in range(2):
                dve.tensor_tensor(wg_lo[s][:], wg_raw[s][:], wg_hi[s][:].bitcast(F32), ALU.subtract)\
                    .then_inc(rg_w_ready, 1)
            for s in range(2):
                step(dve.memset(xrp[s][:, 0:CW - 1], 0.0))
            done = 2
            for job in JOBS:
                kind = job[0]
                done = job_splits(job, done, lo_part)
                if kind == "xr":
                    m = job[1]
                    wait_read(dve, job)
                    s = m % 2
                    if m >= 2:
                        wait_full(dve, ("rgx", m - 2))
                        dve.wait_ge(rg_done, m - 1)
                    taps = [params[:, RB * j + m:RB * j + m + 1] for j in range(CW)]
                    step(dve.tensor_scalar(xc[s][:], xrp[s][:, 0:S], taps[0],
                                           params[:, CW * RB + m:CW * RB + m + 1], ALU.mult, ALU.add))
                    for j in range(1, CW):
                        step(dve.scalar_tensor_tensor(out=xc[s][:], in0=xrp[s][:, j:j + S], scalar=taps[j],
                                                      in1=xc[s][:], op0=ALU.mult, op1=ALU.add))
                    step(dve.tensor_copy(xc_hi[s][:], xc[s][:]))
                    dve.tensor_tensor(xc_lo[s][:], xc[s][:], xc_hi[s][:].bitcast(F32), ALU.subtract)\
                        .then_inc(xc_ready, 1)
                elif kind == "rec":
                    m = job[1]
                    s = m % 2
                    dve.wait_ge(a_ready, m + 1)
                    dve.wait_ge(root_ready, m + 1)
                    step(dve.scalar_tensor_tensor(out=th[s][:], in0=rr[s][:], scalar=1.0, in1=th[s][:],
                                                  op0=ALU.add, op1=ALU.mult))
                    dve.wait_ge(ig_ready, m + 1)
                    step(dve.tensor_tensor(th[s][:], th[s][:], ig[s][:], ALU.mult))
                    step(dve.tensor_tensor_scan(xc[s][:], rr[s][:], th[s][:], 0.0, ALU.mult, ALU.add))
                    dve.wait_ge(ge_th, m + 1)
                    step(dve.scalar_tensor_tensor(out=ge[s][:], in0=ge[s][:], scalar=1.0, in1=xgs[s][:],
                                                  op0=ALU.add, op1=ALU.mult))
                    step(dve.scalar_tensor_tensor(out=ge[s][:], in0=xc[s][:], scalar=0.5, in1=ge[s][:],
                                                  op0=ALU.mult, op1=ALU.mult))
                    if m == 0:
                        dve.wait_ge(table_zeroed, 16)
                    step(dve.tensor_copy(r_hi[:, m, :], ge[s][:]))
                    dve.tensor_tensor(r_lo[:, m, :], ge[s][:], r_hi[:, m, :].bitcast(F32), ALU.subtract)\
                        .then_inc(rg_done, 1)
                elif kind in ("q", "k", "v"):
                    _, g, j = job
                    b = wait_full(dve, job)
                    n = 6 * g + 2 * "qkv".index(kind) + j + 1
                    dve.wait_ge(qkv_hi, n)
                    hi_t, lo_t = {"q": (q_hi, q_lo), "k": (k_hi, k_lo), "v": (v_hi, v_lo)}[kind]
                    if kind == "v":
                        hs, ls = hi_t[:, 2 * j:2 * j + 2, :], lo_t[:, 2 * j:2 * j + 2, :]
                        src = b[:].rearrange("p (a n) -> p a n", a=2)
                    else:
                        hs, ls, src = hi_t[:, j, :], lo_t[:, j, :], b[:]
                    dve.scalar_tensor_tensor(out=ls, in0=src, scalar=SCALE if kind == "q" else 1.0,
                                             in1=hs.bitcast(F32), op0=ALU.mult, op1=ALU.subtract)\
                        .then_inc(free_of(job), 1)
                elif kind == "z":
                    h = job[1]
                    if h == 0:
                        dve.wait_ge(rg_done, RB)
                        for i in range(T):
                            end = left_at[i] + seen[i]
                            dve.memset(left[:, end:end + 1], 1.0).then_inc(ones_set, 1)
                        dve.wait_ge(ones_set, T)
                    else:
                        dve.wait_ge(weights_ready, h)
                    for b in range(3):
                        wait_read(dve, ("z", h, b))
                        for i, _ in Z_IN[b]:
                            w = seen[i]
                            dve.tensor_tensor_scan(left[:, left_at[i]:left_at[i] + w][:, ::-1],
                                                   rest[:, z_at[i]:z_at[i] + w][:, ::-1],
                                                   ones[:, 0:1].broadcast_to([P, w]), 1.0,
                                                   ALU.mult, ALU.mult).then_inc(left_ready, 1)
                    n = 0
                    for b in range(3):
                        for i, _ in Z_IN[b]:
                            n += 1
                            w = seen[i]
                            dve.wait_ge(left_ready, T * h + n)
                            ins = dve.tensor_tensor(beta[:, z_at[i]:z_at[i] + w], beta[:, z_at[i]:z_at[i] + w],
                                                    left[:, left_at[i] + 1:left_at[i] + 1 + w], ALU.mult)
                    ins.then_inc(weights_ready, 1)
                elif kind == "wT":
                    h = job[1]
                    for b in range(3):
                        wb = wait_full(dve, ("wT", h, b))
                        cols = slice(HALF * b, HALF * b + FILL[b])
                        dve.wait_ge(wT_hi_ready, 3 * h + b + 1)
                        dve.tensor_tensor(wT_lo[:, cols], wb[:, 0:FILL[b]], wT_hi[:, cols].bitcast(F32),
                                          ALU.subtract).then_inc(free_of(("wT", h, b)), 1)
                elif kind == "pv":
                    h = job[1]
                    pr, s = h // 2, h % 2
                    b = wait_full(dve, job)
                    dve.wait_ge(o_hi_ready, h + 1)
                    dve.tensor_tensor(o_lo[HD * s:HD * s + HD, pr, :], b[HD * s:HD * s + HD, :],
                                      o_hi[HD * s:HD * s + HD, pr, :].bitcast(F32), ALU.subtract)\
                        .then_inc(free_of(job), 1)
            for c in range(done, chunk_of["ao", 0] + 3):
                lo_part(c)
            done = chunk_of["ao", 0] + 3
            for m in range(KD):
                dve.wait_ge(sig_ready, 2 * m + 2)
                b = wait_full(dve, ("ya", m))
                dve.tensor_tensor(gate_a[:, m, :], b[:], gate_a[:, m, :], ALU.mult).then_inc(free_of(("ya", m)), 1)
                b = wait_full(dve, ("yr", m))
                dve.tensor_tensor(gate_r[:, m, :], b[:], gate_r[:, m, :], ALU.mult).then_inc(free_of(("yr", m)), 1)
                for key in (("ya", m), ("yr", m)):
                    wait_read(dve, key)
                step(dve.tensor_tensor(gate_a[:, m, :], gate_a[:, m, :], gate_r[:, m, :], ALU.add))
                step(dve.tensor_copy(m_hi[:, m, :], gate_a[:, m, :]))
                dve.tensor_tensor(m_lo[:, m, :], gate_a[:, m, :], m_hi[:, m, :].bitcast(F32), ALU.subtract)\
                    .then_inc(merged_ready, 1)
                if m == 3:
                    for c in range(done, done + 2):
                        lo_part(c)
                    done += 2
            dve.wait_ge(x_again, 16 * T)
            for n in range(2):
                while done < chunk_of["wo", n, 1] + 3:
                    lo_part(done)
                    done += 1
                for i in range(T):
                    b = wait_full(dve, ("x2", n, i))
                    xs = x2[:, i, HALF * n:HALF * n + HALF]
                    dve.tensor_tensor(xs, b[:], xs, ALU.add).then_inc(free_of(("x2", n, i)), 1)
            while done < C_MOE + 3:
                lo_part(done)
                done += 1
            for i in range(T):
                mean_sq(1, i)
            dve.wait_ge(gB_in, 16)
            for i in range(T):
                dve.wait_ge(rstd_done, T + i + 1)
                dve.scalar_tensor_tensor(out=h2[:, i, :], in0=x2[:, i, :], scalar=rstd[:, 1, i:i + 1],
                                         in1=gB[:], op0=ALU.mult, op1=ALU.mult).then_inc(h2_ready, 1)
            dve.wait_ge(route_made, 1)
            step(dve.tensor_scalar(rev[:], iota_i[:], -1.0, float(NE), ALU.mult, ALU.add))
            step(dve.tensor_scalar(e_base[:], iota_i[:], float(S), None, ALU.mult))
            for k in range(1, KD, 2):
                b = wait_full(dve, ("h2T", k))
                dve.tensor_copy(h2T[:, k, :], b[:]).then_inc(free_of(("h2T", k)), 1)

            def first_max(src, n, onehot, top):
                r = rev[:, NE - n:NE].unsqueeze(1).broadcast_to([P, T, n])
                step(dve.tensor_reduce(top, src, AX, ALU.max))
                step(dve.tensor_tensor(eq[:, :, 0:n], src, top.unsqueeze(2).broadcast_to([P, T, n]), ALU.is_equal))
                step(dve.tensor_tensor(cand[:, :, 0:n], eq[:, :, 0:n], r, ALU.mult))
                step(dve.tensor_reduce(best[:], cand[:, :, 0:n], AX, ALU.max))
                step(dve.tensor_tensor(onehot, cand[:, :, 0:n], best[:].unsqueeze(2).broadcast_to([P, T, n]),
                                       ALU.is_equal))

            b = wait_full(dve, "logits")
            dve.tensor_copy(lg[:], b[:, 0:T * NL].rearrange("p (i n) -> p i n", n=NL))\
                .then_inc(free_of("logits"), 1)
            wait_read(dve, "logits")
            first_max(lg[:, :, 0:NG], NG, in_group[:], mx[:])
            dve.tensor_tensor(dg[:], lg[:, :, 0:NG], mx[:].unsqueeze(2).broadcast_to([P, T, NG]),
                              ALU.subtract).then_inc(gexp_in, 1)
            step(dve.tensor_scalar(pen[:], in_group[:], BIG, BIG, ALU.mult, ALU.subtract))
            EG = NE // NG
            for i in range(T):
                el_i = el[:, i, :].rearrange("p (g e) -> p g e", e=EG)
                dve_in = lg[:, i, NG:NL].rearrange("p (g e) -> p g e", e=EG)
                step(dve.tensor_tensor(el_i, dve_in, in_group[:, i, :].unsqueeze(2).broadcast_to([P, NG, EG]), ALU.mult))
                step(dve.tensor_tensor(el_i, el_i, pen[:, i, :].unsqueeze(2).broadcast_to([P, NG, EG]), ALU.add))
            first_max(el[:], NE, M[:, 0], v12[:, 0, :])
            step(dve.scalar_tensor_tensor(out=el[:], in0=M[:, 0], scalar=-2 * BIG, in1=el[:],
                                          op0=ALU.mult, op1=ALU.add))
            first_max(el[:], NE, M[:, 1], v12[:, 1, :])
            dve.tensor_tensor(dv[:], v12[:, 1, :], v12[:, 0, :], ALU.subtract).then_inc(vexp_in, 1)
            dve.tensor_tensor(both[:], M[:, 0], M[:, 1], ALU.add).then_inc(both_ready, 1)
            dve.wait_ge(gexp_ready, 1)
            step(dve.tensor_reduce(gsum[:], dg[:], AX, ALU.add))
            step(dve.reciprocal(ggate[:], gsum[:]))
            dve.wait_ge(vexp_ready, 1)
            step(dve.tensor_scalar(gsum[:], dv[:], 1.0, None, ALU.add))
            step(dve.reciprocal(gsum[:], gsum[:]))
            step(dve.tensor_tensor(combine_w[:, 0, :], gsum[:], ggate[:], ALU.mult))
            step(dve.tensor_tensor(combine_w[:, 1, :], combine_w[:, 0, :], dv[:], ALU.mult))
            b = wait_full(dve, "pos")
            dve.tensor_copy(pos[:], b[:, 0:(T + 1) * NE].rearrange("p (i n) -> p i n", n=NE))\
                .then_inc(free_of("pos"), 1)
            wait_read(dve, "pos")
            for k in range(2):
                step(dve.tensor_tensor(eq[:], M[:, k], pos[:, 0:T, :], ALU.mult))
                step(dve.tensor_reduce(place[:, k, :], eq[:], AX, ALU.add))
                step(dve.tensor_tensor(cand[:], M[:, k], e_base[:].unsqueeze(1).broadcast_to([P, T, NE]), ALU.mult))
                step(dve.tensor_reduce(slot[:, k, :], cand[:], AX, ALU.add))
            step(dve.tensor_scalar(over[:], place[:], float(P), None, ALU.is_ge))
            for n in (2, 3):
                step(dve.tensor_scalar(ov2[:], place[:], float(n * P), None, ALU.is_ge))
                step(dve.tensor_tensor(over[:], over[:], ov2[:], ALU.add))
            step(dve.scalar_tensor_tensor(out=ov2[:], in0=slot[:], scalar=1.0 / P, in1=over[:],
                                          op0=ALU.mult, op1=ALU.add))
            step(dve.scalar_tensor_tensor(out=ov2[:], in0=place[:], scalar=float(4 * NE), in1=ov2[:],
                                          op0=ALU.mult, op1=ALU.add))
            step(dve.scalar_tensor_tensor(out=ov2[:], in0=over[:], scalar=-float(P * 4 * NE), in1=ov2[:],
                                          op0=ALU.mult, op1=ALU.add))
            dve.tensor_copy(addr_i[:], ov2[:]).then_inc(slots_ready, 1)
            dve.wait_ge(slots_ready, 1)
            step(dve.tensor_scalar(ov2[:], place[:], float(P - 1), None, ALU.min))
            step(dve.scalar_tensor_tensor(out=ov2[:], in0=slot[:], scalar=float(P) / S, in1=ov2[:],
                                          op0=ALU.mult, op1=ALU.add))
            step(dve.tensor_copy(slot_i[:], ov2[:]))
            step(dve.tensor_scalar(ov2[:], place[:], -float(P), 0.0, ALU.add, ALU.max))
            step(dve.scalar_tensor_tensor(out=ov2[:], in0=slot[:], scalar=float(OVER * P) / S, in1=ov2[:],
                                          op0=ALU.mult, op1=ALU.add))
            step(dve.tensor_copy(over_slot_i[:], ov2[:]))
            step(dve.tensor_scalar(ov2[:], place[:], float(P), None, ALU.is_ge))
            step(dve.tensor_tensor(over_w[:], ov2[:], combine_w[:], ALU.mult))
            step(dve.tensor_tensor(combine_w[:], combine_w[:], over_w[:], ALU.subtract))
            step(dve.tensor_reduce(mx[:, 0:1], pos[:, T, :], AX, ALU.max))
            dve.tensor_copy(most_i[:], mx[:, 0:1]).then_inc(rows_ready, 1)

            def evict_XT(key, par, it, n):
                for a, bk in enumerate(("XT", "XT2")):
                    b = wait_full(dve, (bk, key), it=it)
                    dve.wait_ge(XT_hi_ready, n + a + 1)
                    dve.tensor_tensor(XT_lo[par][:, 4 * a:4 * a + 4, :], b[:].rearrange("p (k t) -> p k t", t=P),
                                      XT_hi[par][:, 4 * a:4 * a + 4, :].bitcast(F32), ALU.subtract)\
                        .then_inc(free_of((bk, key)), 1)

            evict_XT("first", 0, 0, 0)
            lo_part(C_MOE + 3)

            def dve_step(par, it, last=False):
                if not last:
                    evict_XT(par, 1 - par, it, it * 4 + 2 * par + 2)
                c = step_base(par)
                lo_part(c + 2, it)
                lo_part(c + 3, it)
                gkey = ("G", "first") if par == 0 else ("G", 0)
                wait_read(dve, gkey, it=it)
                b = wait_full(dve, ("U", par), it=it)
                dve.tensor_tensor(he[:], b[:], sil[:], ALU.mult).then_inc(free_of(("U", par)), 1)
                if not last:
                    lo_part(c + 4, it)
                b = wait_full(dve, ("heT", par), it=it)
                dve.wait_ge(heT_hi_ready, it * 2 + par + 1)
                dve.tensor_tensor(heT_lo[:], b[:].rearrange("p (k t) -> p k t", t=P), heT_hi[:].bitcast(F32),
                                  ALU.subtract).then_inc(free_of(("heT", par)), 1)
                if not last:
                    lo_part(c + 5, it)
                    c += 2
                lo_part(c + 4, it)
                lo_part(c + 5, it)
                b = wait_full(dve, ("Y", "last" if last else par, 1), it=it)
                wait_read(dve, ("Y", par, 0), it=it)
                if not isinstance(it, int) or it > 0:
                    dve.wait_ge(Y_out[par], it * 16)
                dve.tensor_copy(Y[par][:, HALF:], b[:]).then_inc(free_of(("Y", par, 1)), 1)

            dve_step(0, 0)
            dve_step(1, 0)
            with dve.Fori(1, NE // 2 - 1) as it:
                dve_step(0, it)
                dve_step(1, it)
            dve_step(0, NE // 2 - 1)
            dve_step(1, NE // 2 - 1, last=True)
            lo_part(C_TAIL + 2)

            def over_dve(e, j, n):
                dve.wait_ge(over_XT_hi, n * 2 + 2)
                for a in range(2):
                    dve.tensor_tensor(XT_lo[0][:, 4 * a:4 * a + 4, :],
                                      bank[4 + a][:].rearrange("p (k t) -> p k t", t=P),
                                      XT_hi[0][:, 4 * a:4 * a + 4, :].bitcast(F32), ALU.subtract)\
                        .then_inc(over_XT_ready, 1)
                dve.wait_ge(over_sil, n + 1)
                dve.wait_ge(over_used, n * PER_E + 4)
                dve.tensor_tensor(he[:], bank[1][:], sil[:], ALU.mult).then_inc(over_he, 1)
                dve.wait_ge(over_heT_hi, n + 1)
                dve.tensor_tensor(heT_lo[:], bank[3][:].rearrange("p (k t) -> p k t", t=P),
                                  heT_hi[:].bitcast(F32), ALU.subtract).then_inc(over_heT_ready, 1)

            with dve.If(any_over(dve)):
                further_tiles(dve, over_dve)
                dve.wait_ge(over_rows_in, 16 * 2 * T)
                for i in range(T):
                    for k in range(2):
                        dve.scalar_tensor_tensor(out=x2[:, i, :], in0=yg[i][k][:], scalar=over_w[:, k, i:i + 1],
                                                 in1=x2[:, i, :], op0=ALU.mult, op1=ALU.add)\
                            .then_inc(over_added, 1)
                        dve.wait_ge(over_added, 2 * i + k + 1)
            for k in range(KP):
                b = wait_full(dve, ("pT", k))
                dve.wait_ge(pT_hi_ready, k + 1)
                dve.tensor_tensor(pT_lo[:, k, :], b[:], pT_hi[:, k, :].bitcast(F32), ALU.subtract)\
                    .then_inc(free_of(("pT", k)), 1)

            for i in range(T):
                dve.wait_ge(yg_in[i], 32)
                step(dve.scalar_tensor_tensor(out=x2[:, i, :], in0=yg[i][0][:], scalar=combine_w[:, 0, i:i + 1],
                                              in1=x2[:, i, :], op0=ALU.mult, op1=ALU.add))
                dve.scalar_tensor_tensor(out=x2[:, i, :], in0=yg[i][1][:], scalar=combine_w[:, 1, i:i + 1],
                                         in1=x2[:, i, :], op0=ALU.mult, op1=ALU.add).then_inc(x3_ready, 1)
                mean_sq(2, i)
            for i in range(T):
                dve.wait_ge(rstd_done, 2 * T + i + 1)
                dve.wait_ge(x3_ready, i + 1)
                dve.tensor_scalar(xn3[:, i, :], x2[:, i, :], rstd[:, 2, i:i + 1], None, ALU.mult)\
                    .then_inc(xn3_ready, 1)
            for k in range(KD):
                b = wait_full(dve, ("h3T", k))
                dve.wait_ge(h3_hi_ready, k + 1)
                dve.scalar_tensor_tensor(out=h3_lo[:, k, :], in0=b[:], scalar=g_ple[:, k:k + 1],
                                         in1=h3_hi[:, k, :].bitcast(F32), op0=ALU.mult, op1=ALU.subtract)\
                    .then_inc(free_of(("h3T", k)), 1)
            for c in range(C_TAIL + 3, C_END):
                lo_part(c)
            for n in range(2):
                for i in range(T):
                    j = T * n + i
                    dve.wait_ge(sg_ready, j + 1)
                    wait_read(dve, ("pp", i, n))
                    cols = slice(HALF * n, HALF * n + HALF)
                    step(dve.tensor_tensor(sg[j % 2][:], sg[j % 2][:], pp[:, i, cols], ALU.mult))
                    dve.tensor_tensor(x2[:, i, cols], x2[:, i, cols], sg[j % 2][:], ALU.add).then_inc(x4_ready, 1)
            for i in range(T):
                mean_sq(3, i)
            dve.wait_ge(gB_in, 32)
            for i in range(T):
                dve.wait_ge(rstd_done, 3 * T + i + 1)
                dve.scalar_tensor_tensor(out=xn3[:, i, :], in0=x2[:, i, :], scalar=rstd[:, 3, i:i + 1],
                                         in1=gB[:], op0=ALU.mult, op1=ALU.mult).then_inc(out_ready, 1)

        @block.tensor
        def _(pe):
            def mm3(dst, lhs, rhs, first, last, skip=False):
                pe.matmul(dst, lhs[0], rhs[0], start=first, stop=False, skip_group_check=skip)
                pe.matmul(dst, lhs[0], rhs[1], start=False, stop=False, skip_group_check=skip)
                return pe.matmul(dst, lhs[1], rhs[0], start=False, stop=last, skip_group_check=skip)

            def chunk(c, k, it=0):
                s = c % SPLIT_SLOTS
                n = c + 1 + PER_IT * it
                pe.wait_ge(hi_ready, n)
                pe.wait_ge(lo_dve, n)
                pe.wait_ge(lo_pool, n)
                return [t[s][:].rearrange("p (k n) -> p k n", k=k) for t in (whi, wlo)]

            def used(ins):
                ins.then_inc(w_used, 1)

            pe.wait_ge(consts_made, 1)
            for i in range(T):
                pe.wait_ge(xn_ready, i + 1)
                for k in range(KD):
                    ins = pe.transpose(bank[k][:, P * i:P * i + P], x_sb[:, i, k::KD], ident[:])
                    if i == T - 1:
                        ins.then_inc(full_of(("hT", k)), 1)
            hT = (hT_hi, hT_lo)
            pe.wait_ge(consts_cast, 2)
            for job in JOBS:
                kind = job[0]
                if kind in ("xr", "xg", "q", "k", "g"):
                    if kind == "g":
                        n = job[1] // 2
                        c, j = (chunk_of["ga", n] if n < 4 else chunk_of["gr", n - 4]), job[1] % 2
                    elif kind in ("q", "k"):
                        c, j = chunk_of[kind, job[1]], job[2]
                    else:
                        c, j = chunk_of[kind, job[1] // 2], job[1] % 2
                    w = chunk(c, KD)
                    b = wait_free(pe, job)
                    for k in range(KD):
                        if job == JOBS[0]:
                            wait_read(pe, ("hT", k))
                        ins = mm3(b[:], [t[:, k, P * j:P * j + P] for t in w], [t[:, k, :] for t in hT],
                                  k == 0, k == KD - 1)
                    ins.then_inc(full_of(job), 1)
                    if job == JOBS[0]:
                        n = (CW + 4) * RB
                        pe.wait_ge(params_in, 16 * 5)
                        pb = wait_free(pe, "params")
                        pe.transpose(pb[:, 0:n], par_rows[:], ident[0:n, 0:n]).then_inc(full_of("params"), 1)
                elif kind == "v":
                    _, g, j = job
                    w = chunk(chunk_of["v", g], KD)
                    b = wait_free(pe, job)
                    for a in range(2):
                        i = 2 * j + a
                        for k in range(KD):
                            ins = mm3(b[:, 256 * a:256 * a + 256], [t[:, k, P * i:P * i + P] for t in hT],
                                      [t[:, k, :] for t in w], k == 0, k == KD - 1)
                    ins.then_inc(full_of(job), 1)
                elif kind == "rg":
                    for m in (2 * job[1], 2 * job[1] + 1):
                        pe.wait_ge(xc_ready, m + 1)
                        for s, key in enumerate(("rga", "rgx")):
                            b = wait_free(pe, (key, m))
                            if m == 0 and s == 0:
                                pe.wait_ge(rg_w_ready, 4)
                            ins = mm3(b[:], [t[s][:, m, :] for t in (wg_hi, wg_lo)],
                                      [t[m % 2][:] for t in (xc_hi, xc_lo)], True, True)
                            ins.then_inc(full_of((key, m)), 1)
                elif kind == "z":
                    h = job[1]
                    g = h // 4
                    lp, s = (h % 4) // 2, h % 2
                    if h % 4 == 0:
                        for key in ("q", "k", "v"):
                            for j in range(2):
                                wait_read(pe, (key, g, j))
                    rows = slice(HD * s, HD * s + HD)
                    for b in range(3):
                        zb = wait_free(pe, ("z", h, b))
                        for i, col in Z_IN[b]:
                            q = [t[rows, lp, P * i:P * i + P] for t in (q_hi, q_lo)]
                            k = [t[rows, lp, 0:seen[i]] for t in (k_hi, k_lo)]
                            zt = zb[:, col:col + seen[i]]
                            pe.matmul(zt, q[0], k[0], start=True, stop=False, skip_group_check=True)
                            pe.matmul(zb[:, col + P * i:col + P * i + P], hidden[:], ident_r[:], start=False,
                                      stop=False, skip_group_check=True)
                            pe.matmul(zt, q[0], k[1], start=False, stop=False, skip_group_check=True)
                            ins = pe.matmul(zt, q[1], k[0], start=False, stop=True, skip_group_check=True)
                        ins.then_inc(full_of(("z", h, b)), 1)
                elif kind == "wT":
                    h = job[1]
                    pe.wait_ge(weights_ready, h + 1)
                    for b in range(3):
                        wb = wait_free(pe, ("wT", h, b))
                        for j, col in W_IN[b]:
                            for i in range(j, T):
                                at_t = col + P * (i - j)
                                ins = pe.transpose(wb[:, at_t:at_t + P], beta[:, z_at[i] + P * j:z_at[i] + P * j + P],
                                                   ident[:])
                        ins.then_inc(full_of(("wT", h, b)), 1)
                elif kind == "pv":
                    h = job[1]
                    lp = (h % 4) // 2
                    for b in range(3):
                        wait_read(pe, ("wT", h, b))
                    b = wait_free(pe, job)
                    for j in range(T):
                        ins = mm3(b[:, P * j:], [t[:, j, P * lp:P * lp + P] for t in (v_hi, v_lo)],
                                  [t[:, w_at[j]:w_at[j] + S - P * j] for t in (wT_hi, wT_lo)], j == 0, j == T - 1)
                    ins.then_inc(full_of(job), 1)
            wait_read(pe, ("pv", H - 2))
            wait_read(pe, ("pv", H - 1))
            pe.wait_ge(rg_done, RB)
            for n in range(2):
                wa = chunk(chunk_of["ao", n], 4)
                wr = chunk(chunk_of["ro", n], 4)
                for j in range(4):
                    m = 4 * n + j
                    for key, w, src in (("ya", wa, (o_hi, o_lo)), ("yr", wr, (r_hi, r_lo))):
                        b = wait_free(pe, (key, m))
                        for k in range(4):
                            ins = mm3(b[:], [t[:, k, P * j:P * j + P] for t in w], [t[:, k, :] for t in src],
                                      k == 0, k == 3)
                        ins.then_inc(full_of((key, m)), 1)
            pe.wait_ge(merged_ready, KD)
            for n in range(2):
                for kh in range(2):
                    w = chunk(chunk_of["wo", n, kh], 4)
                    for i in range(T):
                        key = ("x2", n, i)
                        b = wait_free(pe, key) if kh == 0 else bank[banks.at[key][0]]
                        for k in range(4):
                            ins = mm3(b[:], [t[:, 4 * kh + k, P * i:P * i + P] for t in (m_hi, m_lo)],
                                      [t[:, k, :] for t in w], kh == 0 and k == 0, kh == 1 and k == 3)
                        if kh == 1:
                            ins.then_inc(full_of(key), 1)
                        elif i == T - 1:
                            ins.then_inc(w_used, 1)
            for i in range(T):
                pe.wait_ge(h2_ready, i + 1)
            for k in range(KD):
                key = ("h2T", k)
                b = wait_free(pe, key)
                for i in range(T):
                    ins = pe.transpose(b[:, P * i:P * i + P], h2[:, i, k::KD], ident[:])
                ins.then_inc(full_of(key), 1)
            for k in range(KD):
                wait_read(pe, ("h2T", k))
            pe.wait_ge(small_in, 64)
            b = wait_free(pe, "logits")
            for i in range(T):
                cols = b[:, NL * i:NL * i + NL]
                for k in range(KD):
                    pe.matmul(cols, h2T[:, k, P * i:P * i + P], w_route[:, k, :], start=(k == 0), stop=False)
                ins = pe.matmul(cols, ones[0:1, :], b_route[:], start=False, stop=True)
            ins.then_inc(full_of("logits"), 1)
            pe.wait_ge(both_ready, 1)
            b = wait_free(pe, "pos")
            for i in range(T + 1):
                cols = b[:, NE * i:NE * i + NE]
                for j in range(min(i + 1, T)):
                    lhs = before if j == i else ones
                    ins = pe.matmul(cols, lhs[:], both[:, j, :], start=(j == 0), stop=(j == min(i, T - 1)))
            ins.then_inc(full_of("pos"), 1)

            def transpose_X(key, par, it, n):
                pe.wait_ge(X_in[par], n)
                for a, bk in enumerate(("XT", "XT2")):
                    b = wait_free(pe, (bk, key), it=it)
                    for k in range(4):
                        ins = pe.transpose(b[:, P * k:P * k + P], X[par][:, 4 * a + k::KD], ident[:])
                    ins.then_inc(full_of((bk, key)), 1)

            def up_or_gate(key, c, it, par, between=None):
                b = wait_free(pe, key, it=it)
                for half in range(2):
                    if half == 1 and between:
                        between()
                    w = chunk(c + half, 4, it)
                    for k in range(4):
                        kk = 4 * half + k
                        ins = mm3(b[:], [t[par][:, kk, :] for t in (XT_hi, XT_lo)], [t[:, k, :] for t in w],
                                  kk == 0, kk == KD - 1)
                    ins.then_inc(w_used, 1)

            def XT_done(key, it):
                for bk in ("XT", "XT2"):
                    wait_read(pe, (bk, key), it=it)

            transpose_X("first", 0, 0, 16)
            XT_done("first", 0)
            up_or_gate(("G", "first"), C_MOE, 0, 0)

            def pe_step(par, it, last=False):
                c = step_base(par)
                if not last:
                    transpose_X(par, 1 - par, it, it * 16 + 16 + 16 * par)
                up_or_gate(("U", par), c, it, par)

                def transpose_he():
                    wait_read(pe, ("U", par), it=it)
                    b = wait_free(pe, ("heT", par), it=it)
                    for k in range(KF):
                        ins = pe.transpose(b[:, P * k:P * k + P], he[:, k::KF], ident[:])
                    ins.then_inc(full_of(("heT", par)), 1)

                if last:
                    transpose_he()
                else:
                    XT_done(par, it)
                    up_or_gate(("G", par), c + 2, it, 1 - par, between=transpose_he)
                    c += 2
                wait_read(pe, ("heT", par), it=it)
                ys = [wait_free(pe, ("Y", par, n), it=it) for n in range(2)]
                for half in range(2):
                    w = chunk(c + 2 + half, 2, it)
                    for k in range(2):
                        kk = 2 * half + k
                        for n in range(2):
                            ins = mm3(ys[n][:], [t[:, kk, :] for t in (heT_hi, heT_lo)],
                                      [t[:, k, HALF * n:HALF * n + HALF] for t in w], kk == 0, kk == KF - 1)
                            if kk == KF - 1:
                                ins.then_inc(full_of(("Y", par, n)), 1)
                    if half == 0:
                        ins.then_inc(w_used, 1)

            with pe.Fori(0, NE // 2 - 1) as it:
                pe_step(0, it)
                pe_step(1, it)
            pe_step(0, NE // 2 - 1)
            pe_step(1, NE // 2 - 1, last=True)

            def over_pe(e, j, n):
                def use(c, k, products):
                    pe.wait_ge(over_lo_ready, n * PER_E + c + 1)
                    products([t[:].rearrange("p (k n) -> p k n", k=k) for t in (over_hi, over_lo)])\
                        .then_inc(over_used, 1)

                def in_features(b, half):
                    def products(w):
                        for k in range(4):
                            kk = 4 * half + k
                            ins = mm3(b[:], [t[0][:, kk, :] for t in (XT_hi, XT_lo)], [t[:, k, :] for t in w],
                                      kk == 0, kk == KD - 1)
                        return ins
                    return products

                def down(half):
                    def products(w):
                        for h in range(2):
                            for k in range(2):
                                kk = 2 * half + k
                                ins = mm3(bank[6 + h][:], [t[:, kk, :] for t in (heT_hi, heT_lo)],
                                          [t[:, k, HALF * h:HALF * h + HALF] for t in w], kk == 0, kk == KF - 1)
                        return ins
                    return products

                pe.wait_ge(over_X_in, n * 16 + 16)
                for k in range(KD):
                    ins = pe.transpose(bank[4 + k // 4][:, P * (k % 4):P * (k % 4) + P], X[0][:, k::KD], ident[:])
                ins.then_inc(over_XT, 1)
                pe.wait_ge(over_XT_ready, n * 2 + 2)
                for half in range(2):
                    use(half, 4, in_features(bank[0], half))
                for half in range(2):
                    use(2 + half, 4, in_features(bank[1], half))
                pe.wait_ge(over_he, n + 1)
                for k in range(KF):
                    ins = pe.transpose(bank[3][:, P * k:P * k + P], he[:, k::KF], ident[:])
                ins.then_inc(over_heT, 1)
                pe.wait_ge(over_heT_ready, n + 1)
                for half in range(2):
                    use(4 + half, 2, down(half))
                pe.wait_ge(over_Y_ready, n * 2 + 2)

            with pe.If(any_over(pe)):
                for b in range(8):
                    pe.wait_ge(free[b], free_after_experts[b])
                further_tiles(pe, over_pe)

            pe.wait_ge(p_in, 16)
            for k in range(KP):
                b = wait_free(pe, ("pT", k))
                for i in range(T):
                    ins = pe.transpose(b[:, P * i:P * i + P], p_sb[:, i, k::KP], ident[:])
                ins.then_inc(full_of(("pT", k)), 1)
            for k in range(KP):
                wait_read(pe, ("pT", k))
            w = chunk(C_TAIL, KP)
            for i in range(T):
                for n in range(2):
                    b = wait_free(pe, ("pp", i, n))
                    for k in range(KP):
                        ins = mm3(b[:], [t[:, k, P * i:P * i + P] for t in (pT_hi, pT_lo)],
                                  [t[:, k, HALF * n:HALF * n + HALF] for t in w], k == 0, k == KP - 1)
                    ins.then_inc(full_of(("pp", i, n)), 1)
            for i in range(T):
                pe.wait_ge(xn3_ready, i + 1)
            for k in range(KD):
                b = wait_free(pe, ("h3T", k))
                for i in range(T):
                    ins = pe.transpose(b[:, P * i:P * i + P], xn3[:, i, k::KD], ident[:])
                ins.then_inc(full_of(("h3T", k)), 1)
            for k in range(KD):
                wait_read(pe, ("h3T", k))
            for n in range(2):
                for kh in range(2):
                    w = chunk(C_TAIL + 1 + 2 * n + kh, 4)
                    for i in range(T):
                        key = ("pg", n, i)
                        b = bank[banks.at[key][0]]
                        for k in range(4):
                            ins = mm3(b[:], [t[:, 4 * kh + k, P * i:P * i + P] for t in (h3_hi, h3_lo)],
                                      [t[:, k, :] for t in w], kh == 0 and k == 0, kh == 1 and k == 3)
                        if kh == 1:
                            ins.then_inc(full_of(key), 1)
                        elif i == T - 1:
                            ins.then_inc(w_used, 1)


_INS = ["x", "p", "norm_mix", "w_in", "conv_w", "conv_b", "w_rg_a", "b_rg_a", "w_rg_x", "b_rg_x", "rg_lambda",
        "w_attn_o", "w_rnn_o", "w_out", "norm_moe", "w_router_group", "b_router_group", "w_router_expert",
        "b_router_expert", "w_exp_gate", "w_exp_up", "w_exp_down", "norm_ple", "w_ple_gate", "w_ple_proj",
        "norm_final"]
_OUTS = [((1, 512, 1024), "float32")]


def kernel(**inputs):
    import numpy as _np
    import concourse.bacc as _bacc
    from concourse import mybir as _mybir
    from concourse.bass_utils import run_bass_kernel_spmd as _run

    nc = _bacc.Bacc("TRN2", target_bir_lowering=False, num_devices=1)
    arrays, args = {}, []
    for name in _INS:
        a = _np.ascontiguousarray(inputs[name])
        arrays[f"in_{name}_dram"] = a
        args.append(nc.dram_tensor(f"in_{name}_dram", a.shape, _mybir.dt.from_np(a.dtype), kind="ExternalInput").ap())
    for i, (shape, dtype) in enumerate(_OUTS):
        dt = _mybir.dt.from_np(_np.dtype(dtype))
        args.append(nc.dram_tensor(f"out_{i}_dram", shape, dt, kind="ExternalOutput").ap())
    trunk(nc, *args)
    r = _run(nc, [arrays], core_ids=[0])
    return r.results[0]["out_0_dram"]
```

```python
from contextlib import ExitStack

import concourse.bass as bass
from concourse import mybir

ALU = mybir.AluOpType
ACT = mybir.ActivationFunctionType
F32 = mybir.dt.float32
F32R = mybir.dt.float32r
BF16 = mybir.dt.bfloat16
I32 = mybir.dt.int32
U32 = mybir.dt.uint32
AX = mybir.AxisListType.X

P = 128
KB = 1024
BIG = 1e30
EPS = 1e-6
RAW_SLOTS = 4
MORE_SLOTS = 6
SPLIT_SLOTS = 3
CH = 2048
DVE_COLS = 1536


class Banks:

    def __init__(self):
        self.full = [0] * 8
        self.free = [0] * 8
        self.at = {}

    def take(self, key, bank, fills=1, ends=None):
        self.at[key] = (bank, self.free[bank], self.full[bank], ends)
        self.full[bank] += fills if ends is None else 0
        self.free[bank] += 1


def trunk(nc, x, p, norm_mix, w_in, conv_w, conv_b, w_rg_a, b_rg_a, w_rg_x, b_rg_x, rg_lambda,
          w_attn_o, w_rnn_o, w_out, norm_moe, w_router_group, b_router_group, w_router_expert,
          b_router_expert, w_exp_gate, w_exp_up, w_exp_down, norm_ple, w_ple_gate, w_ple_proj,
          norm_final, out):
    _, S, D = x.shape
    T = S // P
    KD = D // P
    DA = w_attn_o.shape[1]
    DR = w_rnn_o.shape[1]
    HD = 64
    H = DA // HD
    NG = w_router_group.shape[2]
    NE = w_exp_gate.shape[1]
    NL = NG + NE
    PD = p.shape[3]
    HALF = 512
    RB = DR // P
    GW = w_rg_a.shape[2]
    CW = conv_w.shape[1]
    SCALE = float(HD) ** -0.5
    assert T * P == HALF and KD == 8 and H == 8 and GW * 2 == P and NE % 2 == 0

    gates_d = nc.dram_tensor("gates_scratch", (2 * KD, P, S), F32).ap()
    h2_d = nc.dram_tensor("h2_scratch", (S, D), F32).ap()
    y_d = nc.dram_tensor("expert_out_scratch", (NE * P, D), F32).ap()
    OVER = S // P - 1
    y_over_d = nc.dram_tensor("expert_over_scratch", (NE * OVER * P, D), F32).ap()

    first_col = {"q": 0, "k": DA, "v": 2 * DA, "xr": 3 * DA, "xg": 3 * DA + DR,
                 "ga": 3 * DA + 2 * DR, "gr": 3 * DA + 2 * DR + D}
    IN_ORDER = ([("xr", 0), ("xg", 0), ("q", 0), ("xr", 1), ("xg", 1), ("k", 0), ("v", 0)]
                + [("ga", n) for n in range(4)] + [("q", 1), ("k", 1), ("v", 1)]
                + [("gr", n) for n in range(4)])
    chunk_of = {key: c for c, key in enumerate(IN_ORDER)}
    chunks = [w_in[0, :, first_col[key] + 256 * n:first_col[key] + 256 * n + 256]
              .rearrange("(p k) n -> p k n", k=KD) for key, n in IN_ORDER]
    for key, w in (("ro", w_rnn_o), ("ao", w_attn_o)):
        for n in range(2):
            chunk_of[key, n] = len(chunks)
            chunks.append(w[0, :, HALF * n:HALF * n + HALF].rearrange("(k p) n -> p k n", p=P))
    for n in range(2):
        for k in range(2):
            chunk_of["wo", n, k] = len(chunks)
            chunks.append(w_out[0, HALF * k:HALF * k + HALF, HALF * n:HALF * n + HALF]
                          .rearrange("(k p) n -> p k n", p=P))
    C_MOE = len(chunks)
    PER_E = 6
    PER_IT = 2 * PER_E
    assert PER_IT % MORE_SLOTS == 0 and PER_IT % SPLIT_SLOTS == 0
    C_TAIL = C_MOE + PER_E * NE
    proj_tail = w_ple_proj[0].rearrange("(p k) n -> p k n", k=PD // P)
    gate_tail = w_ple_gate[0].rearrange("(p k) n -> p k n", k=KD)
    tail_chunks = [proj_tail] + [gate_tail[:, 4 * k:4 * k + 4, HALF * n:HALF * n + HALF]
                                 for n in range(2) for k in range(2)]
    C_END = C_TAIL + len(tail_chunks)

    C_MORE = C_MOE + 2
    assert C_MORE % RAW_SLOTS == 0
    slot_order = list(range(RAW_SLOTS, MORE_SLOTS)) + list(range(RAW_SLOTS))
    raw_slot = [c % RAW_SLOTS if c < C_MORE else slot_order[(c - C_MORE) % MORE_SLOTS] for c in range(C_END)]
    raw_nth = [raw_slot[:c + 1].count(raw_slot[c]) for c in range(C_END)]

    def step_base(e):
        return C_MOE + 2 + PER_E * e

    def gate_src(e, half):
        return w_exp_gate[0, e].rearrange("(p k) n -> p k n", k=KD)[:, 4 * half:4 * half + 4, :]

    banks = Banks()
    for k in range(KD):
        banks.take(("hT", k), k)
    banks.take("params", 7)
    ring = 0
    JOBS = []

    def add(job, bank=None, fills=1):
        nonlocal ring
        if bank is None:
            bank, ring = ring % 2, ring + 1
        banks.take(job, bank, fills, ends=chunk_ended_by(job))
        JOBS.append(job)

    def chunk_ended_by(job):
        kind = job[0]
        if kind in ("xr", "xg") and job[1] % 2 == 1:
            return chunk_of[kind, job[1] // 2]
        if kind in ("q", "k", "v") and job[2] == 1:
            return chunk_of[kind, job[1]]
        if kind == "g" and job[1] % 2 == 1:
            n = job[1] // 2
            return chunk_of["ga", n] if n < 4 else chunk_of["gr", n - 4]
        if kind == "yr" and job[1] % 4 == 3:
            return chunk_of["ro", job[1] // 4]
        return None

    def add_rg(pair):
        for m in (2 * pair, 2 * pair + 1):
            banks.take(("rga", m), 2 + 2 * (m % 2))
            banks.take(("rgx", m), 3 + 2 * (m % 2))
        JOBS.append(("rg", pair))

    def add_rg2(pair):
        JOBS.append(("rg2", pair))

    def add_rec(m):
        JOBS.append(("rec", m))

    def add_pair(pair):
        for kind in ("xr", "xg"):
            for m in (2 * pair, 2 * pair + 1):
                add((kind, m))
        add_rg(pair)

    add_pair(0)
    add(("q", 0, 0))
    add_rg2(0)
    add(("q", 0, 1))
    add_rec(0)
    add_rec(1)
    add_pair(1)
    add(("k", 0, 0))
    add_rg2(1)
    add(("k", 0, 1))
    add(("v", 0, 0))
    add_rec(2)
    add(("v", 0, 1))
    add_rec(3)

    def add_z(h):
        for b in range(3):
            banks.take(("z", h, b), 2 + b)
        JOBS.append(("z", h))

    def add_wT(h):
        for b in range(3):
            banks.take(("wT", h, b), 5 + b)
        JOBS.append(("wT", h))

    fillers = [("g", m) for m in range(2 * KD)]
    for g in range(2):
        if g == 1:
            for b in range(2):
                add(("q", g, b))
            add(("pv", H // 2 - 1))
            for kind in ("k", "v"):
                for b in range(2):
                    add((kind, g, b))
        for h in range(4 * g, 4 * g + 4):
            add_z(h)
            add(fillers.pop(0))
            if h % 4 > 0:
                add(("pv", h - 1))
            add(fillers.pop(0))
            add_wT(h)
    for m in range(KD // 2):
        add(("yr", m))
    add(("pv", H - 1))
    for m in range(KD // 2, KD):
        add(("yr", m))
    for m in range(KD):
        last = m % 4 == 3
        banks.take(("ya", m), (m + 2) % 8, ends=chunk_of["ao", m // 4] if last else None)
    for n in range(2):
        for i in range(T):
            banks.take(("x2", n, i), (4 + i) if n == 0 else i,
                       ends=chunk_of["wo", n, 1] if i == T - 1 else None)
    for k in range(KD):
        banks.take(("h2T", k), (4 + k) % 8)
    banks.take("logitsT", 4)
    banks.take("logits", 5)
    banks.take("pos", 6)
    banks.take("lists", 7)
    banks.take(("XT", "first"), 4)
    banks.take(("XT2", "first"), 5)
    banks.take(("G", "first"), 0, ends=C_MOE + 1)
    per_free = [1, 1, 2, 2, 2, 2, 2, 2]
    per_full = [0, 0, 0, 2, 2, 2, 2, 0]

    def take_step(par, last=False):
        c = step_base(par)
        if not last:
            banks.take(("XT", par), 4)
            banks.take(("XT2", par), 5)
        banks.take(("U", par), 2, ends=c + 1)
        if not last:
            banks.take(("G", par), (par + 1) % 2, ends=c + 3)
            c += 2
        banks.take(("heT", par), 3)
        banks.take(("Y", par, 0), 6)
        banks.take(("Y", par, 1), 7, ends=c + 3)

    keep = {}
    for e in range(NE):
        take_step(e % 2, last=(e == NE - 1))
        if e == 1:
            keep = dict(banks.at)
    banks.at = {**banks.at, **keep}
    free_after_experts = list(banks.free)
    banks.at[("Y", "last", 1)] = (*banks.at[("Y", 1, 1)][:3], banks.at[("Y", 1, 1)][3] - 2)
    for k in range(PD // P):
        banks.take(("pT", k), k)
    for i in range(T):
        for n in range(2):
            banks.take(("pp", i, n), 2 + (2 * i + n) % 6, ends=C_TAIL if (i, n) == (T - 1, 1) else None)
    for k in range(KD):
        banks.take(("h3T", k), k)
    for n in range(2):
        for i in range(T):
            banks.take(("pg", n, i), 4 * n + i, ends=C_TAIL + 2 + 2 * n if i == T - 1 else None)

    with ExitStack() as ctx:
        def sem(name):
            return ctx.enter_context(nc.semaphore(name))

        SLAB = 207 * KB
        ctx.enter_context(nc.sbuf_tensor("slab", [P, SLAB // 4], F32))
        origin = nc.sbuf_base - SLAB
        BYTES = 4

        def at(name, shape, offset, dt=F32):
            n = BYTES
            for d in shape[1:]:
                n *= d
            assert offset + n <= SLAB, name
            return nc.alloc_sbuf_tensor_at(name, shape, dt, offset=origin + offset)

        RAW0, HI0, LO0 = 0, 32 * KB, 56 * KB
        C0 = 80 * KB
        RA = 86 * KB
        RQ = RA + 32 * KB
        RO = RQ + 24 * KB
        RR = RO + 16 * KB
        RT = RR + 16 * KB

        raw = [at(f"raw{s}", [P, CH], RAW0 + 8 * KB * s if s < RAW_SLOTS else RT + 5 * KB + 8 * KB * (s - RAW_SLOTS))
               for s in range(MORE_SLOTS)]
        whi = [at(f"whi{s}", [P, CH], HI0 + 8 * KB * s, F32R) for s in range(SPLIT_SLOTS)]
        wlo = [at(f"wlo{s}", [P, CH], LO0 + 8 * KB * s, F32R) for s in range(SPLIT_SLOTS)]

        off = C0

        def small(name, shape, dt=F32):
            nonlocal off
            t = at(name, shape, off, dt)
            n = BYTES
            for d in shape[1:]:
                n *= d
            off += (n + 31) // 32 * 32
            assert off <= RA
            return t

        ident = small("ident", [P, P])
        ident_r = small("ident_r", [P, P], F32R)
        ones = small("ones", [P, P])
        before = small("before", [P, P])
        hidden = small("hidden", [P, P], F32R)
        g_mix = small("g_mix", [P, KD])
        g_ple = small("g_ple", [P, KD])
        params = small("params", [P, CW * RB + 4 * RB])
        lam = small("lam", [P, 6, RB])
        decay = small("decay", [P, RB])
        log_a = small("log_a", [P, RB])
        neghalf_col = small("neghalf_col", [P, 1])
        ss = small("ss", [P, 4, T])
        ms = small("ms", [P, 4, T])
        rstd = small("rstd", [P, 4, T])
        combine_w = small("combine_w", [P, 2, T])
        over_w = small("over_w", [P, 2, T])
        over_slot_i = small("over_slot_i", [P, 2, T], I32)
        slot_i = small("slot_i", [P, 2, T], I32)
        w_route = small("w_route", [P, KD, NL])
        b_route = small("b_route", [NL, 1])
        before_b = small("before_b", [P, P // 2])
        ones_b = small("ones_b", [P, P // 2])
        token_id = small("token_id", [P, T], I32)
        token_of = small("token_of", [P, 4 * NE], I32)
        idx_now = [small(f"idx_now{s}", [P, 1], I32) for s in range(2)]
        most_i = small("most_i", [P, 1], I32)

        hT_hi = at("hT_hi", [P, KD, S], RA, F32R)
        hT_lo = at("hT_lo", [P, KD, S], RA + 16 * KB, F32R)
        x_sb = at("x_sb", [P, T, D], RQ)
        junk = at("junk", [P, D], RQ + 16 * KB)
        par_rows = at("par_rows", [CW * RB + 4 * RB, P], RQ + 20 * KB)
        wg_raw = [at(f"wg_raw{s}", [P, RB, P], RO + 2 * KB * s) for s in range(2)]
        wg_hi = [at(f"wg_hi{s}", [P, RB, P], RO + 4 * KB + 2 * KB * s, F32R) for s in range(2)]
        wg_lo = [at(f"wg_lo{s}", [P, RB, P], RO + 8 * KB + 2 * KB * s, F32R) for s in range(2)]
        q_hi = at("q_hi", [P, 2, S], RQ, F32R)
        q_lo = at("q_lo", [P, 2, S], RQ + 4 * KB, F32R)
        k_hi = at("k_hi", [P, 2, S], RQ + 8 * KB, F32R)
        k_lo = at("k_lo", [P, 2, S], RQ + 12 * KB, F32R)
        v_hi = at("v_hi", [P, T, 256], RQ + 16 * KB, F32R)
        v_lo = at("v_lo", [P, T, 256], RQ + 20 * KB, F32R)
        o_hi = at("o_hi", [P, H // 2, S], RO, F32R)
        o_lo = at("o_lo", [P, H // 2, S], RO + 8 * KB, F32R)
        r_hi = at("r_hi", [P, RB, S], RR, F32R)
        r_lo = at("r_lo", [P, RB, S], RR + 8 * KB, F32R)
        XRW = S + CW - 1
        xrp = [at(f"xrp{s}", [P, XRW], RT + 2080 * s) for s in range(2)]
        t0 = RT + 2080 * 2
        xgs, xc, xc_hi, xc_lo, rr, th, ig = [
            [at(f"{n}{s}", [P, S], t0 + 2 * KB * (2 * j + s), F32R if n in ("xc_hi", "xc_lo") else F32)
             for s in range(2)] for j, n in enumerate(("xgs", "xc", "xc_hi", "xc_lo", "rr", "th", "ig"))]
        ge = [at(f"ge{s}", [P, S], RO + 12 * KB + 2 * KB * s) for s in range(2)]
        seen = [P * (i + 1) for i in range(T)]
        Z_IN = [[(3, 0)], [(2, 0), (0, seen[2])], [(1, 0)]]
        W_IN = [[(0, 0)], [(1, 0), (3, seen[2])], [(2, 0)]]
        FILL = [HALF, HALF, seen[1]]
        W5 = sum(FILL)
        z_at = {i: HALF * b + col for b in range(3) for i, col in Z_IN[b]}
        w_at = {j: HALF * b + col for b in range(3) for j, col in W_IN[b]}
        beta = at("beta", [P, W5], RT)
        rest = at("rest", [P, W5], RT + 5 * KB)
        left = at("left", [P, W5 + T], RT + 10 * KB)
        left_at = {i: z_at[i] + n for n, i in enumerate(sorted(range(T), key=lambda i: z_at[i]))}
        wT_hi = at("wT_hi", [P, W5], RT + 15 * KB + 32, F32R)
        wT_lo = at("wT_lo", [P, W5], RT + 20 * KB + 32, F32R)
        STAGES = 3
        stage = [at(f"stage{s}", [P, S], RT + 25 * KB + 32 + 2 * KB * s) for s in range(STAGES)]
        gate_a = at("gate_a", [P, KD, S], RA)
        gate_r = at("gate_r", [P, KD, S], RA + 16 * KB)
        yr = at("yr", [P, KD, S], RQ)
        m_hi = at("m_hi", [P, KD, S], RT, F32R)
        m_lo = at("m_lo", [P, KD, S], RT + 16 * KB, F32R)
        x2 = at("x2", [P, T, D], RQ)
        gB = at("gB", [P, D], RQ + 20 * KB)
        h2 = at("h2", [P, T, D], RR)
        h2T = at("h2T", [P, KD, S], RO)
        off_r = RA + 20 * KB

        def route(name, shape, dt=F32):
            nonlocal off_r
            t = at(name, shape, off_r, dt)
            n = BYTES
            for d in shape[1:]:
                n *= d
            off_r += (n + 31) // 32 * 32
            assert off_r <= RA + 32 * KB
            return t

        X = [at(f"X{s}", [P, D], RA + 4 * KB * s) for s in range(2)]
        XT_hi = [at(f"XT_hi{s}", [P, KD, P], RA + 8 * KB + 4 * KB * s, F32R) for s in range(2)]
        XT_lo = [at(f"XT_lo{s}", [P, KD, P], RA + 16 * KB + 4 * KB * s, F32R) for s in range(2)]
        Y = [at(f"Y{s}", [P, D], RA + 24 * KB + 4 * KB * s) for s in range(2)]
        KF = HALF // P
        sil = at("sil", [P, HALF], RT + 25 * KB)
        he = at("he", [P, HALF], RT + 27 * KB)
        heT_hi = at("heT_hi", [P, KF, P], RT + 29 * KB, F32R)
        heT_lo = at("heT_lo", [P, KF, P], RT + 31 * KB, F32R)
        over_raw = at("over_raw", [P, CH], RO)
        over_hi = at("over_hi", [P, CH], RO + 8 * KB, F32R)
        over_lo = at("over_lo", [P, CH], RO + 16 * KB, F32R)
        p_sb = at("p_sb", [P, T, PD], RT + 21 * KB)
        yg = [[at(f"yg{i}{k}", [P, D], RO + 4 * KB * (2 * i + k)) for k in range(2)] for i in range(T)]
        pp = at("pp", [P, T, D], RA)
        KP = PD // P
        pT_hi = at("pT_hi", [P, KP, S], RA + 16 * KB, F32R)
        pT_lo = at("pT_lo", [P, KP, S], RA + 20 * KB, F32R)
        sg = [at(f"sg{s}", [P, HALF], RA + 24 * KB + 2 * KB * s) for s in range(2)]
        junk2 = at("junk2", [P, D], RQ + 16 * KB)
        xn3 = at("xn3", [P, T, D], RT + 1 * KB + 4 * KB)
        h3_hi = at("h3_hi", [P, KD, S], RO, F32R)
        h3_lo = at("h3_lo", [P, KD, S], RR, F32R)

        lg = route("lg", [P, T, NL])
        lgT = route("lgT", [NL, S])
        iota_i = route("iota_i", [P, P], I32)
        iota_f = route("iota_f", [P, P])
        token_f = route("token_f", [P, T])
        rev = route("rev", [P, NE])
        e_base = route("e_base", [P, NE])
        eq = route("eq", [P, T, NE])
        cand = route("cand", [P, T, NE])
        mx = route("mx", [P, T])
        best = route("best", [P, T])
        in_group = route("in_group", [P, T, NG])
        dg = route("dg", [P, T, NG])
        gsum = route("gsum", [P, T])
        ggate = route("ggate", [P, T])
        el = route("el", [P, T, NE])
        pen = route("pen", [P, T, NG])
        M = route("M", [P, 2, T, NE])
        both = route("both", [P, T, NE // 2])
        v12 = route("v12", [P, 2, T])
        dv = route("dv", [P, T])
        pos = route("pos", [P, T + 1, NE])
        slot = route("slot", [P, 2, T])
        place = route("place", [P, 2, T])
        row = route("row", [P, 2, T])
        tile_at = route("tile_at", [P, 2, T])
        over = route("over", [P, 2, T])
        ov2 = route("ov2", [P, 2, T])
        TL = 4 * NE
        in_row = at("in_row", [P, 2, T, P], RA + 12 * KB, F32R)
        in_tile = at("in_tile", [P, 2, T, TL], RA + 16 * KB, F32R)

        bank = [ctx.enter_context(nc.psum_tensor(f"bank{b}", [P, HALF], F32)) for b in range(8)]

        full = [sem(f"bank{b}_full") for b in range(8)]
        free = [sem(f"bank{b}_free") for b in range(8)]
        raw_in = [sem(f"raw{s}_in") for s in range(MORE_SLOTS)]
        hi_ready = sem("hi_ready")
        lo_dve = sem("lo_dve_ready")
        lo_pool = sem("lo_pool_ready")
        w_used = sem("w_used")
        x_in = [sem(f"x_in{i}") for i in range(T)]
        params_in = sem("params_in")
        g_mix_in = sem("g_mix_in")
        g_ple_in = sem("g_ple_in")
        rg_weights_in = sem("rg_weights_in")
        rg_zeroed = sem("rg_zeroed")
        consts_made = sem("consts_made")
        consts_cast = sem("consts_cast")
        ss_done = sem("ss_done")
        ms_done = sem("ms_done")
        rstd_done = sem("rstd_done")
        xn_ready = sem("xn_ready")
        hT_hi_ready = sem("hT_hi_ready")
        lam_exp = sem("lam_exp")
        decay_ready = sem("decay_ready")
        rg_w_ready = sem("rg_w_ready")
        xc_ready = sem("xc_ready")
        th_ready = sem("th_ready")
        root_ready = sem("root_ready")
        a_ready = sem("a_ready")
        ig_ready = sem("input_gated")
        ge_sq = sem("ge_sq")
        ge_in = sem("ge_in")
        ge_th = sem("ge_th")
        rg_done = sem("rg_done")
        qkv_hi = sem("qkv_hi_ready")
        stage_out = [sem(f"stage{s}_out") for s in range(STAGES)]
        ones_set = sem("left_ones_set")
        left_ready = sem("left_ready")
        weights_ready = sem("attention_weights_ready")
        wT_hi_ready = sem("wT_hi_ready")
        o_hi_ready = sem("o_hi_ready")
        gates_in = [sem("gates_a_in"), sem("gates_r_in")]
        gated = sem("rnn_gated")
        merged_ready = sem("merged_ready")
        x_again = sem("x_again")
        gB_in = sem("gB_in")
        small_in = sem("small_in")
        route_made = sem("route_made")
        h2_ready = sem("h2_ready")
        h2_out = sem("h2_out")
        gexp_in = sem("gexp_in")
        gexp_ready = sem("gexp_ready")
        vexp_in = sem("vexp_in")
        vexp_ready = sem("vexp_ready")
        both_ready = sem("both_ready")
        marks_ready = sem("list_marks_ready")
        rows_ready = sem("rows_ready")
        X_in = [sem(f"X{s}_in") for s in range(2)]
        XT_hi_ready = sem("XT_hi_ready")
        heT_hi_ready = sem("heT_hi_ready")
        Y_out = [sem(f"Y{s}_out") for s in range(2)]
        p_in = sem("p_in")
        pT_hi_ready = sem("pT_hi_ready")
        yg_in = [sem(f"yg_in{i}") for i in range(T)]
        x3_ready = sem("x3_ready")
        h3_hi_ready = sem("h3_hi_ready")
        sg_ready = sem("sg_ready")
        x4_ready = sem("x4_ready")
        out_ready = sem("out_ready")
        out_done = sem("out_done")
        act_chain = sem("act_chain")
        dve_chain = sem("dve_chain")
        pool_chain = sem("pool_chain")
        index_ready = sem("index_ready")
        over_raw_in = sem("over_raw_in")
        over_hi_ready = sem("over_hi_ready")
        over_lo_ready = sem("over_lo_ready")
        over_used = sem("over_used")
        over_index = sem("over_index_ready")
        over_X_in = sem("over_X_in")
        over_XT = sem("over_XT_full")
        over_XT_hi = sem("over_XT_hi_ready")
        over_XT_ready = sem("over_XT_ready")
        over_sil = sem("over_sil_ready")
        over_he = sem("over_he_ready")
        over_heT = sem("over_heT_full")
        over_heT_hi = sem("over_heT_hi_ready")
        over_heT_ready = sem("over_heT_ready")
        over_Y_ready = sem("over_Y_ready")
        over_Y_out = sem("over_Y_out")
        over_rows_in = sem("over_rows_in")
        over_added = sem("over_added")

        block = ctx.enter_context(nc.Block())

        def wait_full(eng, key, nth=1, it=0):
            b, _, f, ends = banks.at[key]
            if ends is None:
                eng.wait_ge(full[b], f + nth + it * per_full[b])
            else:
                eng.wait_ge(w_used, ends + 1 + PER_IT * it)
            return bank[b]

        def wait_free(eng, key, it=0):
            b, r, _, _ = banks.at[key]
            if not isinstance(it, int) or r + it * per_free[b] > 0:
                eng.wait_ge(free[b], r + it * per_free[b])
            return bank[b]

        def wait_read(eng, key, it=0):
            b, r, _, _ = banks.at[key]
            eng.wait_ge(free[b], r + 1 + it * per_free[b])

        def full_of(key):
            b, _, _, ends = banks.at[key]
            return full[b] if ends is None else w_used

        def free_of(key):
            return free[banks.at[key][0]]

        def job_splits(job, done, split):
            kind = job[0]
            if kind in ("xr", "xg"):
                c = chunk_of[kind, job[1] // 2]
            elif kind in ("q", "k", "v"):
                c = chunk_of[kind, job[1]]
            elif kind == "g":
                n = job[1] // 2
                c = chunk_of["ga", n] if n < 4 else chunk_of["gr", n - 4]
            elif kind == "yr":
                c = chunk_of["ro", job[1] // 4]
            else:
                return done
            while done < c + 3:
                split(done)
                done += 1
            return done

        def further_tiles(eng, tile):
            with eng.Fori(0, NE) as e:
                with eng.Fori(0, OVER) as j:
                    tile(e, j + 1, e * OVER + j)

        def any_over(eng):
            eng.wait_ge(rows_ready, 1)
            return eng.value_load(most_i[0:1, 0:1], min_val=0, max_val=S) > P

        def chained(eng, chain):
            count = [0]

            def step(ins):
                ins.then_inc(chain, 1)
                count[0] += 1
                eng.wait_ge(chain, count[0])
            return step

        @block.sync
        def _(sp):
            for i in range(T):
                sp.dma_start(x_sb[:, i, :], x[0, P * i:P * i + P, :]).then_inc(x_in[i], 16)
            sp.dma_start(g_mix[:], norm_mix[0].rearrange("(p k) -> p k", k=KD)).then_inc(g_mix_in, 16)

            def load(c, it, src):
                s = raw_slot[c]
                if raw_nth[c] > 1 or not isinstance(it, int) or it > 0:
                    last = c - (RAW_SLOTS if c < C_MORE else MORE_SLOTS)
                    sp.wait_ge(lo_dve, last + 1 + PER_IT * it)
                    sp.wait_ge(lo_pool, last + 1 + PER_IT * it)
                elif c >= C_MORE:
                    sp.wait_ge(w_used, C_MOE)
                dst = raw[s][:].rearrange("p (k n) -> p k n", k=src.shape[1])
                sp.dma_start(dst, src).then_inc(raw_in[s], 16)

            def load_step(par, it, e, last=False):
                c = step_base(par)
                up = w_exp_up[0, e].rearrange("(p k) n -> p k n", k=KD)
                down = w_exp_down[0, e].rearrange("(p k) n -> p k n", k=KF)
                load(c, it, up[:, 0:4, :])
                load(c + 1, it, up[:, 4:8, :])
                if not last:
                    load(c + 2, it, gate_src(e + 1, 0))
                    load(c + 3, it, gate_src(e + 1, 1))
                    c += 2
                load(c + 2, it, down[:, 0:2, :])
                load(c + 3, it, down[:, 2:4, :])

            load(0, 0, chunks[0])
            rows = [(conv_w[0].rearrange("j (m p) -> (j m) p", p=P), CW * RB)] + [
                (t[0].rearrange("(m p) -> m p", p=P), RB) for t in (conv_b, b_rg_a, b_rg_x, rg_lambda)]
            r0 = 0
            for src, n in rows:
                sp.dma_start(par_rows[r0:r0 + n, :], src).then_inc(params_in, 16)
                r0 += n
            load(1, 0, chunks[1])
            sp.wait_ge(rg_zeroed, 2)
            for s, w in enumerate((w_rg_a, w_rg_x)):
                pairs = w[0].rearrange("(m a) i j -> a i m j", a=2)
                for a in range(2):
                    sp.dma_start(wg_raw[s][GW * a:GW * a + GW, :, GW * a:GW * a + GW], pairs[a])\
                        .then_inc(rg_weights_in, 16)
            sp.dma_start(g_ple[:], norm_ple[0].rearrange("(p k) -> p k", k=KD)).then_inc(g_ple_in, 16)
            sp.dma_start(w_route[:, :, 0:NG], w_router_group[0].rearrange("(p k) n -> p k n", k=KD)).then_inc(small_in, 16)
            sp.dma_start(w_route[:, :, NG:NL], w_router_expert[0].rearrange("(p k) n -> p k n", k=KD)).then_inc(small_in, 16)
            sp.dma_start(b_route[0:NG, :], b_router_group[0].rearrange("(n o) -> n o", o=1)).then_inc(small_in, 16)
            sp.dma_start(b_route[NG:NL, :], b_router_expert[0].rearrange("(n o) -> n o", o=1)).then_inc(small_in, 16)
            for c, src in list(enumerate(chunks))[2:]:
                load(c, 0, src)
            for half in range(2):
                load(C_MOE + half, 0, gate_src(0, half))
            def rows_out(par, it):
                wait_read(sp, ("Y", par, 1), it=it)
                sp.dma_start(y_d.rearrange("(e r) d -> e r d", e=NE)[it * 2 + par], Y[par][:])\
                    .then_inc(Y_out[par], 16)

            load_step(0, 0, 0)
            load_step(1, 0, 1)
            with sp.Fori(1, NE // 2 - 1) as it:
                rows_out(0, it - 1)
                load_step(0, it, it * 2)
                rows_out(1, it - 1)
                load_step(1, it, it * 2 + 1)
            rows_out(0, NE // 2 - 2)
            load_step(0, NE // 2 - 1, NE - 2)
            rows_out(1, NE // 2 - 2)
            load_step(1, NE // 2 - 1, NE - 1, last=True)
            rows_out(0, NE // 2 - 1)
            for j, src in enumerate(tail_chunks):
                load(C_TAIL + j, 0, src)
            rows_out(1, NE // 2 - 1)
            for i in range(T):
                sp.wait_ge(out_ready, i + 1)
                sp.dma_start(out[0, P * i:P * i + P, :], xn3[:, i, :]).then_inc(out_done, 16)
            sp.wait_ge(out_done, 16 * T)

        @block.gpsimd
        def _(pool):
            step = chained(pool, pool_chain)

            def lo_part(c, it=0):
                pool.wait_ge(hi_ready, c + 1 + PER_IT * it)
                pool.tensor_tensor(wlo[c % SPLIT_SLOTS][:, DVE_COLS:], raw[raw_slot[c]][:, DVE_COLS:],
                                   whi[c % SPLIT_SLOTS][:, DVE_COLS:].bitcast(F32),
                                   ALU.subtract).then_inc(lo_pool, 1)

            def root_of_ms(norm, i):
                pool.wait_ge(ms_done, T * norm + i + 1)
                pool.tensor_tensor(rstd[:, norm, i:i + 1], ms[:, norm, i:i + 1], neghalf_col[:],
                                   ALU.pow).then_inc(rstd_done, 1)

            step(pool.memset(neghalf_col[:], -0.5))
            pool.memset(wg_raw[0][:], 0.0).then_inc(rg_zeroed, 1)
            pool.memset(wg_raw[1][:], 0.0).then_inc(rg_zeroed, 1)
            step(pool.memset(ones[:], 1.0))
            step(pool.affine_select(out=ident[:], in_=ones[:], compare_op=ALU.is_equal, fill=0.0,
                                    base=0, pattern=[[1, P]], channel_multiplier=-1))
            step(pool.affine_select(out=before[:], in_=ones[:], compare_op=ALU.is_gt, fill=0.0,
                                    base=0, pattern=[[1, P]], channel_multiplier=-1))
            pool.iota(token_id[:], pattern=[[P, T]], base=0, channel_multiplier=1).then_inc(consts_made, 1)
            for i in range(T):
                root_of_ms(0, i)
            lo_part(0)
            lo_part(1)

            done = 2
            for job in JOBS:
                done = job_splits(job, done, lo_part)
                if job[0] == "rg":
                    for m in (2 * job[1], 2 * job[1] + 1):
                        pool.wait_ge(ge_sq, m + 1)
                        step(pool.tensor_scalar(ge[m % 2][:], ge[m % 2][:], 0.044715, 1.0, ALU.mult, ALU.add))
                        pool.tensor_tensor(ge[m % 2][:], ge[m % 2][:], xgs[m % 2][:], ALU.mult).then_inc(ge_in, 1)
                    for m in (2 * job[1], 2 * job[1] + 1):
                        wait_read(pool, ("rgx", m))
                        pool.wait_ge(xc_ready, m + 1)
                        pool.tensor_tensor(ig[m % 2][:], ig[m % 2][:], xc[m % 2][:], ALU.mult).then_inc(ig_ready, 1)
            pool.wait_ge(gates_in[1], 16)
            for m in range(KD):
                wait_read(pool, ("yr", m))
                pool.tensor_tensor(gate_r[:, m, :], yr[:, m, :], gate_r[:, m, :], ALU.mult).then_inc(gated, 1)
            for c in range(done, chunk_of["wo", 0, 0] + 3):
                lo_part(c)
            pool.wait_ge(merged_ready, KD)
            pool.iota(iota_i[:], pattern=[[1, P]], base=0, channel_multiplier=0).then_inc(route_made, 1)
            for c in range(chunk_of["wo", 0, 0] + 3, C_MOE + 2):
                lo_part(c)
            for i in range(T):
                root_of_ms(1, i)
            lo_part(C_MOE + 2)
            wait_read(pool, "lists")
            pool.wait_ge(h2_out, 16 * T)

            for par in range(2):
                step(pool.tensor_copy(idx_now[par][:], token_of[:, 4 * par:4 * par + 1]))
                pool.indirect_dma_start(X[par][:], None, h2_d,
                                        bass.IndirectOffsetOnAxis(idx_now[par][:].bitcast(U32), 0))\
                    .then_inc(X_in[par], 16)

            def pool_step(par, it, e, last=False, more=True):
                c = step_base(par)
                if more:
                    wait_read(pool, "lists")
                    wait_full(pool, ("XT2", "first") if par == 0 else ("XT2", 0), it=it)
                    pool.tensor_copy(idx_now[par][:], token_of[:, bass.ds(e * 4 + 8, 1)]).then_inc(index_ready, 1)
                    pool.wait_ge(index_ready, it * 2 + par + 1)
                lo_part(c + 2, it)
                if more:
                    pool.wait_ge(h2_out, 16 * T)
                    pool.indirect_dma_start(X[par][:], None, h2_d,
                                            bass.IndirectOffsetOnAxis(idx_now[par][:].bitcast(U32), 0))\
                        .then_inc(X_in[par], 16)
                for j in range(3, 6 if last else 8):
                    lo_part(c + j, it)

            lo_part(C_MOE + 3)
            with pool.Fori(0, NE // 2 - 1) as it:
                pool_step(0, it, it * 2)
                pool_step(1, it, it * 2 + 1)
            pool_step(0, NE // 2 - 1, NE - 2, more=False)
            pool_step(1, NE // 2 - 1, NE - 1, last=True, more=False)
            lo_part(C_TAIL + 2)

            def over_pool(e, j, n):
                pool.tensor_copy(idx_now[0][:], token_of[:, bass.ds(e * 4 + j, 1)]).then_inc(over_index, 1)
                pool.wait_ge(over_index, n + 1)
                for c in range(PER_E):
                    pool.wait_ge(over_hi_ready, n * PER_E + c + 1)
                    pool.tensor_tensor(over_lo[:], over_raw[:], over_hi[:].bitcast(F32), ALU.subtract)\
                        .then_inc(over_lo_ready, 1)
                    if c == 0:
                        pool.wait_ge(h2_out, 16 * T)
                        pool.indirect_dma_start(X[0][:], None, h2_d,
                                                bass.IndirectOffsetOnAxis(idx_now[0][:].bitcast(U32), 0))\
                            .then_inc(over_X_in, 16)
                    pool.wait_ge(over_used, n * PER_E + c + 1)

            with pool.If(any_over(pool)):
                wait_full(pool, ("XT2", 0), it=NE // 2 - 2)
                further_tiles(pool, over_pool)
                pool.wait_ge(over_Y_out, 16 * NE * OVER)
                for i in range(T):
                    for k in range(2):
                        pool.indirect_dma_start(yg[i][k][:], None, y_over_d,
                                                bass.IndirectOffsetOnAxis(over_slot_i[:, k, i:i + 1].bitcast(U32), 0))\
                            .then_inc(over_rows_in, 16)
                pool.wait_ge(over_added, 2 * T)
            for s in range(2):
                pool.wait_ge(Y_out[s], 16 * (NE // 2))
            for i in range(T):
                for k in range(2):
                    pool.indirect_dma_start(yg[i][k][:], None, y_d,
                                            bass.IndirectOffsetOnAxis(slot_i[:, k, i:i + 1].bitcast(U32), 0))\
                        .then_inc(yg_in[i], 16)
            lo_part(C_TAIL + 3)
            for i in range(T):
                root_of_ms(2, i)
            lo_part(C_TAIL + 4)
            for i in range(T):
                root_of_ms(3, i)

        @block.scalar
        def _(act):
            step = chained(act, act_chain)
            copy = ACT.Copy

            def hi_part(c, it=0):
                if c >= SPLIT_SLOTS:
                    act.wait_ge(w_used, c + 1 - SPLIT_SLOTS + PER_IT * it)
                act.wait_ge(raw_in[raw_slot[c]], 16 * (raw_nth[c] + PER_IT // MORE_SLOTS * it))
                act.activation(whi[c % SPLIT_SLOTS][:], raw[raw_slot[c]][:], copy).then_inc(hi_ready, 1)

            def squares(norm, i, src, scrap):
                if T * norm + i > 0:
                    act.wait_ge(ss_done, T * norm + i)
                act.activation(scrap[:], src, ACT.Square, accum_out=ss[:, norm, i:i + 1]).then_inc(ss_done, 1)

            for i in range(T):
                act.wait_ge(x_in[i], 16)
                squares(0, i, x_sb[:, i, :], junk)
            hi_part(0)
            act.wait_ge(g_mix_in, 16)
            for k in range(KD):
                b = wait_full(act, ("hT", k))
                act.activation(hT_hi[:, k, :], b[:], copy, scale=g_mix[:, k:k + 1]).then_inc(hT_hi_ready, 1)
            hi_part(1)
            act.wait_ge(rg_weights_in, 64)
            for s in range(2):
                act.activation(wg_hi[s][:], wg_raw[s][:], copy).then_inc(rg_w_ready, 1)
            wait_read(act, "params")
            step(act.activation(lam[:, 0, :], params[:, (CW + 3) * RB:(CW + 4) * RB], ACT.Abs))
            act.activation(lam[:, 1, :], lam[:, 0, :], ACT.Exp, scale=-1.0).then_inc(lam_exp, 1)
            done = 2
            gate_n = 0
            for job in JOBS:
                kind = job[0]
                done = job_splits(job, done, hi_part)
                if kind == "xr":
                    m = job[1]
                    b = wait_full(act, job)
                    if m >= 2:
                        act.wait_ge(rg_done, m - 1)
                    act.activation(xrp[m % 2][:, CW - 1:], b[:], copy).then_inc(free_of(job), 1)
                elif kind == "xg":
                    m = job[1]
                    b = wait_full(act, job)
                    if m >= 2:
                        act.wait_ge(rg_done, m - 1)
                    act.activation(xgs[m % 2][:], b[:], copy).then_inc(free_of(job), 1)
                elif kind == "rg":
                    ms_ = (2 * job[1], 2 * job[1] + 1)
                    if job[1] > 0:
                        act.wait_ge(rg_done, ms_[0])
                    else:
                        act.wait_ge(decay_ready, 2)
                    for m in ms_:
                        ba = params[:, (CW + 1) * RB + m:(CW + 1) * RB + m + 1]
                        bx = params[:, (CW + 2) * RB + m:(CW + 2) * RB + m + 1]
                        b = wait_full(act, ("rga", m))
                        act.activation(rr[m % 2][:], b[:], ACT.Sigmoid, bias=ba).then_inc(free_of(("rga", m)), 1)
                        b = wait_full(act, ("rgx", m))
                        act.activation(ig[m % 2][:], b[:], ACT.Sigmoid, bias=bx).then_inc(free_of(("rgx", m)), 1)
                    for m in ms_:
                        wait_read(act, ("xg", m))
                        act.activation(ge[m % 2][:], xgs[m % 2][:], ACT.Square).then_inc(ge_sq, 1)
                    for m in ms_:
                        wait_read(act, ("rga", m))
                        act.activation(th[m % 2][:], rr[m % 2][:], ACT.Tanh, scale=decay[:, m:m + 1])\
                            .then_inc(th_ready, 1)
                elif kind == "rg2":
                    ms_ = (2 * job[1], 2 * job[1] + 1)
                    for m in ms_:
                        act.wait_ge(ge_in, m + 1)
                        act.activation(ge[m % 2][:], ge[m % 2][:], ACT.Tanh, scale=0.7978845608028654)\
                            .then_inc(ge_th, 1)
                    for m in ms_:
                        act.wait_ge(th_ready, m + 1)
                        act.activation(rr[m % 2][:], rr[m % 2][:], ACT.Exp, scale=log_a[:, m:m + 1])\
                            .then_inc(a_ready, 1)
                    for m in ms_:
                        act.activation(th[m % 2][:], th[m % 2][:], ACT.Sqrt).then_inc(root_ready, 1)
                elif kind in ("q", "k", "v"):
                    _, g, j = job
                    b = wait_full(act, job)
                    dst = {"q": q_hi, "k": k_hi, "v": v_hi}[kind]
                    d = dst[:, 2 * j:2 * j + 2, :] if kind == "v" else dst[:, j, :]
                    src = b[:].rearrange("p (a n) -> p a n", a=2) if kind == "v" else b[:]
                    if g == 1:
                        if kind == "v":
                            wait_full(act, ("pv", H // 2 - 1))
                        else:
                            wait_full(act, ("wT", H // 2 - 1, 2))
                    act.activation(d, src, copy, scale=SCALE if kind == "q" else 1.0).then_inc(qkv_hi, 1)
                elif kind == "g":
                    s = gate_n % STAGES
                    b = wait_full(act, job)
                    if gate_n >= STAGES:
                        act.wait_ge(stage_out[s], 16 * (gate_n // STAGES))
                    if gate_n == 0:
                        act.wait_ge(rg_done, RB)
                    act.activation(stage[s][:], b[:], ACT.Sigmoid).then_inc(free_of(job), 1)
                    wait_read(act, job)
                    act.dma_start(gates_d[job[1]], stage[s][:]).then_inc(stage_out[s], 16)
                    gate_n += 1
                elif kind == "yr":
                    m = job[1]
                    b = wait_full(act, job)
                    if m == 0:
                        wait_full(act, ("z", H - 1, 2))
                    act.activation(yr[:, m, :], b[:], copy).then_inc(free_of(job), 1)
                elif kind == "z":
                    h = job[1]
                    if h == 0:
                        act.wait_ge(rg_done, RB)
                    else:
                        wait_full(act, ("wT", h - 1, 2))
                    for b in range(3):
                        zb = wait_full(act, ("z", h, b))
                        cols = slice(HALF * b, HALF * b + FILL[b])
                        act.activation(beta[:, cols], zb[:, 0:FILL[b]], ACT.Sigmoid)
                        act.activation(rest[:, cols], zb[:, 0:FILL[b]], ACT.Sigmoid, scale=-1.0)\
                            .then_inc(free_of(("z", h, b)), 1)
                elif kind == "wT":
                    h = job[1]
                    if h > 0:
                        wait_full(act, ("pv", h - 1))
                    for b in range(3):
                        wb = wait_full(act, ("wT", h, b))
                        act.activation(wT_hi[:, HALF * b:HALF * b + FILL[b]], wb[:, 0:FILL[b]], copy)\
                            .then_inc(wT_hi_ready, 1)
                    if h == H - 1:
                        for t in range(STAGES):
                            act.wait_ge(stage_out[t], 16 * len(range(t, 2 * KD, STAGES)))
                        for g, t in reversed(list(enumerate((gate_a, gate_r)))):
                            act.dma_start(t[:], gates_d[KD * g:KD * g + KD].rearrange("m p t -> p m t"))\
                                .then_inc(gates_in[g], 16)
                elif kind == "pv":
                    h = job[1]
                    pr, s = h // 2, h % 2
                    b = wait_full(act, job)
                    act.activation(o_hi[HD * s:HD * s + HD, pr, :], b[HD * s:HD * s + HD, :], copy)\
                        .then_inc(o_hi_ready, 1)
            for c in range(done, chunk_of["ao", 0] + 3):
                hi_part(c)
            done = chunk_of["ao", 0] + 3
            wait_read(act, ("pv", H - 1))
            act.dma_start(gB[:], norm_moe[0:1, :].broadcast_to([P, D])).then_inc(gB_in, 16)
            for c in range(done, chunk_of["wo", 0, 0] + 3):
                hi_part(c)
            act.wait_ge(merged_ready, KD)
            for i in range(T):
                act.dma_start(x2[:, i, :], x[0, P * i:P * i + P, :]).then_inc(x_again, 16)
            for c in range(chunk_of["wo", 0, 0] + 3, C_MOE + 2):
                hi_part(c)
            for i in range(T):
                wait_read(act, ("x2", 0, i))
                wait_read(act, ("x2", 1, i))
                squares(1, i, x2[:, i, :], junk2)
            for i in range(T - 1):
                act.wait_ge(h2_ready, i + 1)
                act.dma_start(h2_d[P * i:P * i + P, :], h2[:, i, :]).then_inc(h2_out, 16)
            for k in range(0, KD, 2):
                b = wait_full(act, ("h2T", k))
                act.activation(h2T[:, k, :], b[:], copy).then_inc(free_of(("h2T", k)), 1)
            act.wait_ge(h2_ready, T)
            act.dma_start(h2_d[P * (T - 1):P * T, :], h2[:, T - 1, :]).then_inc(h2_out, 16)
            hi_part(C_MOE + 2)
            act.wait_ge(merged_ready, KD)
            act.dma_start(p_sb[:], p[0, 0].rearrange("(i p) n -> p i n", p=P)).then_inc(p_in, 16)
            b = wait_full(act, "logitsT")
            act.activation(lgT[:], b[0:NL, :], ACT.Identity, bias=b_route[:]).then_inc(free_of("logitsT"), 1)
            act.wait_ge(gexp_in, 1)
            act.activation(dg[:], dg[:], ACT.Exp).then_inc(gexp_ready, 1)
            act.wait_ge(vexp_in, 1)
            act.activation(dv[:], dv[:], ACT.Exp).then_inc(vexp_ready, 1)

            def evict_XT(key, par, it):
                for a, bk in enumerate(("XT", "XT2")):
                    b = wait_full(act, (bk, key), it=it)
                    act.activation(XT_hi[par][:, 4 * a:4 * a + 4, :], b[:].rearrange("p (k t) -> p k t", t=P),
                                   copy).then_inc(XT_hi_ready, 1)

            evict_XT("first", 0, 0)
            hi_part(C_MOE + 3)

            def act_step(par, it, last=False):
                gkey = ("G", "first") if par == 0 else ("G", 0)
                b = wait_full(act, gkey, it=it)
                wait_free(act, ("U", par), it=it)
                act.activation(sil[:], b[:], ACT.Silu).then_inc(free_of(gkey), 1)
                if not last:
                    evict_XT(par, 1 - par, it)
                c = step_base(par)
                hi_part(c + 2, it)
                hi_part(c + 3, it)
                if not last:
                    hi_part(c + 4, it)
                b = wait_full(act, ("heT", par), it=it)
                act.activation(heT_hi[:], b[:].rearrange("p (k t) -> p k t", t=P), copy).then_inc(heT_hi_ready, 1)
                if not last:
                    hi_part(c + 5, it)
                    c += 2
                hi_part(c + 4, it)
                hi_part(c + 5, it)
                b = wait_full(act, ("Y", par, 0), it=it)
                if not isinstance(it, int) or it > 0:
                    act.wait_ge(Y_out[par], it * 16)
                act.activation(Y[par][:, 0:HALF], b[:], copy).then_inc(free_of(("Y", par, 0)), 1)

            act_step(0, 0)
            act_step(1, 0)
            with act.Fori(1, NE // 2 - 1) as it:
                act_step(0, it)
                act_step(1, it)
            act_step(0, NE // 2 - 1)
            act_step(1, NE // 2 - 1, last=True)
            hi_part(C_TAIL + 2)

            def over_act(e, j, n):
                gate, up = [w[0, e].rearrange("(p k) n -> p k n", k=KD) for w in (w_exp_gate, w_exp_up)]
                down = w_exp_down[0, e].rearrange("(p k) n -> p k n", k=KF)
                parts = [gate[:, 0:4, :], gate[:, 4:8, :], up[:, 0:4, :], up[:, 4:8, :],
                         down[:, 0:2, :], down[:, 2:4, :]]

                def hi(c):
                    act.dma_start(over_raw[:].rearrange("p (k n) -> p k n", k=parts[c].shape[1]), parts[c])\
                        .then_inc(over_raw_in, 16)
                    act.wait_ge(over_raw_in, n * (16 * PER_E) + 16 * (c + 1))
                    act.activation(over_hi[:], over_raw[:], copy).then_inc(over_hi_ready, 1)
                    if c == 0:
                        act.wait_ge(over_XT, n + 1)
                        for a in range(2):
                            act.activation(XT_hi[0][:, 4 * a:4 * a + 4, :],
                                           bank[4 + a][:].rearrange("p (k t) -> p k t", t=P), copy)\
                                .then_inc(over_XT_hi, 1)
                    if c == 3:
                        act.wait_ge(over_used, n * PER_E + 2)
                        act.activation(sil[:], bank[0][:], ACT.Silu).then_inc(over_sil, 1)
                        act.wait_ge(over_heT, n + 1)
                        act.activation(heT_hi[:], bank[3][:].rearrange("p (k t) -> p k t", t=P), copy)\
                            .then_inc(over_heT_hi, 1)
                    act.wait_ge(over_used, n * PER_E + c + 1)
                for c in range(PER_E):
                    hi(c)
                for h in range(2):
                    act.activation(Y[0][:, HALF * h:HALF * h + HALF], bank[6 + h][:], copy).then_inc(over_Y_ready, 1)
                act.wait_ge(over_Y_ready, n * 2 + 2)
                act.dma_start(y_over_d.rearrange("(n r) d -> n r d", r=P)[n], Y[0][:]).then_inc(over_Y_out, 16)
                act.wait_ge(over_Y_out, n * 16 + 16)

            with act.If(any_over(act)):
                act.wait_ge(h2_out, 16 * T)
                act.wait_ge(Y_out[0], 16 * (NE // 2))
                further_tiles(act, over_act)
            for k in range(KP):
                b = wait_full(act, ("pT", k))
                act.activation(pT_hi[:, k, :], b[:], copy).then_inc(pT_hi_ready, 1)
            for i in range(T):
                for n in range(2):
                    b = wait_full(act, ("pp", i, n))
                    act.activation(pp[:, i, HALF * n:HALF * n + HALF], b[:], copy).then_inc(free_of(("pp", i, n)), 1)
            act.dma_start(gB[:], norm_final.rearrange("(o n) -> o n", o=1).broadcast_to([P, D])).then_inc(gB_in, 16)
            for k in range(KD):
                b = wait_full(act, ("h3T", k))
                if k == 0:
                    act.wait_ge(g_ple_in, 16)
                act.activation(h3_hi[:, k, :], b[:], copy, scale=g_ple[:, k:k + 1]).then_inc(h3_hi_ready, 1)
            hi_part(C_TAIL + 3)
            for i in range(T):
                act.wait_ge(x3_ready, i + 1)
                squares(2, i, x2[:, i, :], junk2)
            hi_part(C_TAIL + 4)
            for n in range(2):
                for i in range(T):
                    j = T * n + i
                    b = wait_full(act, ("pg", n, i))
                    if j == 0:
                        act.wait_ge(rstd_done, 3 * T)
                    if j >= 2:
                        act.wait_ge(x4_ready, j - 1)
                    act.activation(sg[j % 2][:], b[:], ACT.Sigmoid, scale=rstd[:, 2, i:i + 1]).then_inc(sg_ready, 1)
                    if n == 1 and i > 0:
                        act.wait_ge(x4_ready, T + i)
                        squares(3, i - 1, x2[:, i - 1, :], junk2)
            act.wait_ge(x4_ready, 2 * T)
            squares(3, T - 1, x2[:, T - 1, :], junk2)

        @block.vector
        def _(dve):
            step = chained(dve, dve_chain)

            def lo_part(c, it=0):
                dve.wait_ge(hi_ready, c + 1 + PER_IT * it)
                dve.tensor_tensor(wlo[c % SPLIT_SLOTS][:, 0:DVE_COLS], raw[raw_slot[c]][:, 0:DVE_COLS],
                                  whi[c % SPLIT_SLOTS][:, 0:DVE_COLS].bitcast(F32),
                                  ALU.subtract).then_inc(lo_dve, 1)

            def mean_sq(norm, i):
                dve.wait_ge(ss_done, T * norm + i + 1)
                dve.tensor_scalar(ms[:, norm, i:i + 1], ss[:, norm, i:i + 1], 1.0 / D, EPS,
                                  ALU.mult, ALU.add).then_inc(ms_done, 1)

            for i in range(T):
                mean_sq(0, i)
                dve.wait_ge(rstd_done, i + 1)
                dve.tensor_scalar(x_sb[:, i, :], x_sb[:, i, :], rstd[:, 0, i:i + 1], None, ALU.mult)\
                    .then_inc(xn_ready, 1)
            dve.wait_ge(consts_made, 1)
            dve.tensor_copy(ident_r[:], ident[:]).then_inc(consts_cast, 1)
            dve.tensor_copy(before_b[:].bitcast(BF16), before[:]).then_inc(consts_cast, 1)
            dve.tensor_copy(ones_b[:].bitcast(BF16), ones[:]).then_inc(consts_cast, 1)
            dve.tensor_scalar(hidden[:], before[:], BIG, BIG, ALU.mult, ALU.subtract).then_inc(consts_cast, 1)
            lo_part(0)
            for k in range(KD):
                dve.wait_ge(hT_hi_ready, k + 1)
                b = wait_full(dve, ("hT", k))
                if k == 0:
                    dve.wait_ge(g_mix_in, 16)
                dve.scalar_tensor_tensor(out=hT_lo[:, k, :], in0=b[:], scalar=g_mix[:, k:k + 1],
                                         in1=hT_hi[:, k, :].bitcast(F32), op0=ALU.mult, op1=ALU.subtract)\
                    .then_inc(free_of(("hT", k)), 1)
            lo_part(1)
            b = wait_full(dve, "params")
            dve.tensor_copy(params[:], b[:, 0:(CW + 4) * RB]).then_inc(free_of("params"), 1)
            wait_read(dve, "params")
            lm = params[:, (CW + 3) * RB:(CW + 4) * RB]
            dve.wait_ge(lam_exp, 1)
            step(dve.tensor_scalar(lam[:, 2, :], lam[:, 1, :], 2.0, None, ALU.add))
            step(dve.reciprocal(lam[:, 2, :], lam[:, 2, :]))
            step(dve.tensor_tensor(lam[:, 2, :], lam[:, 1, :], lam[:, 2, :], ALU.mult))
            step(dve.tensor_tensor(lam[:, 3, :], lam[:, 2, :], lam[:, 2, :], ALU.mult))
            step(dve.tensor_scalar(lam[:, 4, :], lam[:, 3, :], 1.0 / 17, 1.0 / 15, ALU.mult, ALU.add))
            for n in (13, 11, 9, 7, 5, 3, 1):
                step(dve.tensor_tensor(lam[:, 4, :], lam[:, 4, :], lam[:, 3, :], ALU.mult))
                step(dve.tensor_scalar(lam[:, 4, :], lam[:, 4, :], 1.0 / n, None, ALU.add))
            step(dve.scalar_tensor_tensor(out=lam[:, 4, :], in0=lam[:, 4, :], scalar=8.0, in1=lam[:, 2, :],
                                          op0=ALU.mult, op1=ALU.mult))
            step(dve.tensor_scalar(lam[:, 5, :], lm, -4.0, 0.0, ALU.mult, ALU.max))
            dve.tensor_tensor(decay[:], lam[:, 4, :], lam[:, 5, :], ALU.add).then_inc(decay_ready, 1)
            dve.wait_ge(decay_ready, 1)
            dve.tensor_scalar(log_a[:], decay[:], -2.0, None, ALU.mult).then_inc(decay_ready, 1)
            dve.wait_ge(rg_w_ready, 2)
            for s in range(2):
                dve.tensor_tensor(wg_lo[s][:], wg_raw[s][:], wg_hi[s][:].bitcast(F32), ALU.subtract)\
                    .then_inc(rg_w_ready, 1)
            for s in range(2):
                step(dve.memset(xrp[s][:, 0:CW - 1], 0.0))
            done = 2
            for job in JOBS:
                kind = job[0]
                done = job_splits(job, done, lo_part)
                if kind == "xr":
                    m = job[1]
                    wait_read(dve, job)
                    s = m % 2
                    if m >= 2:
                        wait_full(dve, ("rgx", m - 2))
                        dve.wait_ge(rg_done, m - 1)
                    taps = [params[:, RB * j + m:RB * j + m + 1] for j in range(CW)]
                    step(dve.tensor_scalar(xc[s][:], xrp[s][:, 0:S], taps[0],
                                           params[:, CW * RB + m:CW * RB + m + 1], ALU.mult, ALU.add))
                    for j in range(1, CW):
                        step(dve.scalar_tensor_tensor(out=xc[s][:], in0=xrp[s][:, j:j + S], scalar=taps[j],
                                                      in1=xc[s][:], op0=ALU.mult, op1=ALU.add))
                    step(dve.tensor_copy(xc_hi[s][:], xc[s][:]))
                    dve.tensor_tensor(xc_lo[s][:], xc[s][:], xc_hi[s][:].bitcast(F32), ALU.subtract)\
                        .then_inc(xc_ready, 1)
                elif kind == "rec":
                    m = job[1]
                    s = m % 2
                    dve.wait_ge(a_ready, m + 1)
                    dve.wait_ge(root_ready, m + 1)
                    step(dve.scalar_tensor_tensor(out=th[s][:], in0=rr[s][:], scalar=1.0, in1=th[s][:],
                                                  op0=ALU.add, op1=ALU.mult))
                    dve.wait_ge(ig_ready, m + 1)
                    step(dve.tensor_tensor(th[s][:], th[s][:], ig[s][:], ALU.mult))
                    step(dve.tensor_tensor_scan(xc[s][:], rr[s][:], th[s][:], 0.0, ALU.mult, ALU.add))
                    dve.wait_ge(ge_th, m + 1)
                    step(dve.scalar_tensor_tensor(out=ge[s][:], in0=ge[s][:], scalar=1.0, in1=xgs[s][:],
                                                  op0=ALU.add, op1=ALU.mult))
                    step(dve.scalar_tensor_tensor(out=ge[s][:], in0=xc[s][:], scalar=0.5, in1=ge[s][:],
                                                  op0=ALU.mult, op1=ALU.mult))
                    step(dve.tensor_copy(r_hi[:, m, :], ge[s][:]))
                    dve.tensor_tensor(r_lo[:, m, :], ge[s][:], r_hi[:, m, :].bitcast(F32), ALU.subtract)\
                        .then_inc(rg_done, 1)
                elif kind in ("q", "k", "v"):
                    _, g, j = job
                    b = wait_full(dve, job)
                    n = 6 * g + 2 * "qkv".index(kind) + j + 1
                    dve.wait_ge(qkv_hi, n)
                    hi_t, lo_t = {"q": (q_hi, q_lo), "k": (k_hi, k_lo), "v": (v_hi, v_lo)}[kind]
                    if kind == "v":
                        hs, ls = hi_t[:, 2 * j:2 * j + 2, :], lo_t[:, 2 * j:2 * j + 2, :]
                        src = b[:].rearrange("p (a n) -> p a n", a=2)
                    else:
                        hs, ls, src = hi_t[:, j, :], lo_t[:, j, :], b[:]
                    dve.scalar_tensor_tensor(out=ls, in0=src, scalar=SCALE if kind == "q" else 1.0,
                                             in1=hs.bitcast(F32), op0=ALU.mult, op1=ALU.subtract)\
                        .then_inc(free_of(job), 1)
                elif kind == "z":
                    h = job[1]
                    if h == 0:
                        dve.wait_ge(rg_done, RB)
                        for i in range(T):
                            end = left_at[i] + seen[i]
                            dve.memset(left[:, end:end + 1], 1.0).then_inc(ones_set, 1)
                        dve.wait_ge(ones_set, T)
                    else:
                        dve.wait_ge(weights_ready, h)
                    for b in range(3):
                        wait_read(dve, ("z", h, b))
                        for i, _ in Z_IN[b]:
                            w = seen[i]
                            dve.tensor_tensor_scan(left[:, left_at[i]:left_at[i] + w][:, ::-1],
                                                   rest[:, z_at[i]:z_at[i] + w][:, ::-1],
                                                   ones[:, 0:1].broadcast_to([P, w]), 1.0,
                                                   ALU.mult, ALU.mult).then_inc(left_ready, 1)
                    n = 0
                    for b in range(3):
                        for i, _ in Z_IN[b]:
                            n += 1
                            w = seen[i]
                            dve.wait_ge(left_ready, T * h + n)
                            ins = dve.tensor_tensor(beta[:, z_at[i]:z_at[i] + w], beta[:, z_at[i]:z_at[i] + w],
                                                    left[:, left_at[i] + 1:left_at[i] + 1 + w], ALU.mult)
                    ins.then_inc(weights_ready, 1)
                elif kind == "wT":
                    h = job[1]
                    for b in range(3):
                        wb = wait_full(dve, ("wT", h, b))
                        cols = slice(HALF * b, HALF * b + FILL[b])
                        dve.wait_ge(wT_hi_ready, 3 * h + b + 1)
                        dve.tensor_tensor(wT_lo[:, cols], wb[:, 0:FILL[b]], wT_hi[:, cols].bitcast(F32),
                                          ALU.subtract).then_inc(free_of(("wT", h, b)), 1)
                elif kind == "pv":
                    h = job[1]
                    pr, s = h // 2, h % 2
                    b = wait_full(dve, job)
                    dve.wait_ge(o_hi_ready, h + 1)
                    dve.tensor_tensor(o_lo[HD * s:HD * s + HD, pr, :], b[HD * s:HD * s + HD, :],
                                      o_hi[HD * s:HD * s + HD, pr, :].bitcast(F32), ALU.subtract)\
                        .then_inc(free_of(job), 1)
            for c in range(done, chunk_of["ao", 0] + 3):
                lo_part(c)
            done = chunk_of["ao", 0] + 3
            dve.wait_ge(gates_in[0], 16)
            for m in range(KD):
                b = wait_full(dve, ("ya", m))
                dve.tensor_tensor(gate_a[:, m, :], b[:], gate_a[:, m, :], ALU.mult).then_inc(free_of(("ya", m)), 1)
                wait_read(dve, ("ya", m))
                dve.wait_ge(gated, m + 1)
                step(dve.tensor_tensor(gate_a[:, m, :], gate_a[:, m, :], gate_r[:, m, :], ALU.add))
                step(dve.tensor_copy(m_hi[:, m, :], gate_a[:, m, :]))
                dve.tensor_tensor(m_lo[:, m, :], gate_a[:, m, :], m_hi[:, m, :].bitcast(F32), ALU.subtract)\
                    .then_inc(merged_ready, 1)
                if m == 3:
                    lo_part(done)
                    done += 1
            dve.wait_ge(route_made, 1)
            step(dve.tensor_copy(iota_f[:], iota_i[:]))
            step(dve.tensor_copy(token_f[:], token_id[:]))
            step(dve.tensor_scalar(rev[:], iota_f[:, 0:NE], -1.0, float(NE), ALU.mult, ALU.add))
            step(dve.tensor_scalar(e_base[:], iota_f[:, 0:NE], float(S), None, ALU.mult))
            dve.wait_ge(x_again, 16 * T)
            dve.wait_ge(gB_in, 16)

            def normed(i):
                mean_sq(1, i)
                dve.wait_ge(rstd_done, T + i + 1)
                dve.scalar_tensor_tensor(out=h2[:, i, :], in0=x2[:, i, :], scalar=rstd[:, 1, i:i + 1],
                                         in1=gB[:], op0=ALU.mult, op1=ALU.mult).then_inc(h2_ready, 1)

            for n in range(2):
                while done < chunk_of["wo", n, 1] + 3:
                    lo_part(done)
                    done += 1
                for i in range(T):
                    b = wait_full(dve, ("x2", n, i))
                    xs = x2[:, i, HALF * n:HALF * n + HALF]
                    dve.tensor_tensor(xs, b[:], xs, ALU.add).then_inc(free_of(("x2", n, i)), 1)
                    if n == 1 and i > 0:
                        normed(i - 1)
            normed(T - 1)
            for k in range(1, KD, 2):
                b = wait_full(dve, ("h2T", k))
                dve.tensor_copy(h2T[:, k, :], b[:]).then_inc(free_of(("h2T", k)), 1)

            def first_max(src, n, onehot, top):
                r = rev[:, NE - n:NE].unsqueeze(1).broadcast_to([P, T, n])
                step(dve.tensor_reduce(top, src, AX, ALU.max))
                step(dve.tensor_tensor(eq[:, :, 0:n], src, top.unsqueeze(2).broadcast_to([P, T, n]), ALU.is_equal))
                step(dve.tensor_tensor(cand[:, :, 0:n], eq[:, :, 0:n], r, ALU.mult))
                step(dve.tensor_reduce(best[:], cand[:, :, 0:n], AX, ALU.max))
                step(dve.tensor_tensor(onehot, cand[:, :, 0:n], best[:].unsqueeze(2).broadcast_to([P, T, n]),
                                       ALU.is_equal))

            lo_part(C_MOE + 2)
            b = wait_full(dve, "logits")
            dve.tensor_copy(lg[:], b[:, 0:T * NL].rearrange("p (i n) -> p i n", n=NL))\
                .then_inc(free_of("logits"), 1)
            wait_read(dve, "logits")
            first_max(lg[:, :, 0:NG], NG, in_group[:], mx[:])
            dve.tensor_tensor(dg[:], lg[:, :, 0:NG], mx[:].unsqueeze(2).broadcast_to([P, T, NG]),
                              ALU.subtract).then_inc(gexp_in, 1)
            step(dve.tensor_scalar(pen[:], in_group[:], BIG, BIG, ALU.mult, ALU.subtract))
            EG = NE // NG
            for i in range(T):
                el_i = el[:, i, :].rearrange("p (g e) -> p g e", e=EG)
                dve_in = lg[:, i, NG:NL].rearrange("p (g e) -> p g e", e=EG)
                step(dve.tensor_tensor(el_i, dve_in, in_group[:, i, :].unsqueeze(2).broadcast_to([P, NG, EG]), ALU.mult))
                step(dve.tensor_tensor(el_i, el_i, pen[:, i, :].unsqueeze(2).broadcast_to([P, NG, EG]), ALU.add))
            first_max(el[:], NE, M[:, 0], v12[:, 0, :])
            step(dve.scalar_tensor_tensor(out=el[:], in0=M[:, 0], scalar=-2 * BIG, in1=el[:],
                                          op0=ALU.mult, op1=ALU.add))
            first_max(el[:], NE, M[:, 1], v12[:, 1, :])
            dve.tensor_tensor(dv[:], v12[:, 1, :], v12[:, 0, :], ALU.subtract).then_inc(vexp_in, 1)
            dve.tensor_tensor(both[:].rearrange("p i n -> p (i n)").bitcast(BF16),
                              M[:, 0].rearrange("p i n -> p (i n)"), M[:, 1].rearrange("p i n -> p (i n)"),
                              ALU.add).then_inc(both_ready, 1)
            dve.wait_ge(gexp_ready, 1)
            step(dve.tensor_reduce(gsum[:], dg[:], AX, ALU.add))
            step(dve.reciprocal(ggate[:], gsum[:]))
            dve.wait_ge(vexp_ready, 1)
            step(dve.tensor_scalar(gsum[:], dv[:], 1.0, None, ALU.add))
            step(dve.reciprocal(gsum[:], gsum[:]))
            step(dve.tensor_tensor(combine_w[:, 0, :], gsum[:], ggate[:], ALU.mult))
            step(dve.tensor_tensor(combine_w[:, 1, :], combine_w[:, 0, :], dv[:], ALU.mult))
            b = wait_full(dve, "pos")
            dve.tensor_copy(pos[:], b[:, 0:(T + 1) * NE].rearrange("p (i n) -> p i n", n=NE))\
                .then_inc(free_of("pos"), 1)
            wait_read(dve, "pos")
            for k in range(2):
                step(dve.tensor_tensor(eq[:], M[:, k], pos[:, 0:T, :], ALU.mult))
                step(dve.tensor_reduce(place[:, k, :], eq[:], AX, ALU.add))
                step(dve.tensor_tensor(cand[:], M[:, k], e_base[:].unsqueeze(1).broadcast_to([P, T, NE]), ALU.mult))
                step(dve.tensor_reduce(slot[:, k, :], cand[:], AX, ALU.add))
            step(dve.tensor_scalar(over[:], place[:], float(P), None, ALU.is_ge))
            for n in (2, 3):
                step(dve.tensor_scalar(ov2[:], place[:], float(n * P), None, ALU.is_ge))
                step(dve.tensor_tensor(over[:], over[:], ov2[:], ALU.add))
            step(dve.scalar_tensor_tensor(out=tile_at[:], in0=slot[:], scalar=1.0 / P, in1=over[:],
                                          op0=ALU.mult, op1=ALU.add))
            step(dve.scalar_tensor_tensor(out=row[:], in0=over[:], scalar=-float(P), in1=place[:],
                                          op0=ALU.mult, op1=ALU.add))
            for k in range(2):
                for i in range(T):
                    dve.tensor_scalar(in_row[:, k, i, :], iota_f[:], row[:, k, i:i + 1], None,
                                      ALU.is_equal).then_inc(marks_ready, 1)
                    dve.tensor_scalar(in_tile[:, k, i, :], iota_f[:, 0:TL], tile_at[:, k, i:i + 1],
                                      token_f[:, i:i + 1], ALU.is_equal, ALU.mult).then_inc(marks_ready, 1)
            b = wait_full(dve, "lists")
            dve.tensor_copy(token_of[:], b[:, 0:TL]).then_inc(free_of("lists"), 1)
            step(dve.tensor_scalar(ov2[:], place[:], float(P - 1), None, ALU.min))
            step(dve.scalar_tensor_tensor(out=ov2[:], in0=slot[:], scalar=float(P) / S, in1=ov2[:],
                                          op0=ALU.mult, op1=ALU.add))
            step(dve.tensor_copy(slot_i[:], ov2[:]))
            step(dve.tensor_scalar(ov2[:], place[:], -float(P), 0.0, ALU.add, ALU.max))
            step(dve.scalar_tensor_tensor(out=ov2[:], in0=slot[:], scalar=float(OVER * P) / S, in1=ov2[:],
                                          op0=ALU.mult, op1=ALU.add))
            step(dve.tensor_copy(over_slot_i[:], ov2[:]))
            step(dve.tensor_scalar(ov2[:], place[:], float(P), None, ALU.is_ge))
            step(dve.tensor_tensor(over_w[:], ov2[:], combine_w[:], ALU.mult))
            step(dve.tensor_tensor(combine_w[:], combine_w[:], over_w[:], ALU.subtract))
            step(dve.tensor_reduce(mx[:, 0:1], pos[:, T, :], AX, ALU.max))
            dve.tensor_copy(most_i[:], mx[:, 0:1]).then_inc(rows_ready, 1)

            def evict_XT(key, par, it, n):
                for a, bk in enumerate(("XT", "XT2")):
                    b = wait_full(dve, (bk, key), it=it)
                    dve.wait_ge(XT_hi_ready, n + a + 1)
                    dve.tensor_tensor(XT_lo[par][:, 4 * a:4 * a + 4, :], b[:].rearrange("p (k t) -> p k t", t=P),
                                      XT_hi[par][:, 4 * a:4 * a + 4, :].bitcast(F32), ALU.subtract)\
                        .then_inc(free_of((bk, key)), 1)

            evict_XT("first", 0, 0, 0)
            lo_part(C_MOE + 3)

            def dve_step(par, it, last=False):
                if not last:
                    evict_XT(par, 1 - par, it, it * 4 + 2 * par + 2)
                c = step_base(par)
                lo_part(c + 2, it)
                lo_part(c + 3, it)
                gkey = ("G", "first") if par == 0 else ("G", 0)
                wait_read(dve, gkey, it=it)
                b = wait_full(dve, ("U", par), it=it)
                dve.tensor_tensor(he[:], b[:], sil[:], ALU.mult).then_inc(free_of(("U", par)), 1)
                if not last:
                    lo_part(c + 4, it)
                b = wait_full(dve, ("heT", par), it=it)
                dve.wait_ge(heT_hi_ready, it * 2 + par + 1)
                dve.tensor_tensor(heT_lo[:], b[:].rearrange("p (k t) -> p k t", t=P), heT_hi[:].bitcast(F32),
                                  ALU.subtract).then_inc(free_of(("heT", par)), 1)
                if not last:
                    lo_part(c + 5, it)
                    c += 2
                lo_part(c + 4, it)
                lo_part(c + 5, it)
                b = wait_full(dve, ("Y", "last" if last else par, 1), it=it)
                wait_read(dve, ("Y", par, 0), it=it)
                if not isinstance(it, int) or it > 0:
                    dve.wait_ge(Y_out[par], it * 16)
                dve.tensor_copy(Y[par][:, HALF:], b[:]).then_inc(free_of(("Y", par, 1)), 1)

            dve_step(0, 0)
            dve_step(1, 0)
            with dve.Fori(1, NE // 2 - 1) as it:
                dve_step(0, it)
                dve_step(1, it)
            dve_step(0, NE // 2 - 1)
            dve_step(1, NE // 2 - 1, last=True)
            lo_part(C_TAIL + 2)

            def over_dve(e, j, n):
                dve.wait_ge(over_XT_hi, n * 2 + 2)
                for a in range(2):
                    dve.tensor_tensor(XT_lo[0][:, 4 * a:4 * a + 4, :],
                                      bank[4 + a][:].rearrange("p (k t) -> p k t", t=P),
                                      XT_hi[0][:, 4 * a:4 * a + 4, :].bitcast(F32), ALU.subtract)\
                        .then_inc(over_XT_ready, 1)
                dve.wait_ge(over_sil, n + 1)
                dve.wait_ge(over_used, n * PER_E + 4)
                dve.tensor_tensor(he[:], bank[1][:], sil[:], ALU.mult).then_inc(over_he, 1)
                dve.wait_ge(over_heT_hi, n + 1)
                dve.tensor_tensor(heT_lo[:], bank[3][:].rearrange("p (k t) -> p k t", t=P),
                                  heT_hi[:].bitcast(F32), ALU.subtract).then_inc(over_heT_ready, 1)

            with dve.If(any_over(dve)):
                further_tiles(dve, over_dve)
                dve.wait_ge(over_rows_in, 16 * 2 * T)
                for i in range(T):
                    for k in range(2):
                        dve.scalar_tensor_tensor(out=x2[:, i, :], in0=yg[i][k][:], scalar=over_w[:, k, i:i + 1],
                                                 in1=x2[:, i, :], op0=ALU.mult, op1=ALU.add)\
                            .then_inc(over_added, 1)
                        dve.wait_ge(over_added, 2 * i + k + 1)
            for k in range(KP):
                b = wait_full(dve, ("pT", k))
                dve.wait_ge(pT_hi_ready, k + 1)
                dve.tensor_tensor(pT_lo[:, k, :], b[:], pT_hi[:, k, :].bitcast(F32), ALU.subtract)\
                    .then_inc(free_of(("pT", k)), 1)

            for i in range(T):
                dve.wait_ge(yg_in[i], 32)
                step(dve.scalar_tensor_tensor(out=x2[:, i, :], in0=yg[i][0][:], scalar=combine_w[:, 0, i:i + 1],
                                              in1=x2[:, i, :], op0=ALU.mult, op1=ALU.add))
                dve.scalar_tensor_tensor(out=x2[:, i, :], in0=yg[i][1][:], scalar=combine_w[:, 1, i:i + 1],
                                         in1=x2[:, i, :], op0=ALU.mult, op1=ALU.add).then_inc(x3_ready, 1)
            for k in range(KD):
                b = wait_full(dve, ("h3T", k))
                dve.wait_ge(h3_hi_ready, k + 1)
                dve.scalar_tensor_tensor(out=h3_lo[:, k, :], in0=b[:], scalar=g_ple[:, k:k + 1],
                                         in1=h3_hi[:, k, :].bitcast(F32), op0=ALU.mult, op1=ALU.subtract)\
                    .then_inc(free_of(("h3T", k)), 1)
            lo_part(C_TAIL + 3)
            for i in range(T):
                mean_sq(2, i)
            lo_part(C_TAIL + 4)
            dve.wait_ge(gB_in, 32)

            def final_norm(i):
                mean_sq(3, i)
                dve.wait_ge(rstd_done, 3 * T + i + 1)
                dve.scalar_tensor_tensor(out=xn3[:, i, :], in0=x2[:, i, :], scalar=rstd[:, 3, i:i + 1],
                                         in1=gB[:], op0=ALU.mult, op1=ALU.mult).then_inc(out_ready, 1)

            for n in range(2):
                for i in range(T):
                    j = T * n + i
                    dve.wait_ge(sg_ready, j + 1)
                    wait_read(dve, ("pp", i, n))
                    cols = slice(HALF * n, HALF * n + HALF)
                    step(dve.tensor_tensor(sg[j % 2][:], sg[j % 2][:], pp[:, i, cols], ALU.mult))
                    if n == 0:
                        wait_full(dve, ("h3T", KD - 1))
                    dve.tensor_tensor(x2[:, i, cols], x2[:, i, cols], sg[j % 2][:], ALU.add).then_inc(x4_ready, 1)
                    if n == 1 and i > 0:
                        final_norm(i - 1)
            final_norm(T - 1)

        @block.tensor
        def _(pe):
            def mm3(dst, lhs, rhs, first, last):
                pe.matmul(dst, lhs[0], rhs[0], start=first, stop=False)
                pe.matmul(dst, lhs[0], rhs[1], start=False, stop=False)
                return pe.matmul(dst, lhs[1], rhs[0], start=False, stop=last)

            def chunk(c, k, it=0):
                s = c % SPLIT_SLOTS
                n = c + 1 + PER_IT * it
                pe.wait_ge(hi_ready, n)
                pe.wait_ge(lo_dve, n)
                pe.wait_ge(lo_pool, n)
                return [t[s][:].rearrange("p (k n) -> p k n", k=k) for t in (whi, wlo)]

            def used(ins):
                ins.then_inc(w_used, 1)

            pe.wait_ge(consts_made, 1)
            for i in range(T):
                pe.wait_ge(xn_ready, i + 1)
                for k in range(KD):
                    ins = pe.transpose(bank[k][:, P * i:P * i + P], x_sb[:, i, k::KD], ident[:])
                    if i == T - 1:
                        ins.then_inc(full_of(("hT", k)), 1)
            hT = (hT_hi, hT_lo)
            pe.wait_ge(consts_cast, 4)
            for job in JOBS:
                kind = job[0]
                if kind in ("xr", "xg", "q", "k", "g"):
                    if kind == "g":
                        n = job[1] // 2
                        c, j = (chunk_of["ga", n] if n < 4 else chunk_of["gr", n - 4]), job[1] % 2
                    elif kind in ("q", "k"):
                        c, j = chunk_of[kind, job[1]], job[2]
                    else:
                        c, j = chunk_of[kind, job[1] // 2], job[1] % 2
                    w = chunk(c, KD)
                    b = wait_free(pe, job)
                    for k in range(KD):
                        if job == JOBS[0]:
                            wait_read(pe, ("hT", k))
                        ins = mm3(b[:], [t[:, k, P * j:P * j + P] for t in w], [t[:, k, :] for t in hT],
                                  k == 0, k == KD - 1)
                    ins.then_inc(full_of(job), 1)
                    if job == JOBS[0]:
                        n = (CW + 4) * RB
                        pe.wait_ge(params_in, 16 * 5)
                        pb = wait_free(pe, "params")
                        pe.transpose(pb[:, 0:n], par_rows[:], ident[0:n, 0:n]).then_inc(full_of("params"), 1)
                elif kind == "v":
                    _, g, j = job
                    w = chunk(chunk_of["v", g], KD)
                    b = wait_free(pe, job)
                    for a in range(2):
                        i = 2 * j + a
                        for k in range(KD):
                            ins = mm3(b[:, 256 * a:256 * a + 256], [t[:, k, P * i:P * i + P] for t in hT],
                                      [t[:, k, :] for t in w], k == 0, k == KD - 1)
                    ins.then_inc(full_of(job), 1)
                elif kind == "yr":
                    m = job[1]
                    w = chunk(chunk_of["ro", m // 4], 4)
                    b = wait_free(pe, job)
                    if m == 0:
                        pe.wait_ge(rg_done, RB)
                    for k in range(4):
                        ins = mm3(b[:], [t[:, k, P * (m % 4):P * (m % 4) + P] for t in w],
                                  [t[:, k, :] for t in (r_hi, r_lo)], k == 0, k == 3)
                    ins.then_inc(full_of(job), 1)
                elif kind == "rg":
                    for m in (2 * job[1], 2 * job[1] + 1):
                        pe.wait_ge(xc_ready, m + 1)
                        for s, key in enumerate(("rga", "rgx")):
                            b = wait_free(pe, (key, m))
                            if m == 0 and s == 0:
                                pe.wait_ge(rg_w_ready, 4)
                            ins = mm3(b[:], [t[s][:, m, :] for t in (wg_hi, wg_lo)],
                                      [t[m % 2][:] for t in (xc_hi, xc_lo)], True, True)
                            ins.then_inc(full_of((key, m)), 1)
                elif kind == "z":
                    h = job[1]
                    g = h // 4
                    lp, s = (h % 4) // 2, h % 2
                    if h % 4 == 0:
                        for key in ("q", "k", "v"):
                            for j in range(2):
                                wait_read(pe, (key, g, j))
                    rows = slice(HD * s, HD * s + HD)
                    for b in range(3):
                        zb = wait_free(pe, ("z", h, b))
                        for i, col in Z_IN[b]:
                            q = [t[rows, lp, P * i:P * i + P] for t in (q_hi, q_lo)]
                            k = [t[rows, lp, 0:seen[i]] for t in (k_hi, k_lo)]
                            zt = zb[:, col:col + seen[i]]
                            pe.matmul(zt, q[0], k[0], start=True, stop=False, skip_group_check=True)
                            pe.matmul(zb[:, col + P * i:col + P * i + P], hidden[:], ident_r[:], start=False,
                                      stop=False, skip_group_check=True)
                            pe.matmul(zt, q[0], k[1], start=False, stop=False, skip_group_check=True)
                            ins = pe.matmul(zt, q[1], k[0], start=False, stop=True, skip_group_check=True)
                        ins.then_inc(full_of(("z", h, b)), 1)
                elif kind == "wT":
                    h = job[1]
                    pe.wait_ge(weights_ready, h + 1)
                    for b in range(3):
                        wb = wait_free(pe, ("wT", h, b))
                        for j, col in W_IN[b]:
                            for i in range(j, T):
                                at_t = col + P * (i - j)
                                ins = pe.transpose(wb[:, at_t:at_t + P], beta[:, z_at[i] + P * j:z_at[i] + P * j + P],
                                                   ident[:])
                        ins.then_inc(full_of(("wT", h, b)), 1)
                elif kind == "pv":
                    h = job[1]
                    lp = (h % 4) // 2
                    for b in range(3):
                        wait_read(pe, ("wT", h, b))
                    b = wait_free(pe, job)
                    for j in range(T):
                        ins = mm3(b[:, P * j:], [t[:, j, P * lp:P * lp + P] for t in (v_hi, v_lo)],
                                  [t[:, w_at[j]:w_at[j] + S - P * j] for t in (wT_hi, wT_lo)], j == 0, j == T - 1)
                    ins.then_inc(full_of(job), 1)
            wait_read(pe, ("pv", H - 2))
            wait_read(pe, ("pv", H - 1))
            for m in range(KD):
                w = chunk(chunk_of["ao", m // 4], 4)
                b = wait_free(pe, ("ya", m))
                for k in range(4):
                    ins = mm3(b[:], [t[:, k, P * (m % 4):P * (m % 4) + P] for t in w],
                              [t[:, k, :] for t in (o_hi, o_lo)], k == 0, k == 3)
                ins.then_inc(full_of(("ya", m)), 1)
            for n in range(2):
                for kh in range(2):
                    w = chunk(chunk_of["wo", n, kh], 4)
                    for i in range(T):
                        key = ("x2", n, i)
                        b = wait_free(pe, key) if kh == 0 else bank[banks.at[key][0]]
                        for k in range(4):
                            if n == 0 and i == 0:
                                pe.wait_ge(merged_ready, 4 * kh + k + 1)
                            ins = mm3(b[:], [t[:, 4 * kh + k, P * i:P * i + P] for t in (m_hi, m_lo)],
                                      [t[:, k, :] for t in w], kh == 0 and k == 0, kh == 1 and k == 3)
                        if kh == 1:
                            ins.then_inc(full_of(key), 1)
                        elif i == T - 1:
                            ins.then_inc(w_used, 1)
            for i in range(T):
                pe.wait_ge(h2_ready, i + 1)
                for k in range(KD):
                    b = wait_free(pe, ("h2T", k)) if i == 0 else bank[(4 + k) % 8]
                    ins = pe.transpose(b[:, P * i:P * i + P], h2[:, i, k::KD], ident[:])
                    if i == T - 1:
                        ins.then_inc(full_of(("h2T", k)), 1)
            pe.wait_ge(small_in, 64)
            for k in range(KD):
                wait_read(pe, ("h2T", k))
                if k == 0:
                    b = wait_free(pe, "logitsT")
                ins = pe.matmul(b[0:NL, :], w_route[:, k, :], h2T[:, k, :], start=(k == 0), stop=(k == KD - 1))
            ins.then_inc(full_of("logitsT"), 1)
            wait_read(pe, "logitsT")
            b = wait_free(pe, "logits")
            for i in range(T):
                ins = pe.transpose(b[:, NL * i:NL * i + NL], lgT[:, P * i:P * i + P], ident[0:NL, 0:NL])
            ins.then_inc(full_of("logits"), 1)
            pe.wait_ge(both_ready, 1)
            b = wait_free(pe, "pos")
            for i in range(T + 1):
                cols = b[:, NE * i:NE * i + NE]
                for j in range(min(i + 1, T)):
                    lhs = before_b if j == i else ones_b
                    ins = pe.matmul(cols, lhs[:].bitcast(BF16), both[:, j, :].bitcast(BF16),
                                    start=(j == 0), stop=(j == min(i, T - 1)))
            ins.then_inc(full_of("pos"), 1)
            b = wait_free(pe, "lists")
            for k in range(2):
                for i in range(T):
                    n = T * k + i + 1
                    pe.wait_ge(marks_ready, 2 * n)
                    ins = pe.matmul(b[:, 0:TL], in_row[:, k, i, :], in_tile[:, k, i, :], start=(n == 1),
                                    stop=(n == 2 * T))
            ins.then_inc(full_of("lists"), 1)

            def transpose_X(key, par, it, n):
                pe.wait_ge(X_in[par], n)
                for a, bk in enumerate(("XT", "XT2")):
                    b = wait_free(pe, (bk, key), it=it)
                    for k in range(4):
                        ins = pe.transpose(b[:, P * k:P * k + P], X[par][:, 4 * a + k::KD], ident[:])
                    ins.then_inc(full_of((bk, key)), 1)

            def up_or_gate(key, c, it, par, between=None):
                b = wait_free(pe, key, it=it)
                for half in range(2):
                    if half == 1 and between:
                        between()
                    w = chunk(c + half, 4, it)
                    for k in range(4):
                        kk = 4 * half + k
                        ins = mm3(b[:], [t[par][:, kk, :] for t in (XT_hi, XT_lo)], [t[:, k, :] for t in w],
                                  kk == 0, kk == KD - 1)
                    ins.then_inc(w_used, 1)

            def XT_done(key, it):
                for bk in ("XT", "XT2"):
                    wait_read(pe, (bk, key), it=it)

            transpose_X("first", 0, 0, 16)
            XT_done("first", 0)
            up_or_gate(("G", "first"), C_MOE, 0, 0)

            def pe_step(par, it, last=False):
                c = step_base(par)
                if not last:
                    transpose_X(par, 1 - par, it, it * 16 + 16 + 16 * par)
                up_or_gate(("U", par), c, it, par)

                def transpose_he():
                    wait_read(pe, ("U", par), it=it)
                    b = wait_free(pe, ("heT", par), it=it)
                    for k in range(KF):
                        ins = pe.transpose(b[:, P * k:P * k + P], he[:, k::KF], ident[:])
                    ins.then_inc(full_of(("heT", par)), 1)

                if last:
                    transpose_he()
                else:
                    XT_done(par, it)
                    up_or_gate(("G", par), c + 2, it, 1 - par, between=transpose_he)
                    c += 2
                wait_read(pe, ("heT", par), it=it)
                ys = [wait_free(pe, ("Y", par, n), it=it) for n in range(2)]
                for half in range(2):
                    w = chunk(c + 2 + half, 2, it)
                    for k in range(2):
                        kk = 2 * half + k
                        for n in range(2):
                            ins = mm3(ys[n][:], [t[:, kk, :] for t in (heT_hi, heT_lo)],
                                      [t[:, k, HALF * n:HALF * n + HALF] for t in w], kk == 0, kk == KF - 1)
                            if kk == KF - 1:
                                ins.then_inc(full_of(("Y", par, n)), 1)
                    if half == 0:
                        ins.then_inc(w_used, 1)

            with pe.Fori(0, NE // 2 - 1) as it:
                pe_step(0, it)
                pe_step(1, it)
            pe_step(0, NE // 2 - 1)
            pe_step(1, NE // 2 - 1, last=True)

            def over_pe(e, j, n):
                def use(c, k, products):
                    pe.wait_ge(over_lo_ready, n * PER_E + c + 1)
                    products([t[:].rearrange("p (k n) -> p k n", k=k) for t in (over_hi, over_lo)])\
                        .then_inc(over_used, 1)

                def in_features(b, half):
                    def products(w):
                        for k in range(4):
                            kk = 4 * half + k
                            ins = mm3(b[:], [t[0][:, kk, :] for t in (XT_hi, XT_lo)], [t[:, k, :] for t in w],
                                      kk == 0, kk == KD - 1)
                        return ins
                    return products

                def down(half):
                    def products(w):
                        for h in range(2):
                            for k in range(2):
                                kk = 2 * half + k
                                ins = mm3(bank[6 + h][:], [t[:, kk, :] for t in (heT_hi, heT_lo)],
                                          [t[:, k, HALF * h:HALF * h + HALF] for t in w], kk == 0, kk == KF - 1)
                        return ins
                    return products

                pe.wait_ge(over_X_in, n * 16 + 16)
                for k in range(KD):
                    ins = pe.transpose(bank[4 + k // 4][:, P * (k % 4):P * (k % 4) + P], X[0][:, k::KD], ident[:])
                ins.then_inc(over_XT, 1)
                pe.wait_ge(over_XT_ready, n * 2 + 2)
                for half in range(2):
                    use(half, 4, in_features(bank[0], half))
                for half in range(2):
                    use(2 + half, 4, in_features(bank[1], half))
                pe.wait_ge(over_he, n + 1)
                for k in range(KF):
                    ins = pe.transpose(bank[3][:, P * k:P * k + P], he[:, k::KF], ident[:])
                ins.then_inc(over_heT, 1)
                pe.wait_ge(over_heT_ready, n + 1)
                for half in range(2):
                    use(4 + half, 2, down(half))
                pe.wait_ge(over_Y_ready, n * 2 + 2)

            with pe.If(any_over(pe)):
                for b in range(8):
                    pe.wait_ge(free[b], free_after_experts[b])
                further_tiles(pe, over_pe)

            pe.wait_ge(p_in, 16)
            for k in range(KP):
                b = wait_free(pe, ("pT", k))
                for i in range(T):
                    ins = pe.transpose(b[:, P * i:P * i + P], p_sb[:, i, k::KP], ident[:])
                ins.then_inc(full_of(("pT", k)), 1)
            for k in range(KP):
                wait_read(pe, ("pT", k))
            w = chunk(C_TAIL, KP)
            for i in range(T):
                for n in range(2):
                    b = wait_free(pe, ("pp", i, n))
                    for k in range(KP):
                        ins = mm3(b[:], [t[:, k, P * i:P * i + P] for t in (pT_hi, pT_lo)],
                                  [t[:, k, HALF * n:HALF * n + HALF] for t in w], k == 0, k == KP - 1)
                    ins.then_inc(full_of(("pp", i, n)), 1)
            for i in range(T):
                pe.wait_ge(x3_ready, i + 1)
                for k in range(KD):
                    b = wait_free(pe, ("h3T", k)) if i == 0 else bank[k]
                    ins = pe.transpose(b[:, P * i:P * i + P], x2[:, i, k::KD], ident[:])
                    if i == T - 1:
                        ins.then_inc(full_of(("h3T", k)), 1)
            for n in range(2):
                for kh in range(2):
                    w = chunk(C_TAIL + 1 + 2 * n + kh, 4)
                    for i in range(T):
                        key = ("pg", n, i)
                        b = wait_free(pe, key) if kh == 0 else bank[banks.at[key][0]]
                        for k in range(4):
                            if n == 0 and i == 0:
                                wait_read(pe, ("h3T", 4 * kh + k))
                            ins = mm3(b[:], [t[:, 4 * kh + k, P * i:P * i + P] for t in (h3_hi, h3_lo)],
                                      [t[:, k, :] for t in w], kh == 0 and k == 0, kh == 1 and k == 3)
                        if kh == 1:
                            ins.then_inc(full_of(key), 1)
                        elif i == T - 1:
                            ins.then_inc(w_used, 1)


_INS = ["x", "p", "norm_mix", "w_in", "conv_w", "conv_b", "w_rg_a", "b_rg_a", "w_rg_x", "b_rg_x", "rg_lambda",
        "w_attn_o", "w_rnn_o", "w_out", "norm_moe", "w_router_group", "b_router_group", "w_router_expert",
        "b_router_expert", "w_exp_gate", "w_exp_up", "w_exp_down", "norm_ple", "w_ple_gate", "w_ple_proj",
        "norm_final"]
_OUTS = [((1, 512, 1024), "float32")]


def kernel(**inputs):
    import numpy as _np
    import concourse.bacc as _bacc
    from concourse import mybir as _mybir
    from concourse.bass_utils import run_bass_kernel_spmd as _run

    nc = _bacc.Bacc("TRN2", target_bir_lowering=False, num_devices=1)
    arrays, args = {}, []
    for name in _INS:
        a = _np.ascontiguousarray(inputs[name])
        arrays[f"in_{name}_dram"] = a
        args.append(nc.dram_tensor(f"in_{name}_dram", a.shape, _mybir.dt.from_np(a.dtype), kind="ExternalInput").ap())
    for i, (shape, dtype) in enumerate(_OUTS):
        dt = _mybir.dt.from_np(_np.dtype(dtype))
        args.append(nc.dram_tensor(f"out_{i}_dram", shape, dt, kind="ExternalOutput").ap())
    trunk(nc, *args)
    r = _run(nc, [arrays], core_ids=[0])
    return r.results[0]["out_0_dram"]
```
